# Optimizing a Trainium2 kernel written in Bass

```python
import math
import jax, jax.numpy as jnp
from jax import lax
import numpy as np

D_MODEL = 1024
BATCH = 1
SEQ = 512
DEPTH = 1

CHUNK = 64
Q_BLOCK = 128
MEM_TOKENS = 256
D_MIX = D_MODEL
RWKV_HEAD = 64
RWKV_WIDTH = D_MIX // 2
RWKV_HEADS = RWKV_WIDTH // RWKV_HEAD
DECAY_LORA = 64
AAA_LORA = 64
GATE_LORA = 128
RWKV_COLS = 3 * RWKV_WIDTH + DECAY_LORA + AAA_LORA + GATE_LORA
GN_EPS = 64e-5
DIFF_WIDTH = D_MIX - RWKV_WIDTH
DIFF_HEADS = 4
DIFF_VDIM = DIFF_WIDTH // DIFF_HEADS
DIFF_QKDIM = DIFF_VDIM // 2
DIFF_COLS = 3 * DIFF_WIDTH
D_IN_TOTAL = RWKV_COLS + DIFF_COLS
MEM_HEADS = 4
MEM_HEAD_DIM = D_MODEL // MEM_HEADS
D_FF = 4 * D_MODEL
RMS_EPS = 1e-5
NEG_INF = -1e30


def rms_norm(x, w, eps=RMS_EPS):
    xf = x.astype(jnp.float32)
    y = xf * lax.rsqrt(jnp.mean(jnp.square(xf), axis=-1, keepdims=True) + eps)
    return (y * w.astype(jnp.float32)).astype(x.dtype)

def rwkv7_scan(r, decay, k, v, kk, a):
    B, S, H, N = r.shape
    xs = tuple(jnp.moveaxis(t, 1, 0) for t in (r, decay, k, v, kk, a))

    def step(state, inp):
        r_t, w_t, k_t, v_t, kk_t, a_t = inp
        sa = jnp.einsum("bhvk,bhk->bhv", state, -kk_t)
        state = (state * w_t[:, :, None, :]
                 + sa[..., None] * (kk_t * a_t)[:, :, None, :]
                 + v_t[..., None] * k_t[:, :, None, :])
        y = jnp.einsum("bhvk,bhk->bhv", state, r_t)
        return state, y

    s0 = jnp.zeros((B, H, N, N), jnp.float32)
    _, ys = lax.scan(step, s0, xs)
    return jnp.moveaxis(ys, 0, 1)

def rwkv7_group(p, mu, w0, w_dec_up, a0, a_up, g_up, k_k, k_a, r_k, lnx_w, lnx_b):
    B, S, _ = p.shape
    p_prev = jnp.pad(p, ((0, 0), (1, 0), (0, 0)))[:, :-1]
    p = p + (p_prev - p) * mu
    r, k, v, wd, ad, gd = jnp.split(
        p, [RWKV_WIDTH, 2 * RWKV_WIDTH, 3 * RWKV_WIDTH,
            3 * RWKV_WIDTH + DECAY_LORA, 3 * RWKV_WIDTH + DECAY_LORA + AAA_LORA], axis=-1)
    f32 = jnp.float32
    w_log = -jax.nn.softplus(-(w0 + jnp.tanh(wd) @ w_dec_up)) - 0.5
    decay = jnp.exp(-jnp.exp(w_log.astype(f32)))
    a = jax.nn.sigmoid((a0 + ad @ a_up).astype(f32))
    g = jax.nn.sigmoid(gd) @ g_up
    heads = lambda t: t.astype(f32).reshape(B, S, RWKV_HEADS, RWKV_HEAD)
    kk = heads(k * k_k)
    kk = kk / jnp.maximum(jnp.sqrt(jnp.sum(jnp.square(kk), -1, keepdims=True)), 1e-12)
    k_mod = k.astype(f32) * (1.0 + (a - 1.0) * k_a)
    rh, kh, vh, ah, wh = heads(r), heads(k_mod), heads(v), heads(a), heads(decay)
    y = rwkv7_scan(rh, wh, kh, vh, kk, ah)
    mean = jnp.mean(y, -1, keepdims=True)
    var = jnp.mean(jnp.square(y - mean), -1, keepdims=True)
    y = ((y - mean) * lax.rsqrt(var + GN_EPS)).reshape(B, S, RWKV_WIDTH)
    y = y * lnx_w + lnx_b
    bonus = jnp.sum(rh * kh * r_k, -1, keepdims=True) * vh
    y = y + bonus.reshape(B, S, RWKV_WIDTH)
    return (y * g).astype(p.dtype)

def diff_attn_group(p, lam_q1, lam_k1, lam_q2, lam_k2, subln_w, lam_init):
    B, S, _ = p.shape
    q, k, v = jnp.split(p, [DIFF_WIDTH, 2 * DIFF_WIDTH], axis=-1)
    q = q.reshape(B, S, DIFF_HEADS, 2, DIFF_QKDIM)
    k = k.reshape(B, S, DIFF_HEADS, 2, DIFF_QKDIM)
    v = v.reshape(B, S, DIFF_HEADS, DIFF_VDIM)
    q1, q2 = q[..., 0, :], q[..., 1, :]
    k1, k2 = k[..., 0, :], k[..., 1, :]
    f32 = jnp.float32
    lam = (jnp.exp(jnp.sum(lam_q1 * lam_k1).astype(f32))
           - jnp.exp(jnp.sum(lam_q2 * lam_k2).astype(f32)) + lam_init)
    scale = DIFF_QKDIM ** -0.5
    outs = []
    for qb in range(S // Q_BLOCK):
        qs, qe = qb * Q_BLOCK, (qb + 1) * Q_BLOCK
        mask = (jnp.arange(qe) // CHUNK)[None, :] <= (jnp.arange(qs, qe) // CHUNK)[:, None]
        s1 = jnp.einsum("bqhd,bkhd->bhqk", q1[:, qs:qe], k1[:, :qe]).astype(f32) * scale
        s2 = jnp.einsum("bqhd,bkhd->bhqk", q2[:, qs:qe], k2[:, :qe]).astype(f32) * scale
        p1 = jax.nn.softmax(jnp.where(mask, s1, NEG_INF), axis=-1)
        p2 = jax.nn.softmax(jnp.where(mask, s2, NEG_INF), axis=-1)
        attn = (p1 - lam * p2).astype(v.dtype)
        outs.append(jnp.einsum("bhqk,bkhd->bqhd", attn, v[:, :qe]))
    o = jnp.concatenate(outs, axis=1)
    o = rms_norm(o, subln_w) * (1.0 - lam_init)
    return o.reshape(B, S, DIFF_WIDTH)

def memory_cross_attn(hn, memn, w_mq, w_mk, w_mv, w_mo):
    B, S, _ = hn.shape
    M = memn.shape[1]
    q = (hn @ w_mq).reshape(B, S, MEM_HEADS, MEM_HEAD_DIM)
    k = (memn @ w_mk).reshape(B, M, MEM_HEADS, MEM_HEAD_DIM)
    v = (memn @ w_mv).reshape(B, M, MEM_HEADS, MEM_HEAD_DIM)
    s = jnp.einsum("bshd,bmhd->bhsm", q, k).astype(jnp.float32) * (MEM_HEAD_DIM ** -0.5)
    pr = jax.nn.softmax(s, axis=-1).astype(v.dtype)
    o = jnp.einsum("bhsm,bmhd->bshd", pr, v).reshape(B, S, D_MODEL)
    return o @ w_mo

def first_inputs(seed: int = 0) -> dict:
    key = jax.random.key(seed)
    ks = jax.random.split(key, 32)
    f32 = jnp.float32
    nrm = lambda k, shape, s: jax.random.normal(k, shape, f32) * s
    L = DEPTH
    return {
        "x": nrm(ks[0], (BATCH, SEQ, D_MODEL), 1.0),
        "mem": nrm(ks[1], (BATCH, MEM_TOKENS, D_MODEL), 1.0),
        "norm_mix_w": 1.0 + nrm(ks[2], (L, D_MODEL), 0.05),
        "w_in": nrm(ks[3], (L, D_MODEL, D_IN_TOTAL), D_MODEL ** -0.5),
        "mu_shift": jax.random.uniform(ks[4], (L, RWKV_COLS), f32),
        "w_decay0": jnp.linspace(-6.0, -1.0, RWKV_WIDTH, dtype=f32)[None] + nrm(ks[5], (L, RWKV_WIDTH), 0.1),
        "w_decay_up": nrm(ks[6], (L, DECAY_LORA, RWKV_WIDTH), 0.1),
        "a0": nrm(ks[7], (L, RWKV_WIDTH), 0.1),
        "a_up": nrm(ks[8], (L, AAA_LORA, RWKV_WIDTH), AAA_LORA ** -0.5),
        "g_up": nrm(ks[9], (L, GATE_LORA, RWKV_WIDTH), GATE_LORA ** -0.5),
        "k_k": 0.85 + nrm(ks[10], (L, RWKV_WIDTH), 0.05),
        "k_a": 1.0 + nrm(ks[11], (L, RWKV_WIDTH), 0.05),
        "r_k": nrm(ks[12], (L, RWKV_HEADS, RWKV_HEAD), 0.1),
        "lnx_w": 1.0 + nrm(ks[13], (L, RWKV_WIDTH), 0.05),
        "lnx_b": nrm(ks[14], (L, RWKV_WIDTH), 0.02),
        "lam_q1": nrm(ks[15], (L, DIFF_QKDIM), 0.1),
        "lam_k1": nrm(ks[16], (L, DIFF_QKDIM), 0.1),
        "lam_q2": nrm(ks[17], (L, DIFF_QKDIM), 0.1),
        "lam_k2": nrm(ks[18], (L, DIFF_QKDIM), 0.1),
        "subln_w": 1.0 + nrm(ks[19], (L, DIFF_VDIM), 0.05),
        "w_out": nrm(ks[20], (L, D_MIX, D_MODEL), D_MIX ** -0.5),
        "norm_mem_w": 1.0 + nrm(ks[21], (L, D_MODEL), 0.05),
        "norm_src_w": 1.0 + nrm(ks[22], (L, D_MODEL), 0.05),
        "w_mq": nrm(ks[23], (L, D_MODEL, D_MODEL), D_MODEL ** -0.5),
        "w_mk": nrm(ks[24], (L, D_MODEL, D_MODEL), D_MODEL ** -0.5),
        "w_mv": nrm(ks[25], (L, D_MODEL, D_MODEL), D_MODEL ** -0.5),
        "w_mo": nrm(ks[26], (L, D_MODEL, D_MODEL), D_MODEL ** -0.5),
        "norm_mlp_w": 1.0 + nrm(ks[27], (L, D_MODEL), 0.05),
        "w_up": nrm(ks[28], (L, D_MODEL, D_FF), D_MODEL ** -0.5),
        "w_down": nrm(ks[29], (L, D_FF, D_MODEL), D_FF ** -0.5),
        "norm_final_w": 1.0 + nrm(ks[30], (D_MODEL,), 0.05),
    }

def first_block(x, mem, norm_mix_w, w_in, mu_shift, w_decay0, w_decay_up, a0, a_up, g_up,
              k_k, k_a, r_k, lnx_w, lnx_b, lam_q1, lam_k1, lam_q2, lam_k2, subln_w, w_out,
              norm_mem_w, norm_src_w, w_mq, w_mk, w_mv, w_mo, norm_mlp_w, w_up, w_down,
              norm_final_w):
    h = x
    for l in range(DEPTH):
        lam_init = 0.8 - 0.6 * math.exp(-0.3 * l)
        proj = rms_norm(h, norm_mix_w[l]) @ w_in[l]
        p_rwkv, p_diff = proj[..., :RWKV_COLS], proj[..., RWKV_COLS:]
        y_rwkv = rwkv7_group(p_rwkv, mu_shift[l], w_decay0[l], w_decay_up[l], a0[l], a_up[l],
                             g_up[l], k_k[l], k_a[l], r_k[l], lnx_w[l], lnx_b[l])
        y_diff = diff_attn_group(p_diff, lam_q1[l], lam_k1[l], lam_q2[l], lam_k2[l],
                                 subln_w[l], lam_init)
        h = h + jnp.concatenate([y_rwkv, y_diff], axis=-1) @ w_out[l]
        h = h + memory_cross_attn(rms_norm(h, norm_mem_w[l]), rms_norm(mem, norm_src_w[l]),
                                  w_mq[l], w_mk[l], w_mv[l], w_mo[l])
        hn = rms_norm(h, norm_mlp_w[l])
        h = h + jnp.square(jax.nn.relu(hn @ w_up[l])) @ w_down[l]
    return rms_norm(h, norm_final_w)


DEPTH_2 = 2

N_A_LAYERS = DEPTH_2 // 2
N_B_LAYERS = DEPTH_2 - N_A_LAYERS

GLA_HEADS = 4
GLA_KEY_DIM = D_MODEL // 2
GLA_VAL_DIM = D_MODEL
GLA_HK = GLA_KEY_DIM // GLA_HEADS
GLA_HV = GLA_VAL_DIM // GLA_HEADS
GLA_GATE_RANK = 16
GLA_GATE_NORM = 16.0
GLA_CHUNK = 64
A_PROJ = 2 * GLA_KEY_DIM + 2 * GLA_VAL_DIM + GLA_GATE_RANK

SWA_HEAD_DIM = 64
SWA_Q_HEADS = D_MODEL // SWA_HEAD_DIM
SWA_GROUP = 8
SWA_KV_HEADS = SWA_Q_HEADS // SWA_GROUP
WINDOW = 128
BLOCK = 128
KV_PROJ = 2 * SWA_KV_HEADS * SWA_HEAD_DIM

REL_BUCKETS = 32
REL_MAX_DIST = 128

D_FF_2 = 4 * D_MODEL
EPS = 1e-6
NEG = -1e30


def rmsnorm(x, g):
    xf = x.astype(jnp.float32)
    y = xf * lax.rsqrt(jnp.mean(xf * xf, axis=-1, keepdims=True) + EPS) * g.astype(jnp.float32)
    return y.astype(x.dtype)

def sq_relu_mlp(h, w_up, w_down):
    u = jax.nn.relu(h @ w_up)
    return (u * u) @ w_down

def gla_mixer(h, w_in, w_gk2, b_gk, g_onorm, w_out):
    B, T, _ = h.shape
    C = GLA_CHUNK
    NC = T // C
    f32 = jnp.float32
    proj = h @ w_in
    q, k, v, gate, glr = jnp.split(
        proj, [GLA_KEY_DIM, 2 * GLA_KEY_DIM, 2 * GLA_KEY_DIM + GLA_VAL_DIM,
               2 * GLA_KEY_DIM + 2 * GLA_VAL_DIM], axis=-1)
    gk = jax.nn.log_sigmoid((glr @ w_gk2 + b_gk).astype(f32)) / GLA_GATE_NORM

    def heads(t, d):
        return t.astype(f32).reshape(B, NC, C, GLA_HEADS, d).transpose(1, 0, 3, 2, 4)

    qf = heads(q, GLA_HK) * (GLA_HK ** -0.5)
    kf = heads(k, GLA_HK)
    vf = heads(v, GLA_HV)
    bcum = jnp.cumsum(heads(gk, GLA_HK), axis=-2)
    q_t = qf * jnp.exp(bcum)
    k_t = kf * jnp.exp(-bcum)
    causal = jnp.asarray(np.tril(np.ones((C, C), dtype=bool)))
    attn = jnp.where(causal, jnp.einsum('nbhik,nbhjk->nbhij', q_t, k_t), 0.0)
    o_intra = jnp.einsum('nbhij,nbhjv->nbhiv', attn, vf)
    b_last = bcum[..., -1:, :]
    k_dec = kf * jnp.exp(b_last - bcum)

    def step(S, xs):
        q_c, k_c, v_c, bl = xs
        o = jnp.einsum('bhik,bhkv->bhiv', q_c, S)
        S = S * jnp.exp(bl)[..., 0, :, None] + jnp.einsum('bhjk,bhjv->bhkv', k_c, v_c)
        return S, o

    S0 = jnp.zeros((B, GLA_HEADS, GLA_HK, GLA_HV), f32)
    _, o_inter = lax.scan(step, S0, (q_t, k_dec, vf, b_last))
    o = (o_intra + o_inter).transpose(1, 0, 3, 2, 4).reshape(B, T, GLA_HEADS, GLA_HV)
    o = o * lax.rsqrt(jnp.mean(o * o, axis=-1, keepdims=True) + EPS) * g_onorm.astype(f32)
    o = o * jax.nn.silu(gate.astype(f32).reshape(B, T, GLA_HEADS, GLA_HV))
    return o.reshape(B, T, GLA_VAL_DIM).astype(h.dtype) @ w_out

def rel_bucket_band():
    i = np.arange(BLOCK)[:, None]
    j = np.arange(2 * BLOCK)[None, :]
    dist = i + BLOCK - j
    n = np.maximum(dist, 0)
    max_exact = REL_BUCKETS // 2
    large = max_exact + (np.log(np.maximum(n, 1) / max_exact)
                         / np.log(REL_MAX_DIST / max_exact)
                         * (REL_BUCKETS - max_exact)).astype(np.int32)
    large = np.minimum(large, REL_BUCKETS - 1)
    bucket = np.where(n < max_exact, n, large).astype(np.int32)
    valid = (dist >= 0) & (dist < WINDOW)
    return bucket, valid

def shared_kv(h, w_kv):
    B, T, _ = h.shape
    NB = T // BLOCK
    k, v = jnp.split(h @ w_kv, 2, axis=-1)

    def band(t):
        t = t.reshape(B, NB, BLOCK, SWA_KV_HEADS, SWA_HEAD_DIM)
        prev = jnp.concatenate([jnp.zeros_like(t[:, :1]), t[:, :-1]], axis=1)
        return jnp.concatenate([prev, t], axis=2)

    return band(k), band(v)

def swa_mixer(h, kb, vb, w_q, sinks, rel_table, w_out):
    B, T, _ = h.shape
    NB = T // BLOCK
    q = (h @ w_q).reshape(B, NB, BLOCK, SWA_KV_HEADS, SWA_GROUP, SWA_HEAD_DIM)
    s = jnp.einsum('bnqhgd,bnkhd->bnhgqk', q, kb).astype(jnp.float32) * (SWA_HEAD_DIM ** -0.5)
    bucket, valid = rel_bucket_band()
    bias = rel_table.astype(jnp.float32)[bucket]
    bias = bias.transpose(2, 0, 1).reshape(SWA_KV_HEADS, SWA_GROUP, BLOCK, 2 * BLOCK)
    first = (np.arange(NB)[:, None] == 0) & (np.arange(2 * BLOCK)[None, :] < BLOCK)
    mask = jnp.asarray(valid[None] & ~first[:, None, :])
    s = jnp.where(mask[None, :, None, None], s + bias, NEG)
    sink = sinks.astype(jnp.float32).reshape(SWA_KV_HEADS, SWA_GROUP, 1, 1)
    m = jnp.maximum(jnp.max(s, axis=-1, keepdims=True), sink)
    p = jnp.exp(s - m)
    p = p / (jnp.sum(p, axis=-1, keepdims=True) + jnp.exp(sink - m))
    o = jnp.einsum('bnhgqk,bnkhd->bnqhgd', p.astype(vb.dtype), vb)
    return o.reshape(B, T, SWA_Q_HEADS * SWA_HEAD_DIM) @ w_out

def second_inputs(seed: int = 0) -> dict:
    key = jax.random.key(seed)
    ks = jax.random.split(key, 20)
    f32 = jnp.float32

    def w(k, shape, fan_in, scale=1.0):
        return jax.random.normal(k, shape, f32) * (scale * fan_in ** -0.5)

    def gain(k, shape):
        return 1.0 + 0.02 * jax.random.normal(k, shape, f32)

    return {
        "x": jax.random.normal(ks[0], (BATCH, SEQ, D_MODEL), f32),
        "a_w_in": w(ks[1], (N_A_LAYERS, D_MODEL, A_PROJ), D_MODEL),
        "a_w_gk2": w(ks[2], (N_A_LAYERS, GLA_GATE_RANK, GLA_KEY_DIM), GLA_GATE_RANK),
        "a_b_gk": 0.1 * jax.random.normal(ks[3], (N_A_LAYERS, GLA_KEY_DIM), f32),
        "a_onorm": gain(ks[4], (N_A_LAYERS, GLA_HV)),
        "a_w_out": w(ks[5], (N_A_LAYERS, GLA_VAL_DIM, D_MODEL), GLA_VAL_DIM),
        "kv_norm": gain(ks[6], (D_MODEL,)),
        "w_kv": w(ks[7], (D_MODEL, KV_PROJ), D_MODEL),
        "b_w_q": w(ks[8], (N_B_LAYERS, D_MODEL, SWA_Q_HEADS * SWA_HEAD_DIM), D_MODEL),
        "b_sinks": 0.5 * jax.random.normal(ks[9], (N_B_LAYERS, SWA_Q_HEADS), f32),
        "b_w_out": w(ks[10], (N_B_LAYERS, SWA_Q_HEADS * SWA_HEAD_DIM, D_MODEL), D_MODEL),
        "rel_table": 0.5 * jax.random.normal(ks[11], (REL_BUCKETS, SWA_Q_HEADS), f32),
        "ln_mix": gain(ks[12], (DEPTH_2, D_MODEL)),
        "ln_mlp": gain(ks[13], (DEPTH_2, D_MODEL)),
        "w_up": w(ks[14], (DEPTH_2, D_MODEL, D_FF_2), D_MODEL),
        "w_down": w(ks[15], (DEPTH_2, D_FF_2, D_MODEL), D_FF_2, scale=0.5),
        "ln_final": gain(ks[16], (D_MODEL,)),
    }

def second_block(x, a_w_in, a_w_gk2, a_b_gk, a_onorm, a_w_out, kv_norm, w_kv, b_w_q, b_sinks,
              b_w_out, rel_table, ln_mix, ln_mlp, w_up, w_down, ln_final):
    h = x
    kb = vb = None
    for layer in range(DEPTH_2):
        if layer < N_A_LAYERS:
            h = h + gla_mixer(rmsnorm(h, ln_mix[layer]), a_w_in[layer], a_w_gk2[layer],
                              a_b_gk[layer], a_onorm[layer], a_w_out[layer])
        else:
            if layer == N_A_LAYERS:
                kb, vb = shared_kv(rmsnorm(h, kv_norm), w_kv)
            j = layer - N_A_LAYERS
            h = h + swa_mixer(rmsnorm(h, ln_mix[layer]), kb, vb, b_w_q[j], b_sinks[j],
                              rel_table, b_w_out[j])
        h = h + sq_relu_mlp(rmsnorm(h, ln_mlp[layer]), w_up[layer], w_down[layer])
    return rmsnorm(h, ln_final)


def setup_inputs(seed=0):
    out = dict(first_inputs(seed))
    for name, value in second_inputs(seed + 1).items():
        if name != "x":
            out[name + "_2"] = value
    return out


def reference(
    x, mem, norm_mix_w, w_in, mu_shift, w_decay0, w_decay_up, a0, a_up, g_up, k_k, k_a, r_k,
    lnx_w, lnx_b, lam_q1, lam_k1, lam_q2, lam_k2, subln_w, w_out, norm_mem_w, norm_src_w, w_mq,
    w_mk, w_mv, w_mo, norm_mlp_w, w_up, w_down, norm_final_w, a_w_in_2, a_w_gk2_2, a_b_gk_2,
    a_onorm_2, a_w_out_2, kv_norm_2, w_kv_2, b_w_q_2, b_sinks_2, b_w_out_2, rel_table_2,
    ln_mix_2, ln_mlp_2, w_up_2, w_down_2, ln_final_2,
):
    x = first_block(
        x, mem, norm_mix_w, w_in, mu_shift, w_decay0, w_decay_up, a0, a_up, g_up, k_k, k_a, r_k,
        lnx_w, lnx_b, lam_q1, lam_k1, lam_q2, lam_k2, subln_w, w_out, norm_mem_w, norm_src_w,
        w_mq, w_mk, w_mv, w_mo, norm_mlp_w, w_up, w_down, norm_final_w,
    )
    return second_block(
        x, a_w_in_2, a_w_gk2_2, a_b_gk_2, a_onorm_2, a_w_out_2, kv_norm_2, w_kv_2, b_w_q_2,
        b_sinks_2, b_w_out_2, rel_table_2, ln_mix_2, ln_mlp_2, w_up_2, w_down_2, ln_final_2,
    )


_drawn_inputs = setup_inputs


def setup_inputs(seed=0):
    import zlib

    import numpy as np

    out = dict(_drawn_inputs(seed))
    spreads = {}
    factors = {'a0': 3.046,
     'k_k': 3.122,
     'lnx_b': 5.122,
     'lam_k2': 2.738,
     'norm_mem_w': 8.0,
     'norm_src_w': 5.659,
     'a_onorm_2': 5.146,
     'kv_norm_2': 8.0,
     'b_sinks_2': 30.828,
     'ln_mlp_2': 3.868,
     'ln_final_2': 7.453}
    for name, (base, spread) in spreads.items():
        noise = np.random.default_rng([zlib.crc32(name.encode()), seed]).standard_normal(out[name].shape)
        drawn = base * np.exp(spread * noise) if base else spread * noise
        out[name] = __import__('jax').numpy.asarray(drawn.astype(out[name].dtype))
    for name, factor in factors.items():
        out[name] = (out[name] * factor).astype(out[name].dtype)
    return out
```

```python
import math
from contextlib import ExitStack

import numpy as np

import concourse.bass as bass
from concourse import mybir

P = 128
T = 512
D = 1024
KT = D // P
BW = 256
TT = T // P
MEM = 256
RW_COLS, RW_W, DIFF_W = 1792, 512, 512
FF = 4 * D
LAM_INIT = 0.8 - 0.6 * math.exp(-0.3 * 0)
C0 = math.exp(-0.5)
NEG = -1e30

VECS = [("norm_mix_w", 8), ("norm_src_w", 8), ("norm_mem_w", 8), ("norm_mlp_w", 8), ("norm_final_w", 8),
        ("mu_shift", 14), ("w_decay0", 4), ("a0", 4), ("k_k", 4), ("k_a", 4), ("r_k", 4), ("lnx_w", 4),
        ("lnx_b", 4), ("subln_w", 1), ("a_b_gk_2", 4), ("a_onorm_2", 2), ("kv_norm_2", 8), ("ln_mix_2", 16),
        ("ln_mlp_2", 16), ("ln_final_2", 8)]
VEC_ROW, _r = {}, 0
for _n, _k in VECS:
    VEC_ROW[_n] = _r
    _r += _k
VEC_ROWS = _r

CONST, _c = {}, 0
for _n, _k in [("ident", 128), ("ones", 128), ("blk64", 128), ("seg", 512), ("lower", 64), ("upper", 64),
               ("upper_in", 64), ("low16", 64), ("up16", 64), ("low32", 64), ("low64", 64), ("eye64", 64),
               ("gla", 128), ("sel0", 128), ("sel1", 128), ("plusminus", 128), ("eps5", 1), ("eps6", 1),
               ("epsgn", 1), ("kkb", 1), ("one", 1), ("zero", 1), ("pad", 2)]:
    CONST[_n] = (_c, _k)
    _c += _k
CONST_COLS = _c


def constants():
    out = np.zeros((P, CONST_COLS), np.float32)

    def put(name, value):
        at, n = CONST[name]
        out[:, at:at + n] = value

    p = np.arange(P)[:, None]
    f = np.arange(P)[None, :]
    a, b = p % 64, np.arange(64)[None, :]
    put("ident", p == f)
    put("ones", 1.0)
    put("blk64", p // 64 == f // 64)
    put("seg", (np.arange(T) % 64 != 0)[None, :])
    put("lower", b < a)
    put("upper", a < b)
    put("upper_in", a <= b)
    put("low16", (b < a) & (a // 16 == b // 16))
    put("up16", (a < b) & (a // 16 == b // 16))
    put("low32", (a // 32 == b // 32) & (a // 16 > b // 16))
    put("low64", a // 32 > b // 32)
    put("eye64", a == b)
    put("gla", (p // 64 == f // 64) & (p <= f))
    put("sel0", p == f % 64)
    put("sel1", p == 64 + f % 64)
    put("plusminus", np.where(p == 0, 1.0, np.where(p == 1, -1.0, 0.0)))
    put("eps5", 1e-5)
    put("eps6", 1e-6)
    put("epsgn", 64e-5)
    put("kkb", 10.0 * math.log(2.0))
    put("one", 1.0)
    return out


def bucket_onehot():
    dist = 255 - np.arange(384)
    n = np.maximum(dist, 0)
    large = 16 + (np.log(np.maximum(n, 1) / 16) / np.log(128 / 16) * 16).astype(np.int32)
    bucket = np.where(n < 16, n, np.minimum(large, 31))
    valid = (dist >= 0) & (dist < 128)
    hot = (bucket[None, :] == np.arange(32)[:, None]) & valid[None, :]
    out = np.zeros((33, 384), np.float32)
    out[:32] = hot
    out[32] = np.where(valid, 0.0, NEG)
    return out


N_DQ, N_DK, N_DV, N_RW = 0, 2, 4, 6
N_WOUT, N_MK, N_MV, N_MQ, N_MO, N_MLP1 = 13, 17, 21, 25, 29, 33
N_GLR, N_GQK, N_GV, N_GG, N_GOUT, N_MLP2 = 65, 66, 70, 74, 78, 82
N_KV, N_WQ, N_SOUT, N_MLP3 = 114, 115, 119, 123
N_END = 155


def acc_before(n):
    return 2 * n - 16 * sum(n >= m + 32 for m in (N_MLP1, N_MLP2, N_MLP3))


RW_STEPS = (["kk2", "bonus", "tA", "tBd", "tKd", "tV", "L", "LT", "RBT", "AKT", "RKT", "X", "P2", "PT2", "TT2", "P4",
             "PT4", "TT3", "P8", "TT4", "T4", "Z", "TT5", "T5", "Z2", "TT6", "W", "G", "MT", "N", "RT"]
            + [f"S{c}" for c in range(1, 7)] + ["Y", "mean", "var", "gate"])
RW_SEQ = []
for _g in range(2):
    RW_SEQ += [(st, hp) for st in ["zw", "za"] + RW_STEPS for hp in (2 * _g, 2 * _g + 1)]
RW_NO = {x: i for i, x in enumerate(RW_SEQ)}


def program(nc, A, out):
    f32, f32r, i32 = mybir.dt.float32, mybir.dt.float32r, mybir.dt.int32
    ALU, ACT, AX = mybir.AluOpType, mybir.ActivationFunctionType, mybir.AxisListType
    ds = bass.ds
    ctx = ExitStack()
    with ctx:
        sem_names = """ld_const ld_vec ld_small ld_lora ld_x ld_mem ld_gk ld_bias ld_rel st_bias st_out raw_lo
            w_hi_ready w_lo_ready acc_done acc_evac vec_tr vec_ready xt_tr xt_ev bias_mm bias_ev
            norm_sq norm_add norm_ss norm_ln norm_rstd norm_x x_hi x_lo h_final
            lam_mul lam_e lam_mm lam_ready
            da_score da_fill da_max da_neg da_exp da_rz da_c2 da_e1 da_attn da_tr da_at da_pv da_o
            da_sq da_ss da_ln da_rstd da_y
            rw_zero rw_shift rw_p rw_act rw_dve rw_half rw_mm rw_ev rw_exp y_hi y_lo
            mt_tr mt_ev ma_score ma_max ma_neg ma_exp ma_rz ma_p ma_tr ma_pt ma_pv ma_hi ma_lo
            up_sq up_hi up_lo
            g_gk g_ab g_ln g_act g_dve g_sc g_at g_kt g_ktev g_n g_s g_o g_oev g_sq g_ss g_rl g_rstd g_hi g_lo g_zero g_o1 g_cs
            sw_dup sw_dupev sw_score sw_s sw_mx sw_m sw_neg sw_e sw_es sw_den sw_rd sw_p sw_tr sw_pt sw_pv sw_hi sw_lo
            fin_tr fin_ev dve_link act_link""".split()
        S = {n: ctx.enter_context(nc.semaphore(n)) for n in sem_names}
        w_arrived = [ctx.enter_context(nc.semaphore(f"w_arrived{i}")) for i in range(4)]

        def at(off, name, shape, dt=f32):
            nbytes = 4 * int(np.prod(shape[1:]))
            t = nc.alloc_sbuf_tensor_at(name, shape, dt, offset=off[0])
            off[0] += (nbytes + 31) // 32 * 32
            return t

        o = [16512]
        h = at(o, "h", [P, KT, T])
        raw = at(o, "raw", [P, 4, KT, BW])
        w_hi = at(o, "w_hi", [P, 2, KT, BW], f32r)
        w_lo = at(o, "w_lo", [P, 2, KT, BW], f32r)
        cst = at(o, "cst", [P, CONST_COLS])
        vec = at(o, "vec", [P, VEC_ROWS])
        rstd = at(o, "rstd", [P, T])
        nt = [at(o, f"nt{i}", [P, T]) for i in range(3)]
        small = at(o, "small", [P, 128])
        arena = o[0]

        o = [arena]
        y_diff = at(o, "y_diff", [P, 4, T])
        p_rw = at(o, "p_rw", [P, 14, T + 1])
        lora = at(o, "lora", [P, RW_W])
        g_up = at(o, "g_up", [P, RW_W])
        mixing = o[0]
        xm_hi, xm_lo = at(o, "xm_hi", [P, KT, T], f32r), at(o, "xm_lo", [P, KT, T], f32r)
        dq, dk = at(o, "dq", [P, 4, T]), at(o, "dk", [P, 4, T])
        dv = at(o, "dv", [P, TT, DIFF_W])
        de_sq = nt[0]
        de = [at(o, f"de{i}", [P, T]) for i in range(2)]
        da_t = at(o, "da_t", [P, TT, P])
        da_out = at(o, "da_out", [P, T])
        top1 = o[0]
        o = [mixing + 2 * 4 * KT * T]
        xt = at(o, "xt", [P, TT, D])
        vrow = at(o, "vrow", [P, 2, P])
        lamv = at(o, "lamv", [2, 2, 64])
        o = [mixing]
        tm = [[at(o, f"tm{b}_{i}", [P, 4, P]) for i in range(4)] for b in range(2)]
        mt = [[at(o, f"mt{b}_{i}", [P, T]) for i in range(11)] for b in range(2)]
        bon = [at(o, f"bon{b}", [P, T]) for b in range(2)]
        top2 = o[0]
        o = [mixing]
        y_hi, y_lo = at(o, "yy_hi", [P, KT, T], f32r), at(o, "yy_lo", [P, KT, T], f32r)
        mrow = at(o, "mrow", [P, 2, D])
        memT = at(o, "memT", [P, KT, MEM])
        m_hi, m_lo = at(o, "m_hi", [P, KT, MEM], f32r), at(o, "m_lo", [P, KT, MEM], f32r)
        top3 = o[0]
        o = [mixing + 2 * 4 * KT * T]
        onehot = at(o, "onehot_sb", [33, 384])
        relx = at(o, "relx", [33, 16])
        biasrow = [at(o, f"biasrow{i}", [P, 384]) for i in range(2)]
        o = [arena]
        mk = at(o, "mk", [P, KT, MEM])
        mv = at(o, "mv", [P, 2, D])
        mq = at(o, "mq", [P, KT, T])
        me = [at(o, f"me{i}", [P, MEM]) for i in range(2)]
        mpt = [at(o, f"mpt{i}", [P, 2, P]) for i in range(2)]
        assert o[0] <= mixing
        o = [arena]
        f_hi, f_lo = at(o, "f_hi", [P, KT, T], f32r), at(o, "f_lo", [P, KT, T], f32r)
        u_hi, u_lo = at(o, "u_hi", [P, 16, T], f32r), at(o, "u_lo", [P, 16, T], f32r)
        ut, us = [at(o, f"ut{i}", [P, T]) for i in range(2)], [nt[0], nt[1]]
        top4 = o[0]
        o = [arena]
        g_hi, g_lo_ = at(o, "gx_hi", [P, KT, T], f32r), at(o, "gx_lo", [P, KT, T], f32r)
        gq, gk, gb = (at(o, n, [P, 4, T]) for n in ("gq", "gk", "gb"))
        gv = at(o, "gv", [P, TT, D])
        gg = at(o, "gg", [P, KT, T])
        gs = [at(o, f"gs{i}", [P, 4, 256]) for i in range(2)]
        gat = [at(o, f"gat{i}", [P, 4, P]) for i in range(2)]
        gkt = at(o, "gkt", [P, 4, P])
        glr = at(o, "glr", [16, T])
        w_gk2 = at(o, "w_gk2", [16, 512])
        top5 = o[0]
        o = [arena]
        s_hi, s_lo = at(o, "sx_hi", [P, KT, T], f32r), at(o, "sx_lo", [P, KT, T], f32r)
        kf = at(o, "kf", [P, T])
        kd = [at(o, f"kd{i}", [P, T]) for i in range(2)]
        sv = at(o, "sv", [P, TT, P])
        sq = at(o, "sq", [P, KT, T])
        bias = at(o, "bias", [P, 16, 256])
        sc = [at(o, f"sc{i}", [P, 2, 256]) for i in range(2)]
        spt = [at(o, f"spt{i}", [P, 4, P]) for i in range(2)]
        top6 = o[0]
        ytm = sq
        assert max(top1, top2, top3, top4, top5, top6) <= 16481 + 212863, (top1, top2, top3, top4, top5, top6)

        Mall = ctx.enter_context(nc.psum_tensor("M", [P, 4, T], f32))
        Xall = ctx.enter_context(nc.psum_tensor("X", [P, 4, T], f32))
        M, X = [Mall[:, i, :] for i in range(4)], [Xall[:, i, :] for i in range(4)]
        RB = X + M

        def sw_banks(u):
            return (Xall[:, 0:2, :], Mall[:, 2:4, :])[u % 2]

        bias_rows = nc.dram_tensor("bias_rows", [16, P, 384], f32, kind="Internal").ap()

        def ytm_view(t):
            return ytm[:, 2 * t:2 * t + 2, :].rearrange("p a n -> p (a n)")

        def C(name, rows=slice(0, P)):
            a, n = CONST[name]
            return cst[rows, a:a + n]

        def V(name, i, rows=slice(0, P)):
            return vec[rows, VEC_ROW[name] + i:VEC_ROW[name] + i + 1]

        lamneg, lame = small[:, 0:1], small[0:2, 1:2]
        lamd, onec = small[0:2, 2:3], small[:, 3:4]
        da_mx, da_ng, da_z, da_r, da_c = (small[:, 4 + 2 * i:6 + 2 * i] for i in range(5))
        sub_w = small[:, 14:15]
        ma_mx, ma_ng, ma_z, ma_r = (small[:, 16 + i:17 + i] for i in range(4))
        sinkb = small[:, 32:48]
        sw_mx_, sw_ng_, sw_z_, sw_es_, sw_r_ = (small[:, 48 + 2 * i:50 + 2 * i] for i in range(5))
        g_el = small[:, 64:96]
        rw_dc = [small[:, 96:104], small[:, 104:112]]
        seg = C("seg")

        def W(ap):
            return ap.rearrange("(k p) n -> p k n", p=P)

        w_in, a_in = W(A["w_in"][0]), W(A["a_w_in_2"][0])
        plain = [(N_DQ, 2, w_in, RW_COLS), (N_DK, 2, w_in, RW_COLS + 512), (N_DV, 2, w_in, RW_COLS + 1024),
                 (N_RW, 7, w_in, 0), (N_WOUT, 4, W(A["w_out"][0]), 0), (N_MK, 4, W(A["w_mk"][0]), 0),
                 (N_MV, 4, W(A["w_mv"][0]), 0), (N_MQ, 4, W(A["w_mq"][0]), 0), (N_MO, 4, W(A["w_mo"][0]), 0),
                 (N_GLR, 1, a_in, 3072), (N_GQK, 4, a_in, 0), (N_GV, 4, a_in, 1024), (N_GG, 4, a_in, 2048),
                 (N_GOUT, 4, W(A["a_w_out_2"][0]), 0), (N_KV, 1, W(A["w_kv_2"]), 0), (N_WQ, 4, W(A["b_w_q_2"][0]), 0),
                 (N_SOUT, 4, W(A["b_w_out_2"][0]), 0)]
        mlps = {N_MLP1: (W(A["w_up"][0]), W(A["w_down"][0])), N_MLP2: (W(A["w_up_2"][0]), W(A["w_down_2"][0])),
                N_MLP3: (W(A["w_up_2"][1]), W(A["w_down_2"][1]))}
        GLR = 16

        HF = 8 * 2
        LAST = N_END
        NVEC = len(VECS) + 1
        bias_skewed = lambda: bass.AP(bias_rows.tensor, P - 1, [[384 - 1, P], [P * 384, 16], [1, 256]])
        block = ctx.enter_context(nc.Block())

        SLOT = dict(P=0, Bd=1, B=2, Kd=3, PT=4, O32=5, O64=6, RBT=7, AKT=8, RKT=9, A=10,
                    P2=1, PT2=3, TT=2, P4=0, PT4=4, P8=1, T=3, Z=4, W=0, G=1, MT=5, N=6, RT=8, X=10, S=3, Y=4,
                    cs=5, sw=6, ex=0, inc=4, neg=7, dec=8, a=9, kk=10, t=1, d=2, dsq=5, rs=7)
        RW_ACT = ["sigw", "siga", "ex", "inc", "neg", "dec", "dc", "sq", "ln", "rn", "dsq", "gln", "grs"]
        RW_DVE = ["csx", "dl", "kkraw", "kmod", "kk", "rk", "beta", "K", "Kd", "R", "B", "Bd", "A", "yb", "yc"]
        pairs = [(0, 1), (2, 3)]
        ACT_NO = {x: i + 3 for i, x in enumerate((op, hp) for g in pairs for op in RW_ACT for hp in g)}
        DVE_NO = {x: i + 1 for i, x in enumerate((op, hp) for g in pairs for op in RW_DVE for hp in g)}

        def ev(st, hp):
            return RW_NO[(st, hp)] + 1

        def sl(name, hp):
            return mt[hp % 2][SLOT[name]]

        def rkv(i, hp, lo_=1):
            return p_rw[:, 4 * i + hp, lo_:lo_ + T]

        def rwkv_pe(pe, mm, wait):
            def blk(t, hh, cp, cpar):
                return t[64 * cpar:64 * cpar + 64, (4 * hh + cp) * 64:(4 * hh + cp) * 64 + 64]

            def fm(t, hh, c):
                return t[64 * hh:64 * hh + 64, 64 * c:64 * c + 64]

            def tmv(i, hp, hh, cp, cpar):
                return tm[hp % 2][i][64 * cpar:64 * cpar + 64, cp, 64 * hh:64 * hh + 64]

            mats = dict(X=("AKT", "V"), P2=("PT", "P"), PT2=("P", "PT"), TT2=("P2", "TT"), P4=("PT2", "P2"),
                        PT4=("P2", "PT2"), TT3=("P4", "TT"), P8=("PT4", "P4"), TT4=("P8", "TT"), T4=("TT", "eye"),
                        Z=("O32", "TT"), TT5=("T", "Z"), T5=("Z", "T"), Z2=("O64", "TT"), TT6=("T", "Z"),
                        W=("TT", "Atm"), G=("TT", "X"))
            feats = dict(L=("A", "B"), LT=("B", "A"), RBT=("B", "R"), AKT=("K", "A"), RKT=("K", "R"))
            tms = dict(Atm=0, Bdtm=1, Kdtm=2, V=3)
            after = dict(L=("dve", "A"), LT=("dve", "A"), RBT=("dve", "A"), AKT=("dve", "A"), RKT=("dve", "A"),
                         tA=("dve", "A"), tBd=("dve", "A"), tKd=("dve", "A"), tV=("dve", "A"), kk2=("act", "sq"),
                         bonus=("dve", "rk"), X="AKT", P2="RBT", PT2="RBT", TT2="P2", P4="PT2", PT4="PT2", TT3="P4",
                         P8="PT4", TT4="P8", T4="TT4", Z="TT4", TT5="Z", T5="TT5", Z2="TT5", TT6="Z2", W="TT6", G="TT6",
                         MT="W", N="G", RT="W", S1="N", Y="S6", mean="Y", var=("act", "dsq"), gate="mean")
            for i in range(2, 7):
                after[f"S{i}"] = f"S{i - 1}"

            def operand(name, hp, hh, cp, cpar):
                if name == "eye":
                    return C("eye64", slice(64 * cpar, 64 * cpar + 64))
                if name in tms:
                    return tmv(tms[name], hp, hh, cp, cpar)
                return blk(sl(name, hp), hh, cp, cpar)

            halves = [0]

            def half_done(ins):
                ins.then_inc(S["rw_half"], 1)
                halves[0] += 1
                wait("rw_half", halves[0])

            for (st, hp), no in RW_NO.items():
                bank = RB[no % 8]
                if no >= 8:
                    wait("rw_ev", no - 7)
                dep = after.get(st)
                if isinstance(dep, tuple):
                    wait("rw_act" if dep[0] == "act" else "rw_dve", (ACT_NO if dep[0] == "act" else DVE_NO)[(dep[1], hp)])
                elif dep:
                    wait("rw_ev", ev(dep, hp))
                fs = slice(hp * P, hp * P + P)
                if st == "zw":
                    wait("ld_lora", 48)
                    last = mm(bank[:], lora[0:64, fs], p_rw[0:64, 12, 1:T + 1], start=True, stop=True)
                elif st == "za":
                    last = mm(bank[:], lora[64:128, fs], p_rw[64:128, 12, 1:T + 1], start=True, stop=True)
                elif st == "gate":
                    last = mm(bank[:], g_up[:, fs], p_rw[:, 13, 1:T + 1], start=True, stop=True)
                elif st in ("kk2", "bonus"):
                    last = mm(bank[:], C("blk64"), nt[hp % 2][:], start=True, stop=True)
                elif st in ("mean", "var"):
                    last = mm(bank[:], C("blk64"), sl("Y" if st == "mean" else "dsq", hp)[:], start=True, stop=True)
                elif st in ("tA", "tBd", "tKd", "tV"):
                    src = rkv(2, hp) if st == "tV" else sl(st[1:], hp)[:]
                    for cp in range(4):
                        last = nc.tensor.transpose(bank[:, cp * P:cp * P + P], src[:, cp * P:cp * P + P], C("ident"))
                elif st in feats:
                    a_, b_ = (rkv(0 if n == "R" else 1, hp) if n in "RK" else sl(n, hp) for n in feats[st])
                    for hh in range(2):
                        if hh:
                            half_done(last)
                        for cp in range(4):
                            for cpar in range(2):
                                c = 2 * cp + cpar
                                last = mm(blk(bank, hh, cp, cpar), fm(a_, hh, c), fm(b_, hh, c), start=True, stop=True)
                elif st in mats:
                    for hh in range(2):
                        for cp in range(4):
                            for cpar in range(2):
                                a_, b_ = (operand(n, hp, hh, cp, cpar) for n in mats[st])
                                last = mm(blk(bank, hh, cp, cpar), a_, b_, start=True, stop=True)
                elif st[0] == "S":
                    c = int(st[1:])
                    for hh in range(2):
                        last = mm(bank[64 * hh:64 * hh + 64, 0:64], fm(sl("MT", hp), hh, c), fm(sl("S", hp), hh, c),
                                  start=True, stop=True)
                elif st != "Y":
                    for turn in range(2):
                        if turn:
                            half_done(last)
                        for cp in range(4):
                            for cpar in range(2):
                                hh = cpar ^ turn
                                o_ = fm(bank, hh, 2 * cp + cpar)
                                if st == "MT":
                                    last = mm(o_, blk(sl("W", hp), hh, cp, cpar), tmv(1, hp, hh, cp, cpar), start=True, stop=True)
                                elif st == "RT":
                                    last = mm(o_, blk(sl("W", hp), hh, cp, cpar), blk(sl("RBT", hp), hh, cp, cpar), start=True, stop=True)
                                else:
                                    mm(o_, tmv(1, hp, hh, cp, cpar), blk(sl("G", hp), hh, cp, cpar), start=True, stop=False)
                                    last = mm(o_, tmv(2, hp, hh, cp, cpar), tmv(3, hp, hh, cp, cpar), start=False, stop=True)
                else:
                    for turn in range(2):
                        if turn:
                            half_done(last)
                        for cp in range(4):
                            for cpar in range(2):
                                hh = cpar ^ turn
                                o_ = fm(bank, hh, 2 * cp + cpar)
                                mm(o_, blk(sl("G", hp), hh, cp, cpar), blk(sl("RBT", hp), hh, cp, cpar),
                                   start=turn == 0 and cp == 0, stop=False, skip_group_check=True)
                                last = mm(o_, tmv(3, hp, hh, cp, cpar), blk(sl("RKT", hp), hh, cp, cpar), start=False,
                                          stop=False, skip_group_check=True)
                    half_done(last)
                    for c in range(1, 8):
                        for hh in range(2):
                            last = mm(fm(bank, hh, c), fm(sl("S", hp), hh, c), fm(sl("RT", hp), hh, c), start=False,
                                      stop=c == 7, skip_group_check=True)
                last.then_inc(S["rw_mm"], 1)

        def rwkv_act(act):
            def go(op, hp, out_, in_, func, **kw):
                nc.scalar.activation(out_, in_, func, **kw).then_inc(S["rw_act"], 1)

            def dve(op, hp):
                act.wait_ge(S["rw_dve"], DVE_NO[(op, hp)])

            def own(op, hp):
                act.wait_ge(S["rw_act"], ACT_NO[(op, hp)])

            for g in pairs:
                for hp in g:
                    act.wait_ge(S["rw_mm"], ev("zw", hp))
                    if hp >= 2:
                        act.wait_ge(S["rw_ev"], ev("gate", hp - 2))
                    go("sigw", hp, sl("sw", hp)[:], RB[RW_NO[("zw", hp)] % 8][:], ACT.Sigmoid, bias=V("w_decay0", hp))
                for hp in g:
                    act.wait_ge(S["rw_mm"], ev("za", hp))
                    go("siga", hp, sl("a", hp)[:], RB[RW_NO[("za", hp)] % 8][:], ACT.Sigmoid, bias=V("a0", hp))
                nc.scalar.preload_act_table_set("natural_log_exp_and_others")
                for hp in g:
                    dve("csx", hp)
                    go("ex", hp, sl("ex", hp)[:], sl("sw", hp)[:], ACT.Exp, scale=-C0)
                for hp in g:
                    go("inc", hp, sl("inc", hp)[:], sl("cs", hp)[:], ACT.Exp, scale=-C0)
                for hp in g:
                    go("neg", hp, sl("neg", hp)[:], sl("cs", hp)[:], ACT.Exp, scale=C0)
                for hp in g:
                    dve("dl", hp)
                    go("dec", hp, sl("dec", hp)[:], sl("dec", hp)[:], ACT.Exp, scale=-C0)
                for hp in g:
                    go("dc", hp, rw_dc[hp % 2], sl("cs", hp)[:].rearrange("p (c t) -> p c t", t=64)[:, :, 63], ACT.Exp,
                       scale=-C0)
                for hp in g:
                    dve("kkraw", hp)
                    go("sq", hp, nt[hp % 2][:], sl("kk", hp)[:], ACT.Square)
                for hp in g:
                    act.wait_ge(S["rw_ev"], ev("kk2", hp))
                    go("ln", hp, nt[hp % 2][:], nt[hp % 2][:], ACT.Ln, scale=float(2 ** 20))
                for hp in g:
                    own("ln", hp)
                    go("rn", hp, nt[hp % 2][:], nt[hp % 2][:], ACT.Exp, scale=-0.5, bias=C("kkb"))
                for hp in g:
                    act.wait_ge(S["rw_ev"], ev("mean", hp))
                    go("dsq", hp, sl("dsq", hp)[:], sl("d", hp)[:], ACT.Square)
                for hp in g:
                    act.wait_ge(S["rw_mm"], ev("var", hp))
                    go("gln", hp, sl("rs", hp)[:], RB[RW_NO[("var", hp)] % 8][:], ACT.Ln, scale=1.0 / 64, bias=C("epsgn"))
                for hp in g:
                    own("gln", hp)
                    go("grs", hp, sl("rs", hp)[:], sl("rs", hp)[:], ACT.Exp, scale=-0.5)

        def rwkv_dve(dve):
            TTO, TS, STT = nc.vector.tensor_tensor, nc.vector.tensor_scalar, nc.vector.scalar_tensor_tensor

            def a8(ap):
                return ap.rearrange("p (c t) -> p c t", t=64)

            def bank(st, hp):
                return RB[RW_NO[(st, hp)] % 8]

            def mm_done(st, hp):
                dve.wait_ge(S["rw_mm"], ev(st, hp))

            def evd(ins):
                ins.then_inc(S["rw_ev"], 1)

            def own(op, hp):
                dve.wait_ge(S["rw_dve"], DVE_NO[(op, hp)])

            def own_ev(st, hp):
                dve.wait_ge(S["rw_ev"], ev(st, hp))

            def act(op, hp):
                dve.wait_ge(S["rw_act"], ACT_NO[(op, hp)])

            def go(ins):
                ins.then_inc(S["rw_dve"], 1)

            def mask(name):
                return C(name).unsqueeze(1).to_broadcast([P, 8, 64])

            for g in pairs:
                for hp in g:
                    act("sigw", hp)
                    evd(nc.vector.tensor_tensor_scan(sl("cs", hp)[:], seg, sl("sw", hp)[:], 0.0, ALU.mult, ALU.add))
                for hp in g:
                    act("siga", hp)
                    evd(TS(sl("t", hp)[:], sl("a", hp)[:], -1.0, V("k_a", hp), ALU.add, ALU.mult))
                for hp in g:
                    own_ev("zw", hp)
                    go(TTO(sl("sw", hp)[:], sl("cs", hp)[:], sl("sw", hp)[:], ALU.subtract))
                for hp in g:
                    cs8 = a8(sl("cs", hp)[:])
                    go(TTO(a8(sl("dec", hp)[:]), cs8[:, :, 63:64].to_broadcast([P, 8, 64]), cs8, ALU.subtract))
                for hp in g:
                    go(TS(sl("kk", hp)[:], rkv(1, hp), V("k_k", hp), None, ALU.mult))
                for hp in g:
                    own_ev("za", hp)
                    go(STT(sl("t", hp)[:], sl("t", hp)[:], 1.0, rkv(1, hp), ALU.add, ALU.mult))
                for hp in g:
                    mm_done("kk2", hp)
                    evd(nc.vector.tensor_scalar_max(nt[hp % 2][:], bank("kk2", hp)[:], 1e-24))
                for hp in g:
                    act("rn", hp)
                    go(TTO(sl("kk", hp)[:], sl("kk", hp)[:], nt[hp % 2][:], ALU.mult))
                for hp in g:
                    own("kmod", hp)
                    own("kk", hp)
                    go(STT(nt[hp % 2][:], rkv(0, hp), V("r_k", hp), sl("t", hp)[:], ALU.mult, ALU.mult))
                for hp in g:
                    mm_done("bonus", hp)
                    evd(TTO(bon[hp % 2][:], bank("bonus", hp)[:], rkv(2, hp), ALU.mult))
                for hp in g:
                    go(TTO(sl("a", hp)[:], sl("kk", hp)[:], sl("a", hp)[:], ALU.mult))
                for hp in g:
                    act("dc", hp)
                    go(TTO(rkv(1, hp), sl("t", hp)[:], sl("neg", hp)[:], ALU.mult))
                for hp in g:
                    go(TTO(sl("Kd", hp)[:], sl("t", hp)[:], sl("dec", hp)[:], ALU.mult))
                for hp in g:
                    go(TTO(rkv(0, hp), rkv(0, hp), sl("inc", hp)[:], ALU.mult))
                for hp in g:
                    own("beta", hp)
                    go(TTO(sl("B", hp)[:], sl("a", hp)[:], sl("neg", hp)[:], ALU.mult))
                for hp in g:
                    own("Kd", hp)
                    go(TTO(sl("Bd", hp)[:], sl("a", hp)[:], sl("dec", hp)[:], ALU.mult))
                for hp in g:
                    go(STT(sl("A", hp)[:], sl("kk", hp)[:], -1.0, sl("ex", hp)[:], ALU.mult, ALU.mult))
                for i, st in enumerate(("tA", "tBd", "tKd", "tV")):
                    for hp in g:
                        mm_done(st, hp)
                        evd(nc.vector.tensor_copy(tm[hp % 2][i][:].rearrange("p c f -> p (c f)"), bank(st, hp)[:]))
                for hp in g:
                    mm_done("L", hp)
                    for name, m in (("P", "low16"), ("O32", "low32"), ("O64", "low64")):
                        last = TTO(a8(sl(name, hp)[:]), a8(bank("L", hp)[:]), mask(m), ALU.mult)
                    evd(last)
                for st, name, m in (("LT", "PT", "up16"), ("RBT", "RBT", "upper_in"), ("AKT", "AKT", "upper"),
                                    ("RKT", "RKT", "upper_in")):
                    for hp in g:
                        mm_done(st, hp)
                        if st == "RBT":
                            own_ev("LT", hp)
                            TTO(a8(sl("TT", hp)[:]), a8(sl("PT", hp)[:]), mask("eye64"), ALU.add)
                        evd(TTO(a8(sl(name, hp)[:]), a8(bank(st, hp)[:]), mask(m), ALU.mult))
                for st, name, add in (("X", "X", 0), ("P2", "P2", 0), ("PT2", "PT2", 0), ("TT2", "TT", 1), ("P4", "P4", 0),
                                      ("PT4", "PT4", 0), ("TT3", "TT", 1), ("P8", "P8", 0), ("TT4", "TT", 1), ("T4", "T", 0),
                                      ("Z", "Z", 0), ("TT5", "TT", 1), ("T5", "T", 1), ("Z2", "Z", 0), ("TT6", "TT", 1),
                                      ("W", "W", 0), ("G", "G", 0)):
                    for hp in g:
                        mm_done(st, hp)
                        if add:
                            evd(TTO(sl(name, hp)[:], bank(st, hp)[:], sl(name, hp)[:], ALU.add))
                        else:
                            evd(nc.vector.tensor_copy(sl(name, hp)[:], bank(st, hp)[:]))
                for hp in g:
                    mm_done("MT", hp)
                    go_diag = TTO(a8(sl("MT", hp)[:]), mask("eye64"),
                                  rw_dc[hp % 2].unsqueeze(2).to_broadcast([P, 8, 64]), ALU.mult)
                    go_diag.then_inc(S["dve_link"], 1)
                    dve.wait_ge(S["dve_link"], hp + 1)
                    evd(TTO(sl("MT", hp)[:], bank("MT", hp)[:], sl("MT", hp)[:], ALU.add))
                for hp in g:
                    mm_done("N", hp)
                    nc.vector.tensor_copy(sl("S", hp)[:, 64:128], bank("N", hp)[:, 0:64])
                    evd(nc.vector.tensor_copy(sl("N", hp)[:], bank("N", hp)[:]))
                for hp in g:
                    mm_done("RT", hp)
                    evd(TTO(sl("RT", hp)[:], bank("RT", hp)[:], rkv(0, hp), ALU.add))
                for c in range(1, 7):
                    for hp in g:
                        mm_done(f"S{c}", hp)
                        evd(TTO(sl("S", hp)[:, 64 * (c + 1):64 * (c + 2)], bank(f"S{c}", hp)[:, 0:64],
                                sl("N", hp)[:, 64 * c:64 * c + 64], ALU.add))
                for hp in g:
                    mm_done("Y", hp)
                    evd(nc.vector.tensor_copy(sl("Y", hp)[:], bank("Y", hp)[:]))
                for hp in g:
                    mm_done("mean", hp)
                    evd(STT(sl("d", hp)[:], bank("mean", hp)[:], -1.0 / 64, sl("Y", hp)[:], ALU.mult, ALU.add))
                for hp in g:
                    act("grs", hp)
                    evd(TTO(sl("d", hp)[:], sl("d", hp)[:], sl("rs", hp)[:], ALU.mult))
                for hp in g:
                    own_ev("var", hp)
                    go(TS(sl("d", hp)[:], sl("d", hp)[:], V("lnx_w", hp), V("lnx_b", hp), ALU.mult, ALU.add))
                for hp in g:
                    own("yb", hp)
                    go(TTO(sl("d", hp)[:], sl("d", hp)[:], bon[hp % 2][:], ALU.add))
                for hp in g:
                    mm_done("gate", hp)
                    own("yc", hp)
                    evd(TTO(rkv(0, hp), bank("gate", hp)[:], sl("d", hp)[:], ALU.mult))

        def gla_pe(pe, mm, wait, chunk, blocks, block_tm):
            chunk(N_GLR, 0, g_hi, g_lo_, first=32, cols=GLR, inc=2)
            blocks(N_GQK, 1, g_hi, g_lo_)
            wait("acc_evac", acc_before(N_GQK))
            wait("ld_gk", 16)
            wait("norm_ln", 6)
            for c in range(4):
                mm(X[c][:], w_gk2[:, c * P:c * P + P], glr[:], start=True, stop=True).then_inc(S["g_gk"], 1)
            blocks(N_GQK + 1, 3, g_hi, g_lo_)
            for b in range(4):
                block_tm(N_GV + b, g_hi, g_lo_, TT, 2)
            blocks(N_GG, 4, g_hi, g_lo_)
            wait("acc_evac", acc_before(N_GOUT))
            wait("g_sc", 4 * 6)
            wait("g_zero", 2)
            for cp in range(4):
                if cp:
                    wait("g_at", cp)
                tok = slice(cp * P, cp * P + P)
                for hd in range(4):
                    last = mm(X[0][:, hd * P:hd * P + P], gb[:, hd, tok], gq[:, hd, tok], start=True, stop=True)
                last.then_inc(S["g_kt"], 1)
                if cp:
                    wait("g_rl", cp)
                for hd in range(4):
                    last = nc.tensor.transpose(X[1][:, hd * P:hd * P + P], gk[:, hd, tok], C("ident"))
                last.then_inc(S["g_kt"], 1)
                if cp >= 2:
                    wait("g_oev", 4 * (cp - 1))
                wait("g_at", cp + 1)
                wait("g_ktev", cp + 1)
                ob = [M[2 * (cp % 2)], M[2 * (cp % 2) + 1]]
                for hd in range(4):
                    for vc in range(2):
                        a_ = (2 * (hd % 2) + vc) * P
                        mm(ob[hd // 2][:, a_:a_ + P], gv[:, cp, hd * 256 + vc * P:hd * 256 + vc * P + P], gat[cp % 2][:, hd, :],
                           start=hd % 2 == 0 and vc == 0, stop=False, skip_group_check=True)
                for c2 in range(2):
                    c = 2 * cp + c2
                    if c:
                        wait("g_s", c)
                        for hd in range(4):
                            for vc in range(2):
                                a_ = (2 * (hd % 2) + vc) * P + 64 * c2
                                last = mm(ob[hd // 2][:, a_:a_ + 64], gs[c % 2][:, hd, vc * P:vc * P + P],
                                          gq[:, hd, 64 * c:64 * c + 64], start=False, stop=c2 == 1, skip_group_check=True)
                    if c2:
                        last.then_inc(S["g_o"], 1)
                    if c < 7:
                        r = slice(64 * c2, 64 * c2 + 64)
                        for hd in range(4):
                            last = mm(X[2 + hd // 2][:, (hd % 2) * 256:(hd % 2) * 256 + 256], gkt[r, hd, :],
                                      gv[r, cp, hd * 256:hd * 256 + 256], start=True, stop=True)
                        last.then_inc(S["g_n"], 1)
                wait("g_sq", 2 * (cp + 1))
                for hd in range(4):
                    for vc in range(2):
                        a_ = (2 * (hd % 2) + vc) * P
                        last = mm(X[1][:, hd * P:hd * P + P], C("ones"), nt[hd // 2][:, a_:a_ + P], start=vc == 0, stop=vc == 1)
                last.then_inc(S["g_ss"], 1)
            wait("g_lo", 8)
            blocks(N_GOUT, 4, g_hi, g_lo_)

        def cs(c):
            return gs[c // 2][:].rearrange("p a n -> p (a n)")[:, (c % 2) * T:(c % 2) * T + T]

        def gla_act(act, hi):
            hi(N_GQK)
            hi(N_GQK + 1)
            for c in range(4):
                act.wait_ge(S["g_gk"], c + 1)
                nc.scalar.activation(cs(c), X[c][:], ACT.Abs, bias=V("a_b_gk_2", c)).then_inc(S["g_ab"], 1)
            for c in range(4):
                act.wait_ge(S["g_ab"], c + 1)
                nc.scalar.activation(cs(c), cs(c), ACT.Exp, scale=-1.0).then_inc(S["g_ab"], 1)
            for c in range(4):
                act.wait_ge(S["g_ab"], 4 + c + 1)
                nc.scalar.activation(cs(c), cs(c), ACT.Ln, bias=C("one")).then_inc(S["g_ln"], 1)
            hi(N_GQK + 2)
            hi(N_GQK + 3)
            hi(N_GV)
            for c in range(4):
                act.wait_ge(S["g_cs"], c + 1)
                if c:
                    act.wait_ge(S["g_sc"], 6 * c)
                nc.scalar.activation(nt[0][:], cs(c), ACT.Exp, scale=1 / 16).then_inc(S["g_act"], 1)
                nc.scalar.activation(gb[:, c, :], cs(c), ACT.Exp, scale=-1 / 16).then_inc(S["g_act"], 1)
                nc.scalar.activation(g_el[:, 8 * c:8 * c + 8], cs(c).rearrange("p (c t) -> p c t", t=64)[:, :, 63],
                                     ACT.Exp, scale=1 / 16).then_inc(S["g_act"], 1)
                act.wait_ge(S["g_dve"], c + 1)
                nc.scalar.activation(nt[1][:], nt[2][:], ACT.Exp, scale=1 / 16).then_inc(S["g_act"], 1)
            for b in range(4):
                hi(N_GV + b + 1)
            for b in range(4):
                hi(N_GG + b + 1)
                for c in range(2):
                    k = 2 * b + c
                    act.wait_ge(S["acc_done"], 2 * (N_GG + b) + c + 1)
                    if k >= 2:
                        act.wait_ge(S["acc_evac"], acc_before(N_GG) + k - 1)
                    nc.scalar.activation(nt[c][:], M[(acc_before(N_GG) + k) % 4][:], ACT.Sigmoid).then_inc(S["g_act"], 1)
            nc.scalar.preload_act_table_set("natural_log_exp_and_others")
            for cp in range(4):
                act.wait_ge(S["g_kt"], 2 * cp + 2)
                nc.scalar.activation(gkt[:].rearrange("p a n -> p (a n)"), X[1][:], ACT.Copy).then_inc(S["g_ktev"], 1)
                act.wait_ge(S["g_o"], cp + 1)
                if cp:
                    act.wait_ge(S["g_ss"], cp)
                else:
                    act.wait_ge(S["acc_evac"], acc_before(N_GOUT))
                for i in range(2):
                    nc.scalar.activation(nt[i][:], M[2 * (cp % 2) + i][:], ACT.Square).then_inc(S["g_sq"], 1)
                act.wait_ge(S["g_ss"], cp + 1)
                if cp:
                    act.wait_ge(S["g_oev"], 4 * cp)
                nc.scalar.activation(rstd[:], X[1][:], ACT.Ln, scale=1.0 / 256, bias=C("eps6")).then_inc(S["g_rl"], 1)
                act.wait_ge(S["g_rl"], cp + 1)
                nc.scalar.activation(rstd[:], rstd[:], ACT.Exp, scale=-0.5).then_inc(S["g_rstd"], 1)
                for i in range(2):
                    act.wait_ge(S["g_oev"], 4 * cp + 3 + i)
                    tok = slice(cp * P, cp * P + P)
                    nc.scalar.activation(g_hi[:, 4 * i:4 * i + 4, tok], gg[:, 4 * i:4 * i + 4, tok], ACT.Copy).then_inc(S["g_hi"], 1)

        def gla_dve(dve, lo, evac_copy, resid):
            TTO, TS, STT = nc.vector.tensor_tensor, nc.vector.tensor_scalar, nc.vector.scalar_tensor_tensor
            for i in range(2):
                nc.vector.memset(gat[i][:], 0.0).then_inc(S["g_zero"], 1)
            lo(N_GQK)
            dve.wait_ge(S["acc_done"], 2 * N_GLR + 2)
            nc.vector.tensor_copy(glr[:], M[acc_before(N_GLR) % 4][0:GLR, :]).then_inc(S["acc_evac"], 2)

            def qk(b):
                lo(N_GQK + b + 1)
                for c in range(2):
                    j = 2 * b + c
                    evac_copy(N_GQK + b, c, (gq if j < 4 else gk)[:, j % 4, :])

            qk(0)
            for c in range(4):
                dve.wait_ge(S["g_ab"], c + 1)
                TS(gb[:, c, :], X[c][:], V("a_b_gk_2", c), 0.0, ALU.add, ALU.min).then_inc(S["g_o1"], 1)
            for c in range(4):
                dve.wait_ge(S["g_ln"], c + 1)
                dve.wait_ge(S["g_o1"], c + 1)
                TTO(gb[:, c, :], gb[:, c, :], cs(c), ALU.subtract).then_inc(S["g_o1"], 1)
            for c in range(4):
                dve.wait_ge(S["g_o1"], 4 + c + 1)
                nc.vector.tensor_tensor_scan(cs(c), seg, gb[:, c, :], 0.0, ALU.mult, ALU.add).then_inc(S["g_cs"], 1)
            qk(1)
            qk(2)
            qk(3)
            for c in range(4):
                dve.wait_ge(S["g_cs"], c + 1)
                c8 = cs(c).rearrange("p (c t) -> p c t", t=64)
                TTO(nt[2][:].rearrange("p (c t) -> p c t", t=64), c8[:, :, 63:64].to_broadcast([P, 8, 64]), c8,
                    ALU.subtract).then_inc(S["g_dve"], 1)
                dve.wait_ge(S["g_act"], 4 * c + 4)
                STT(gq[:, c, :], gq[:, c, :], float(P) ** -0.5, nt[0][:], ALU.mult, ALU.mult).then_inc(S["g_sc"], 2)
                TTO(gb[:, c, :], gk[:, c, :], gb[:, c, :], ALU.mult).then_inc(S["g_sc"], 2)
                TTO(gk[:, c, :], gk[:, c, :], nt[1][:], ALU.mult).then_inc(S["g_sc"], 2)
            for b in range(4):
                lo(N_GV + b + 1)
                for i in range(2):
                    evac_copy(N_GV + b, i, gv[:, 2 * i:2 * i + 2, b * BW:b * BW + BW], two=True)
            for b in range(4):
                lo(N_GG + b + 1)
                for c in range(2):
                    k = 2 * b + c
                    dve.wait_ge(S["g_act"], 16 + k + 1)
                    STT(gg[:, k, :], M[(acc_before(N_GG) + k) % 4][:], V("a_onorm_2", c), nt[c][:], ALU.mult,
                        ALU.mult).then_inc(S["acc_evac"], 1)
            for cp in range(4):
                dve.wait_ge(S["g_kt"], 2 * cp + 1)
                nc.vector.copy_predicated(gat[cp % 2][:], C("gla").bitcast(i32).unsqueeze(1).to_broadcast([P, 4, P]),
                                          X[0][:].rearrange("p (h n) -> p h n", h=4)).then_inc(S["g_at"], 1)
                for c2 in range(2):
                    c = 2 * cp + c2
                    if c < 7:
                        dve.wait_ge(S["g_n"], c + 1)
                        if c:
                            dve.wait_ge(S["g_s"], c)
                        for hd in range(4):
                            n_ = X[2 + hd // 2][:, (hd % 2) * 256:(hd % 2) * 256 + 256]
                            if c == 0:
                                last = nc.vector.tensor_copy(gs[1][:, hd, :], n_)
                            else:
                                last = STT(gs[(c + 1) % 2][:, hd, :], gs[c % 2][:, hd, :],
                                           g_el[:, 8 * hd + c:8 * hd + c + 1], n_, ALU.mult, ALU.add)
                        last.then_inc(S["g_s"], 1)
                tok = slice(cp * P, cp * P + P)
                dve.wait_ge(S["g_o"], cp + 1)
                for i in range(2):
                    dve.wait_ge(S["g_sq"], 2 * cp + i + 1)
                    g_ = gg[:, 4 * i:4 * i + 4, tok]
                    TTO(g_, M[2 * (cp % 2) + i][:].rearrange("p (c n) -> p c n", c=4), g_, ALU.mult).then_inc(S["g_oev"], 1)
                dve.wait_ge(S["g_rstd"], cp + 1)
                for i in range(2):
                    dve.wait_ge(S["g_oev"], 4 * cp + 1 + i)
                    g_ = gg[:, 4 * i:4 * i + 4, tok].rearrange("p (h v) n -> p h v n", h=2)
                    r_ = rstd[:, 2 * i * P:(2 * i + 2) * P].rearrange("p (h n) -> p h n", h=2).unsqueeze(2).to_broadcast([P, 2, 2, P])
                    TTO(g_, g_, r_, ALU.mult).then_inc(S["g_oev"], 1)
                for i in range(2):
                    dve.wait_ge(S["g_hi"], 2 * cp + i + 1)
                    TTO(g_lo_[:, 4 * i:4 * i + 4, tok], gg[:, 4 * i:4 * i + 4, tok],
                        g_hi[:, 4 * i:4 * i + 4, tok].bitcast(f32), ALU.subtract).then_inc(S["g_lo"], 1)
            resid(N_GOUT)

        @block.sync
        def _(sp):
            def load(n, src, cols=BW, r=0):
                if n >= 4:
                    sp.wait_ge(S["w_lo_ready"], n - 3 + r)
                sp.dma_start(raw[:, n % 4, :, 0:cols], src).then_inc(w_arrived[n % 4], 16)

            def load_plain(first):
                _, count, w, col = next(x for x in plain if x[0] == first)
                cols = GLR if first == N_GLR else BW
                for j in range(count):
                    load(first + j, w[:, :, col + BW * j:col + BW * j + cols], cols)

            def load_mlp(n):
                up, down = mlps[n]
                with sp.Fori(0, 2) as half:
                    with sp.Fori(0, 2) as j:
                        for b in range(4):
                            load(n + b, up[:, :, ds(half * 2048 + j * 1024 + b * BW, BW)], r=half * 16 + j * 4)
                    with sp.Fori(0, 2) as q:
                        for b in range(4):
                            kg, cg = b // 2, b % 2
                            load(n + 8 + b, down[:, ds(half * 16 + kg * 8, 8), ds(q * 512 + cg * BW, BW)],
                                 r=half * 16 + q * 4)

            sp.dma_start(cst[:], A["consts"]).then_inc(S["ld_const"], 16)
            sp.dma_start(xt[:], A["x"][0].rearrange("(t p) n -> p t n", p=P)).then_inc(S["ld_x"], 16)
            for n in (N_DQ, N_DK, N_DV, N_RW):
                load_plain(n)
            for n in (N_WOUT, N_MK, N_MV, N_MQ, N_MO):
                load_plain(n)
            load_mlp(N_MLP1)
            for n in (N_GLR, N_GQK, N_GV, N_GG, N_GOUT):
                load_plain(n)
            load_mlp(N_MLP2)
            for n in (N_KV, N_WQ, N_SOUT):
                load_plain(n)
            load_mlp(N_MLP3)
            load(LAST, w_in[:, :, 0:BW])
            for t in range(TT):
                sp.wait_ge(S["fin_ev"], 2 * (t + 1))
                sp.dma_start(out[0].rearrange("(t p) n -> p t n", p=P)[:, t, :], ytm_view(t)).then_inc(S["st_out"], 16)
            sp.wait_ge(S["st_out"], 16 * TT)

        @block.gpsimd
        def _(pool):
            nvec = 0
            for name, rows in VECS:
                flat = A[name] if len(A[name].shape) == 1 else A[name].rearrange(
                    "a b -> (a b)" if len(A[name].shape) == 2 else "a b c -> (a b c)")
                src = flat.rearrange("(r n) -> r n", n=P)
                first = VEC_ROW[name]
                cut = min(max(P - first, 0), rows)
                if cut:
                    pool.dma_start(vrow[first:first + cut, 0, :], src[0:cut]).then_inc(S["ld_vec"], 16)
                    nvec += 1
                if cut < rows:
                    pool.dma_start(vrow[first + cut - P:first + rows - P, 1, :], src[cut:rows]).then_inc(S["ld_vec"], 16)
                    nvec += 1
            assert nvec == NVEC
            for i, name in enumerate(("lam_q1", "lam_q2")):
                pool.dma_start(lamv[i:i + 1, 0, :], A[name]).then_inc(S["ld_small"], 16)
            for i, name in enumerate(("lam_k1", "lam_k2")):
                pool.dma_start(lamv[i:i + 1, 1, :], A[name]).then_inc(S["ld_small"], 16)
            pool.dma_start(sinkb, A["b_sinks_2"].broadcast_to([P, 16])).then_inc(S["ld_small"], 16)
            pool.dma_start(lora[0:64, :], A["w_decay_up"][0]).then_inc(S["ld_lora"], 16)
            pool.dma_start(lora[64:128, :], A["a_up"][0]).then_inc(S["ld_lora"], 16)
            pool.dma_start(g_up[:], A["g_up"][0]).then_inc(S["ld_lora"], 16)
            pool.wait_ge(S["rw_ev"], len(RW_SEQ))
            pool.dma_start(mrow[:], A["mem"][0].rearrange("(t p) n -> p t n", p=P)).then_inc(S["ld_mem"], 16)
            pool.wait_ge(S["acc_evac"], acc_before(N_MQ))
            pool.dma_start(onehot[:], A["onehot"]).then_inc(S["ld_rel"], 16)
            pool.dma_start(relx[0:32, :], A["rel_table_2"]).then_inc(S["ld_rel"], 16)
            pool.dma_start(relx[32:33, :], A["consts"][0:1, CONST["ones"][0]:CONST["ones"][0] + 16]).then_inc(S["ld_rel"], 16)
            for hd in range(16):
                pool.wait_ge(S["bias_ev"], hd + 1)
                pool.dma_start(bias_rows[hd], biasrow[hd % 2][:]).then_inc(S["st_bias"], 16)
                pool.wait_ge(S["st_bias"], 16 * (hd + 1))
            pool.wait_ge(S["acc_evac"], acc_before(N_GLR))
            pool.dma_start(w_gk2[:], A["a_w_gk2_2"][0]).then_inc(S["ld_gk"], 16)
            pool.wait_ge(S["acc_evac"], acc_before(N_KV))
            pool.dma_start(bias[:], bias_skewed()).then_inc(S["ld_bias"], 16)

        @block.tensor
        def _(pe):
            mm = nc.tensor.matmul

            def wait(name, v):
                pe.wait_ge(S[name], v)

            def bank_free(k, r=None):
                if k >= 4:
                    pe.wait_ge(S["acc_evac"], k - 3 if r is None else k - 3 + r)
                return M[k % 4]

            def block_ready(n, r=None):
                pe.wait_ge(S["w_lo_ready"], n + 1 if r is None else n + 1 + r)

            def exact3(dst, wh, wl, xh, xl, start, stop):
                mm(dst, wh, xh, start=start, stop=False)
                mm(dst, wl, xh, start=False, stop=False)
                return mm(dst, wh, xl, start=False, stop=stop)

            def chunk(n, c, hi, lo, first=None, cols=P, tok=T, inc=1):
                if c == 0:
                    block_ready(n)
                k = acc_before(n) + c
                dst = bank_free(k)
                for kt in range(KT):
                    if first is not None:
                        wait("x_lo", first + kt + 1)
                    ws = slice(c * P, c * P + cols)
                    last = exact3(dst[0:cols, 0:tok], w_hi[:, n % 2, kt, ws], w_lo[:, n % 2, kt, ws],
                                  hi[:, kt, 0:tok], lo[:, kt, 0:tok], kt == 0, kt == KT - 1)
                last.then_inc(S["acc_done"], inc)

            def blocks(n, count, hi, lo, first=None, tok=T):
                for b in range(count):
                    for c in range(2):
                        chunk(n + b, c, hi, lo, first if b == 0 and c == 0 else None, tok=tok)

            def block_tm(n, hi, lo, tiles, per, width=BW, at=0, base=None):
                block_ready(n)
                k = acc_before(n) if base is None else base
                for t in range(tiles):
                    if t % per == 0:
                        dst = bank_free(k + t // per)
                    for kt in range(KT):
                        ts_, cs = slice(t * P, t * P + P), slice(at, at + width)
                        o_ = dst[:, (t % per) * width:(t % per + 1) * width]
                        mm(o_, hi[:, kt, ts_], w_hi[:, n % 2, kt, cs], start=kt == 0, stop=False)
                        mm(o_, hi[:, kt, ts_], w_lo[:, n % 2, kt, cs], start=False, stop=False)
                        last = mm(o_, lo[:, kt, ts_], w_hi[:, n % 2, kt, cs], start=False, stop=kt == KT - 1)
                    if t % per == per - 1:
                        last.then_inc(S["acc_done"], 2 // (tiles // per) if base is None else 1)

            def norm_stat(i, tok=T):
                wait("norm_add", 7 * (i + 1))
                mm(X[0][:, 0:tok], C("ones"), nt[2][:, 0:tok], start=True, stop=True).then_inc(S["norm_ss"], 1)

            def mlp(n, first, nth):
                k = acc_before(n)
                with pe.Fori(0, 2) as half:
                    with pe.Fori(0, 2) as j:
                        for b in range(4):
                            block_ready(n + b, half * 16 + j * 4)
                            for c in range(2):
                                dst = bank_free(k + 2 * b + c, half * 24 + j * 8)
                                for kt in range(KT):
                                    if b == 0 and c == 0:
                                        wait("x_lo", first + kt + 1)
                                    ws = slice(c * P, c * P + P)
                                    last = exact3(dst[:], w_hi[:, (n + b) % 2, kt, ws], w_lo[:, (n + b) % 2, kt, ws],
                                                  f_hi[:, kt, :], f_lo[:, kt, :], kt == 0, kt == KT - 1)
                                last.then_inc(S["acc_done"], 1)
                    with pe.Fori(0, 2) as q:
                        for b in range(4):
                            kg = b // 2
                            m = n + 8 + b
                            block_ready(m, half * 16 + q * 4)
                            pe.wait_ge(S["up_lo"], 32 * nth + 8 * kg + 8 + half * 16)
                            for c in range(2):
                                kk = k + 16 + 2 * (b % 2) + c
                                dst = M[kk % 4] if kg else bank_free(kk, half * 24 + q * 4)
                                for kt in range(KT):
                                    ws = slice(c * P, c * P + P)
                                    last = exact3(dst[:], w_hi[:, m % 2, kt, ws], w_lo[:, m % 2, kt, ws],
                                                  u_hi[:, kg * 8 + kt, :], u_lo[:, kg * 8 + kt, :],
                                                  kg == 0 and kt == 0, kg == 1 and kt == KT - 1)
                                last.then_inc(S["acc_done"], 1)

            wait("ld_const", 16)
            wait("ld_vec", 16 * NVEC)
            nc.tensor.transpose(M[0][:, 0:P], vrow[:, 0, :], C("ident"))
            nc.tensor.transpose(M[0][:, P:VEC_ROWS], vrow[0:VEC_ROWS - P, 1, :],
                                C("ident", slice(0, VEC_ROWS - P))[:, 0:VEC_ROWS - P]).then_inc(S["vec_tr"], 1)
            wait("ld_x", 16)
            for c in range(KT):
                if c >= 4:
                    wait("xt_ev", c - 3)
                for t in range(TT):
                    last = nc.tensor.transpose(X[c % 4][:, t * P:t * P + P], xt[:, t, c * P:c * P + P], C("ident"))
                last.then_inc(S["xt_tr"], 1)
            wait("xt_ev", KT)
            norm_stat(0)
            wait("lam_e", 1)
            mm(X[3][:, 0:1], C("plusminus", slice(0, 2)), lame, start=True, stop=True).then_inc(S["lam_mm"], 1)

            blocks(N_DQ, 2, xm_hi, xm_lo, first=0)
            blocks(N_DK, 2, xm_hi, xm_lo)
            for b in range(2):
                block_tm(N_DV + b, xm_hi, xm_lo, TT, 2)
            wait("acc_evac", acc_before(N_RW))
            wait("lam_ready", 1)

            def diff_norm(hd):
                wait("da_sq", hd + 1)
                mm(X[2][:], C("ones"), de_sq[:], start=True, stop=True).then_inc(S["da_ss"], 1)

            for u in range(16):
                hd, qb = u // 4, u % 4
                nk = (qb + 1) * P
                if u:
                    wait("da_exp", 2 * u)
                for m in range(2):
                    r = slice(64 * m, 64 * m + 64)
                    last = mm(X[m][:, 0:nk], dq[r, hd, qb * P:qb * P + P], dk[r, hd, 0:nk], start=True, stop=True)
                last.then_inc(S["da_score"], 1)
                if u < 14:
                    chunk(N_RW + u // 2, u % 2, xm_hi, xm_lo)
                if qb == 0 and hd:
                    wait("da_at", u)
                    diff_norm(hd - 1)
                wait("da_attn", u + 1)
                if u:
                    wait("da_at", u)
                if qb == 0 and hd:
                    wait("da_ln", hd)
                for kb in range(qb + 1):
                    last = nc.tensor.transpose(X[2][:, kb * P:kb * P + P], de[1][:, kb * P:kb * P + P], C("ident"))
                last.then_inc(S["da_tr"], 1)
                wait("da_at", u + 1)
                if qb == 0 and hd:
                    wait("da_o", hd)
                for kb in range(qb + 1):
                    last = mm(X[3][:, qb * P:qb * P + P], dv[:, kb, hd * P:hd * P + P], da_t[:, kb, :],
                              start=kb == 0, stop=kb == qb)
                last.then_inc(S["da_pv"], 1)
            diff_norm(3)
            wait("da_y", 4)

            wait("rw_act", 2)
            rwkv_pe(pe, mm, wait)

            wait("y_lo", KT)
            blocks(N_WOUT, 1, y_hi, y_lo)
            wait("ld_mem", 16)
            for g in range(4):
                for i in range(2):
                    for t in range(2):
                        c = 2 * g + i
                        last = nc.tensor.transpose(X[g][:, i * MEM + t * P:i * MEM + t * P + P],
                                                   mrow[:, t, c * P:c * P + P], C("ident"))
                last.then_inc(S["mt_tr"], 1)
            blocks(N_WOUT + 1, 1, y_hi, y_lo)
            wait("mt_ev", 4)
            norm_stat(1, MEM)
            blocks(N_WOUT + 2, 2, y_hi, y_lo)
            blocks(N_MK, 4, m_hi, m_lo, first=8, tok=MEM)
            block_tm(N_MV, m_hi, m_lo, 2, 1)
            norm_stat(2)
            for b in range(1, 4):
                block_tm(N_MV + b, m_hi, m_lo, 2, 1)
            blocks(N_MQ, 4, y_hi, y_lo, first=16)
            wait("acc_evac", acc_before(N_MO))

            def mem_score(u):
                hd, qb = u // 4, u % 4
                if u >= 2:
                    wait("ma_exp", u - 1)
                for i in range(2):
                    last = mm(X[u % 2][:, 0:MEM], mq[:, 2 * hd + i, qb * P:qb * P + P], mk[:, 2 * hd + i, :],
                              start=i == 0, stop=i == 1)
                last.then_inc(S["ma_score"], 1)

            mem_score(0)
            for u in range(16):
                hd, qb = u // 4, u % 4
                if u < 15:
                    mem_score(u + 1)
                wait("ma_p", u + 1)
                if u:
                    wait("ma_pt", u)
                for t in range(2):
                    last = nc.tensor.transpose(X[2][:, t * P:t * P + P], me[u % 2][:, t * P:t * P + P], C("ident"))
                last.then_inc(S["ma_tr"], 1)
                if u:
                    wait("bias_ev", u)
                else:
                    wait("ld_rel", 48)
                mm(X[3][:, 0:384], relx[:, u:u + 1].to_broadcast([33, P]), onehot[:], start=True,
                   stop=True).then_inc(S["bias_mm"], 1)
                wait("ma_pt", u + 1)
                if qb == 0 and hd >= 2:
                    wait("ma_lo", 2 * (hd - 1))
                for i in range(2):
                    for t in range(2):
                        f = (2 * hd + i) * P
                        last = mm(M[2 * (hd % 2) + i][:, qb * P:qb * P + P], mv[:, t, f:f + P],
                                  mpt[u % 2][:, t, :], start=t == 0, stop=t == 1)
                last.then_inc(S["ma_pv"], 1)
            wait("ma_lo", KT)
            blocks(N_MO, 4, y_hi, y_lo)

            norm_stat(3)
            mlp(N_MLP1, 24, 0)
            norm_stat(4)

            norm_stat(5)
            gla_pe(pe, mm, wait, chunk, blocks, block_tm)
            norm_stat(6)
            mlp(N_MLP2, 40, 1)

            norm_stat(7)
            chunk(N_KV, 0, s_hi, s_lo, first=48)
            block_tm(N_KV, s_hi, s_lo, TT, TT, width=P, at=P, base=acc_before(N_KV) + 1)
            wait("acc_evac", acc_before(N_KV) + 1)
            for i in range(2):
                mm(X[1 + i][:], C(f"sel{i}"), kf[:], start=True, stop=True).then_inc(S["sw_dup"], 1)
            blocks(N_WQ, 4, s_hi, s_lo, first=56)
            wait("acc_evac", acc_before(N_SOUT))
            wait("sw_dupev", 2)

            def sw_score(u):
                c, qb = u // 4, u % 4
                if u >= 2:
                    wait("sw_s", u - 1)
                lo_ = max(qb - 1, 0) * P
                n = (qb + 1) * P - lo_
                for i in range(2):
                    r = slice(64 * i, 64 * i + 64)
                    last = mm(sw_banks(u)[:, i, 256 - n:256], sq[r, c, qb * P:qb * P + P],
                              kd[c // 4][r, lo_:lo_ + n], start=True, stop=True)
                last.then_inc(S["sw_score"], 1)

            sw_score(0)
            for u in range(32):
                c, qb = u // 4, u % 4
                if u < 31:
                    sw_score(u + 1)
                wait("sw_p", u + 1)
                if u:
                    wait("sw_pt", u)
                kbs = (0, 1) if qb else (1,)
                for i in range(2):
                    for kb in kbs:
                        last = nc.tensor.transpose(X[2][:, (2 * i + kb) * P:(2 * i + kb + 1) * P],
                                                   sc[u % 2][:, i, kb * P:kb * P + P], C("ident"))
                last.then_inc(S["sw_tr"], 1)
                wait("sw_pt", u + 1)
                if qb == 0 and c >= 2:
                    wait("sw_lo", c - 1)
                for i in range(2):
                    for kb in kbs:
                        last = mm(M[c % 2][64 * i:64 * i + 64, qb * P:qb * P + P],
                                  sv[:, qb - 1 + kb, (c // 4) * 64:(c // 4) * 64 + 64],
                                  spt[u % 2][:, 2 * i + kb, :], start=kb == kbs[0], stop=kb == 1)
                last.then_inc(S["sw_pv"], 1)
            wait("sw_lo", KT)
            blocks(N_SOUT, 4, s_hi, s_lo)
            norm_stat(8)
            mlp(N_MLP3, 64, 2)
            norm_stat(9)

            wait("acc_evac", acc_before(LAST))
            wait("h_final", HF)
            for t in range(TT):
                for half in range(2):
                    i = 2 * t + half
                    if i >= 2:
                        wait("fin_ev", i - 1)
                    for c in range(4):
                        last = nc.tensor.transpose(X[2 + i % 2][:, c * P:c * P + P], h[:, 4 * half + c, t * P:t * P + P],
                                                   C("ident"))
                    last.then_inc(S["fin_tr"], 1)

        @block.scalar
        def _(act):
            def hi(n, r=None):
                if n >= 2:
                    act.wait_ge(S["acc_done"], 2 * (n - 1) if r is None else 2 * (n - 1) + 2 * r)
                act.wait_ge(w_arrived[n % 4], 16 * (n // 4 + 1) if r is None else 16 * (n // 4 + 1) + 4 * r)
                cols = GLR if n == N_GLR else BW
                nc.scalar.activation(w_hi[:, n % 2, :, 0:cols], raw[:, n % 4, :, 0:cols], ACT.Copy).then_inc(S["w_hi_ready"], 1)

            def norm_square(i, src, tok=T):
                for c in range(KT):
                    if c >= 2:
                        act.wait_ge(S["norm_add"], 7 * i + max(1, c - 2))
                    nc.scalar.activation(nt[c % 2][:, 0:tok], src[:, c, :], ACT.Square).then_inc(S["norm_sq"], 1)

            def norm_rsqrt(i, eps, tok=T):
                act.wait_ge(S["norm_ss"], i + 1)
                nc.scalar.activation(rstd[:, 0:tok], X[0][:, 0:tok], ACT.Ln, scale=1.0 / D, bias=C(eps)).then_inc(S["norm_ln"], 1)
                act.wait_ge(S["norm_ln"], i + 1)
                nc.scalar.activation(rstd[:, 0:tok], rstd[:, 0:tok], ACT.Exp, scale=-0.5).then_inc(S["norm_rstd"], 1)

            def norm_hi(j, dst, tok=T):
                for c in range(KT):
                    act.wait_ge(S["norm_x"], 8 * j + c + 1)
                    nc.scalar.activation(dst[:, c, :], nt[c % 2][:, 0:tok], ACT.Copy).then_inc(S["x_hi"], 1)

            def mlp(n, nth):
                k = acc_before(n)
                with act.Fori(0, 2) as half:
                    with act.Fori(0, 2) as j:
                        for b in range(4):
                            hi(n + b + 1, half * 16 + j * 4)
                            for c in range(2):
                                i = 2 * b + c
                                act.wait_ge(S["acc_evac"], k + i + 1 + half * 24 + j * 8)
                                nc.scalar.activation(us[c][:], ut[c][:], ACT.Square).then_inc(S["up_sq"], 1)
                                act.wait_ge(S["up_sq"], 32 * nth + i + 1 + half * 16 + j * 8)
                                nc.scalar.activation(u_hi[:, ds(j * 8 + i, 1), :], us[c][:].unsqueeze(1), ACT.Copy).then_inc(S["up_hi"], 1)
                    with act.Fori(0, 2) as q:
                        for b in range(4):
                            hi(n + 9 + b, half * 16 + q * 4)

            nc.scalar.preload_act_table_set("natural_log_exp_and_others")
            act.wait_ge(S["lam_mul"], 3)
            nc.scalar.activation(lame, lamd, ACT.Exp).then_inc(S["lam_e"], 1)
            act.wait_ge(S["xt_ev"], KT)
            norm_square(0, h)
            hi(0)
            norm_rsqrt(0, "eps5")
            norm_hi(0, xm_hi)
            for n in range(N_RW):
                hi(n + 1)
            for u in range(16):
                hd, qb = u // 4, u % 4
                nk = (qb + 1) * P
                act.wait_ge(S["da_neg"], u + 1)
                for m in range(2):
                    nc.scalar.activation(de[m][:, 0:nk], X[m][:, 0:nk], ACT.Exp, bias=da_ng[:, m:m + 1], scale=0.125,
                                         accum_out=da_z[:, m:m + 1]).then_inc(S["da_exp"], 1)
                if u % 2 == 0 and u < 14:
                    hi(N_RW + u // 2 + 1)
                if qb == 0 and hd:
                    act.wait_ge(S["da_ss"], hd)
                    nc.scalar.activation(rstd[:], X[2][:], ACT.Ln, scale=1.0 / P, bias=C("eps5")).then_inc(S["da_ln"], 1)
                    act.wait_ge(S["da_ln"], hd)
                    nc.scalar.activation(rstd[:], rstd[:], ACT.Exp, scale=-0.5).then_inc(S["da_rstd"], 1)
                act.wait_ge(S["da_tr"], u + 1)
                nc.scalar.activation(da_t[:, 0:qb + 1, :], X[2][:, 0:nk].rearrange("p (k n) -> p k n", n=P), ACT.Copy).then_inc(S["da_at"], 1)
                if qb == 3:
                    act.wait_ge(S["da_o"], hd + 1)
                    if hd:
                        act.wait_ge(S["da_ss"], hd)
                    nc.scalar.activation(de_sq[:], da_out[:], ACT.Square).then_inc(S["da_sq"], 1)
            act.wait_ge(S["da_ss"], 4)
            nc.scalar.activation(rstd[:], X[2][:], ACT.Ln, scale=1.0 / P, bias=C("eps5")).then_inc(S["da_ln"], 1)
            act.wait_ge(S["da_ln"], 4)
            nc.scalar.activation(rstd[:], rstd[:], ACT.Exp, scale=-0.5).then_inc(S["da_rstd"], 1)
            act.wait_ge(S["rw_p"], 14)
            nc.scalar.activation(p_rw[0:64, 12, 1:T + 1], p_rw[0:64, 12, 1:T + 1], ACT.Tanh).then_inc(S["rw_act"], 1)
            nc.scalar.activation(p_rw[:, 13, 1:T + 1], p_rw[:, 13, 1:T + 1], ACT.Sigmoid).then_inc(S["rw_act"], 1)
            rwkv_act(act)
            for c in range(KT):
                act.wait_ge(S["rw_ev"], ev("gate", min(c, 3)))
                nc.scalar.activation(y_hi[:, c, :], rkv(0, c) if c < 4 else y_diff[:, c - 4, :], ACT.Copy).then_inc(S["y_hi"], 1)
            hi(N_WOUT + 1)
            act.wait_ge(S["mt_ev"], 4)
            norm_square(1, memT, MEM)
            hi(N_WOUT + 2)
            norm_rsqrt(1, "eps5", MEM)
            hi(N_WOUT + 3)
            norm_hi(1, m_hi, MEM)
            hi(N_MK)
            act.wait_ge(S["acc_evac"], acc_before(N_MK))
            norm_square(2, h)
            for n in range(N_MK, N_MV):
                hi(n + 1)
            hi(N_MV + 1)
            norm_rsqrt(2, "eps5")
            norm_hi(2, y_hi)
            for n in range(N_MV + 1, N_MO):
                hi(n + 1)
            for u in range(16):
                hd, qb = u // 4, u % 4
                act.wait_ge(S["ma_neg"], u + 1)
                if u >= 2:
                    act.wait_ge(S["ma_tr"], u - 1)
                nc.scalar.activation(me[u % 2][:], X[u % 2][:, 0:MEM], ACT.Exp, bias=ma_ng, scale=1.0 / 16,
                                     accum_out=ma_z).then_inc(S["ma_exp"], 1)
                act.wait_ge(S["bias_mm"], u + 1)
                if u >= 2:
                    act.wait_ge(S["st_bias"], 16 * (u - 1))
                nc.scalar.activation(biasrow[u % 2][:], X[3][:, 0:384], ACT.Copy).then_inc(S["bias_ev"], 1)
                act.wait_ge(S["ma_tr"], u + 1)
                nc.scalar.activation(mpt[u % 2][:].rearrange("p a n -> p (a n)"), X[2][:, 0:MEM], ACT.Copy).then_inc(S["ma_pt"], 1)
                if qb == 3:
                    act.wait_ge(S["ma_pv"], u + 1)
                    for i in range(2):
                        nc.scalar.activation(y_hi[:, 2 * hd + i, :], M[2 * (hd % 2) + i][:], ACT.Copy).then_inc(S["ma_hi"], 1)
            for n in range(N_MO, N_MLP1):
                hi(n + 1)
            act.wait_ge(S["acc_evac"], acc_before(N_MLP1))
            norm_square(3, h)
            norm_rsqrt(3, "eps5")
            norm_hi(3, f_hi)
            mlp(N_MLP1, 0)
            act.wait_ge(S["acc_evac"], acc_before(N_GLR))
            norm_square(4, h)
            norm_rsqrt(4, "eps5")
            act.wait_ge(S["h_final"], KT)
            norm_square(5, h)
            norm_rsqrt(5, "eps6")
            norm_hi(4, g_hi)
            gla_act(act, hi)
            for b in range(4):
                hi(N_GOUT + b + 1)
            act.wait_ge(S["acc_evac"], acc_before(N_MLP2))
            norm_square(6, h)
            norm_rsqrt(6, "eps6")
            norm_hi(5, f_hi)
            mlp(N_MLP2, 1)
            act.wait_ge(S["acc_evac"], acc_before(N_KV))
            norm_square(7, h)
            norm_rsqrt(7, "eps6")
            norm_hi(6, s_hi)
            hi(N_WQ)
            norm_hi(7, s_hi)
            for n in range(N_WQ, N_SOUT):
                hi(n + 1)
            for u in range(32):
                c, qb = u // 4, u % 4
                off = 0 if qb else P
                act.wait_ge(S["sw_neg"], u + 1)
                for i in range(2):
                    nc.scalar.activation(sc[u % 2][:, i, off:256], sc[u % 2][:, i, off:256], ACT.Exp, bias=sw_ng_[:, i:i + 1],
                                         accum_out=sw_z_[:, i:i + 1]).then_inc(S["sw_e"], 1)
                act.wait_ge(S["sw_es"], u + 1)
                nc.scalar.activation(sw_es_, sw_es_, ACT.Exp).then_inc(S["sw_e"], 1)
                act.wait_ge(S["sw_tr"], u + 1)
                o4 = slice(0 if qb else 1, 2)
                nc.scalar.activation(spt[u % 2][:].rearrange("p (i k) n -> p i k n", i=2)[:, :, o4, :],
                                     X[2][:].rearrange("p (i k n) -> p i k n", i=2, k=2)[:, :, o4, :], ACT.Copy).then_inc(S["sw_pt"], 1)
                if qb == 3:
                    act.wait_ge(S["sw_pv"], u + 1)
                    nc.scalar.activation(s_hi[:, c, :], M[c % 2][:], ACT.Copy).then_inc(S["sw_hi"], 1)
            for n in range(N_SOUT, N_MLP3):
                hi(n + 1)
            act.wait_ge(S["acc_evac"], acc_before(N_MLP3))
            norm_square(8, h)
            norm_rsqrt(8, "eps6")
            norm_hi(8, f_hi)
            mlp(N_MLP3, 2)
            act.wait_ge(S["acc_evac"], acc_before(N_END))
            norm_square(9, h)
            norm_rsqrt(9, "eps6")

        @block.vector
        def _(dve):
            TTO, TS, STT = nc.vector.tensor_tensor, nc.vector.tensor_scalar, nc.vector.scalar_tensor_tensor

            def lo(n, r=None):
                dve.wait_ge(S["w_hi_ready"], n + 1 if r is None else n + 1 + r)
                cols = GLR if n == N_GLR else BW
                TTO(w_lo[:, n % 2, :, 0:cols], raw[:, n % 4, :, 0:cols], w_hi[:, n % 2, :, 0:cols].bitcast(f32),
                    ALU.subtract).then_inc(S["w_lo_ready"], 1)

            def evac_copy(n, c, dst, two=False):
                dve.wait_ge(S["acc_done"], 2 * n + c + 1)
                src = M[(acc_before(n) + c) % 4][:]
                nc.vector.tensor_copy(dst, src.rearrange("p (t n) -> p t n", t=2) if two else src).then_inc(S["acc_evac"], 1)

            def resid(n):
                dve.wait_ge(S["acc_evac"], acc_before(n))
                for b in range(4):
                    lo(n + b + 1)
                    for c in range(2):
                        resid_chunk(n, b, c)

            def resid_chunk(n, b, c):
                i = 2 * b + c
                dve.wait_ge(S["acc_done"], 2 * n + i + 1)
                TTO(h[:, i, :], h[:, i, :], M[(acc_before(n) + i) % 4][:], ALU.add).then_inc(S["acc_evac"], 1)

            def norm_add(i, tok=T):
                for c in range(1, KT):
                    dve.wait_ge(S["norm_sq"], 8 * i + c + 1)
                    if c > 1:
                        dve.wait_ge(S["norm_add"], 7 * i + c - 1)
                    first = nt[0] if c == 1 else nt[2]
                    TTO(nt[2][:, 0:tok], first[:, 0:tok], nt[c % 2][:, 0:tok], ALU.add).then_inc(S["norm_add"], 1)

            def norm_apply(i, j, src, wname, woff, hi_, lo_, tok=T):
                dve.wait_ge(S["norm_rstd"], i + 1)

                def sub(c):
                    dve.wait_ge(S["x_hi"], 8 * j + c + 1)
                    TTO(lo_[:, c, :], nt[c % 2][:, 0:tok], hi_[:, c, :].bitcast(f32), ALU.subtract).then_inc(S["x_lo"], 1)

                for c in range(KT):
                    if c >= 2:
                        dve.wait_ge(S["x_lo"], 8 * j + c - 1)
                    STT(nt[c % 2][:, 0:tok], src[:, c, :], V(wname, woff + c), rstd[:, 0:tok], ALU.mult,
                        ALU.mult).then_inc(S["norm_x"], 1)
                    if c:
                        sub(c - 1)
                sub(KT - 1)

            def norm_final(i, wname):
                dve.wait_ge(S["norm_rstd"], i + 1)
                for c in range(KT):
                    STT(h[:, c, :], h[:, c, :], V(wname, c), rstd[:], ALU.mult, ALU.mult).then_inc(S["h_final"], 1)

            def mlp(n, nth):
                k = acc_before(n)
                with dve.Fori(0, 2) as half:
                    with dve.Fori(0, 2) as j:
                        for b in range(4):
                            lo(n + b + 1, half * 16 + j * 4)
                            for c in range(2):
                                i = 2 * b + c
                                dve.wait_ge(S["acc_done"], 2 * n + i + 1 + half * 32 + j * 8)
                                nc.vector.tensor_scalar_max(ut[c][:], M[(k + i) % 4][:], 0.0).then_inc(S["acc_evac"], 1)
                                dve.wait_ge(S["up_hi"], 32 * nth + i + 1 + half * 16 + j * 8)
                                u_ = ds(j * 8 + i, 1)
                                TTO(u_lo[:, u_, :], us[c][:].unsqueeze(1), u_hi[:, u_, :].bitcast(f32),
                                    ALU.subtract).then_inc(S["up_lo"], 1)
                    with dve.Fori(0, 2) as q:
                        for b in range(4):
                            lo(n + 9 + b, half * 16 + q * 4)
                            if b >= 2:
                                for c in range(2):
                                    i = 2 * (b % 2) + c
                                    dve.wait_ge(S["acc_done"], 2 * (n + 8 + b) + c + 1 + half * 32 + q * 8)
                                    dve.wait_ge(S["acc_evac"], k + 16 + i + half * 24 + q * 4)
                                    h_ = h[:, ds(q * 4 + i, 1), :]
                                    TTO(h_, h_, M[(k + i) % 4][:].unsqueeze(1), ALU.add).then_inc(S["acc_evac"], 1)

            nc.vector.memset(p_rw[:, :, 0:1], 0.0).then_inc(S["rw_zero"], 1)
            dve.wait_ge(S["vec_tr"], 1)
            nc.vector.tensor_copy(vec[:], M[0][:, 0:VEC_ROWS]).then_inc(S["vec_ready"], 1)
            dve.wait_ge(S["ld_small"], 16 * 5)
            TTO(lamv[:, 0, :], lamv[:, 0, :], lamv[:, 1, :], ALU.mult).then_inc(S["lam_mul"], 1)
            dve.wait_ge(S["lam_mul"], 1)
            nc.vector.reduce_sum(lamd, lamv[:, 0, :], AX.X).then_inc(S["lam_mul"], 2)
            dve.wait_ge(S["vec_ready"], 1)
            nc.vector.tensor_scalar(sub_w, V("subln_w", 0), 1.0 - LAM_INIT, None, ALU.mult).then_inc(S["vec_ready"], 1)
            for c in range(KT):
                dve.wait_ge(S["xt_tr"], c + 1)
                nc.vector.tensor_copy(h[:, c, :], X[c % 4][:]).then_inc(S["xt_ev"], 1)
            norm_add(0)
            lo(0)
            dve.wait_ge(S["lam_mm"], 1)
            TS(lamneg, X[3][:, 0:1], -1.0, -LAM_INIT, ALU.mult, ALU.add).then_inc(S["lam_ready"], 1)
            norm_apply(0, 0, h, "norm_mix_w", 0, xm_hi, xm_lo)
            for b in range(4):
                lo(b + 1)
                for c in range(2):
                    i = 2 * b + c
                    evac_copy(b, c, (dq if i < 4 else dk)[:, i % 4, :])
            for b in range(2):
                lo(N_DV + b + 1)
                for i in range(2):
                    evac_copy(N_DV + b, i, dv[:, 2 * i:2 * i + 2, b * BW:b * BW + BW], two=True)
            def diff_y(hd):
                dve.wait_ge(S["da_rstd"], hd + 1)
                STT(y_diff[:, hd, :], da_out[:], sub_w, rstd[:], ALU.mult, ALU.mult).then_inc(S["da_y"], 1)

            for u in range(16):
                hd, qb = u // 4, u % 4
                nk = (qb + 1) * P
                dve.wait_ge(S["da_score"], u + 1)
                for m in range(2):
                    nc.vector.memset(X[m][0:64, nk - 64:nk], NEG).then_inc(S["da_fill"], 1)
                dve.wait_ge(S["da_fill"], 2 * u + 2)
                for m in range(2):
                    nc.vector.reduce_max(da_mx[:, m:m + 1], X[m][:, 0:nk], AX.X).then_inc(S["da_max"], 1)
                dve.wait_ge(S["da_max"], 2 * u + 2)
                TS(da_ng, da_mx, -0.125, None, ALU.mult).then_inc(S["da_neg"], 1)
                dve.wait_ge(S["da_exp"], 2 * u + 2)
                nc.vector.reciprocal(da_r, da_z).then_inc(S["da_rz"], 1)
                dve.wait_ge(S["da_rz"], u + 1)
                TS(da_c[:, 0:1], da_r[:, 1:2], lamneg, None, ALU.mult).then_inc(S["da_c2"], 1)
                TS(de[0][:, 0:nk], de[0][:, 0:nk], da_r[:, 0:1], None, ALU.mult).then_inc(S["da_c2"], 1)
                dve.wait_ge(S["da_c2"], 2 * u + 2)
                STT(de[1][:, 0:nk], de[1][:, 0:nk], da_c[:, 0:1], de[0][:, 0:nk], ALU.mult, ALU.add).then_inc(S["da_attn"], 1)
                if u < 14:
                    n, c = N_RW + u // 2, u % 2
                    if c == 0:
                        lo(n + 1)
                    evac_copy(n, c, p_rw[:, 2 * (n - N_RW) + c, 1:T + 1])
                if qb == 0 and hd:
                    diff_y(hd - 1)
                if qb == 3:
                    dve.wait_ge(S["da_pv"], u + 1)
                    nc.vector.tensor_copy(da_out[:], X[3][:]).then_inc(S["da_o"], 1)
            diff_y(3)
            for c in range(14):
                if c == 0:
                    dve.wait_ge(S["acc_evac"], acc_before(N_WOUT))
                if c >= 2:
                    dve.wait_ge(S["rw_p"], c - 1)
                TTO(nt[c % 2][:], p_rw[:, c, 0:T], p_rw[:, c, 1:T + 1], ALU.subtract).then_inc(S["rw_shift"], 1)
                dve.wait_ge(S["rw_shift"], c + 1)
                STT(p_rw[:, c, 1:T + 1], nt[c % 2][:], V("mu_shift", c), p_rw[:, c, 1:T + 1], ALU.mult,
                    ALU.add).then_inc(S["rw_p"], 1)
            rwkv_dve(dve)
            for c in range(KT):
                dve.wait_ge(S["y_hi"], c + 1)
                TTO(y_lo[:, c, :], rkv(0, c) if c < 4 else y_diff[:, c - 4, :], y_hi[:, c, :].bitcast(f32),
                    ALU.subtract).then_inc(S["y_lo"], 1)
            lo(N_WOUT + 1)
            for c in range(2):
                resid_chunk(N_WOUT, 0, c)
            for g in range(4):
                dve.wait_ge(S["mt_tr"], g + 1)
                nc.vector.tensor_copy(memT[:, 2 * g:2 * g + 2, :], X[g][:].rearrange("p (a n) -> p a n", a=2)).then_inc(S["mt_ev"], 1)
            norm_add(1, MEM)
            lo(N_WOUT + 2)
            for c in range(2):
                resid_chunk(N_WOUT, 1, c)
            lo(N_WOUT + 3)
            norm_apply(1, 1, memT, "norm_src_w", 0, m_hi, m_lo, MEM)
            for c in range(2):
                resid_chunk(N_WOUT, 2, c)
            lo(N_MK)
            for c in range(2):
                resid_chunk(N_WOUT, 3, c)
            norm_add(2)
            for b in range(4):
                lo(N_MK + b + 1)
                for c in range(2):
                    dve.wait_ge(S["acc_done"], 2 * (N_MK + b) + c + 1)
                    nc.vector.tensor_copy(mk[:, 2 * b + c, :], M[(acc_before(N_MK + b) + c) % 4][:, 0:MEM]).then_inc(S["acc_evac"], 1)
            for b in range(4):
                lo(N_MV + b + 1)
                for t in range(2):
                    dve.wait_ge(S["acc_done"], 2 * (N_MV + b) + t + 1)
                    nc.vector.tensor_copy(mv[:, t, b * BW:b * BW + BW],
                                          M[(acc_before(N_MV + b) + t) % 4][:, 0:BW]).then_inc(S["acc_evac"], 1)
                if b == 0:
                    norm_apply(2, 2, h, "norm_mem_w", 0, y_hi, y_lo)
            for b in range(4):
                lo(N_MQ + b + 1)
                for c in range(2):
                    evac_copy(N_MQ + b, c, mq[:, 2 * b + c, :])
            for u in range(16):
                hd, qb = u // 4, u % 4
                dve.wait_ge(S["ma_score"], u + 1)
                nc.vector.reduce_max(ma_mx, X[u % 2][:, 0:MEM], AX.X).then_inc(S["ma_max"], 1)
                dve.wait_ge(S["ma_max"], u + 1)
                TS(ma_ng, ma_mx, -1.0 / 16, None, ALU.mult).then_inc(S["ma_neg"], 1)
                dve.wait_ge(S["ma_exp"], u + 1)
                nc.vector.reciprocal(ma_r, ma_z).then_inc(S["ma_rz"], 1)
                dve.wait_ge(S["ma_rz"], u + 1)
                TS(me[u % 2][:], me[u % 2][:], ma_r, None, ALU.mult).then_inc(S["ma_p"], 1)
                if qb == 3:
                    for i in range(2):
                        dve.wait_ge(S["ma_hi"], 2 * hd + i + 1)
                        TTO(y_lo[:, 2 * hd + i, :], M[2 * (hd % 2) + i][:], y_hi[:, 2 * hd + i, :].bitcast(f32),
                            ALU.subtract).then_inc(S["ma_lo"], 1)
            resid(N_MO)
            norm_add(3)
            dve.wait_ge(S["st_bias"], 16 * 16)
            norm_apply(3, 3, h, "norm_mlp_w", 0, f_hi, f_lo)
            mlp(N_MLP1, 0)
            norm_add(4)
            norm_final(4, "norm_final_w")
            norm_add(5)
            norm_apply(5, 4, h, "ln_mix_2", 0, g_hi, g_lo_)
            gla_dve(dve, lo, evac_copy, resid)
            norm_add(6)
            norm_apply(6, 5, h, "ln_mlp_2", 0, f_hi, f_lo)
            mlp(N_MLP2, 1)
            norm_add(7)
            norm_apply(7, 6, h, "kv_norm_2", 0, s_hi, s_lo)
            lo(N_WQ)
            evac_copy(N_KV, 0, kf[:])
            evac_copy(N_KV, 1, sv[:].rearrange("p t n -> p (t n)"))
            for i in range(2):
                dve.wait_ge(S["sw_dup"], i + 1)
                nc.vector.tensor_copy(kd[i][:], X[1 + i][:]).then_inc(S["sw_dupev"], 1)
            norm_apply(7, 7, h, "ln_mix_2", 8, s_hi, s_lo)
            for b in range(4):
                lo(N_WQ + b + 1)
                for c in range(2):
                    evac_copy(N_WQ + b, c, sq[:, 2 * b + c, :])
            dve.wait_ge(S["ld_bias"], 16)
            for u in range(32):
                c, qb = u // 4, u % 4
                off = 0 if qb else P
                dve.wait_ge(S["sw_score"], u + 1)
                if u >= 2:
                    dve.wait_ge(S["sw_tr"], u - 1)
                s_ = sc[u % 2][:, :, off:256]
                STT(s_, sw_banks(u)[:, :, off:256], 0.125, bias[:, 2 * c:2 * c + 2, off:256],
                    ALU.mult, ALU.add).then_inc(S["sw_s"], 1)
                dve.wait_ge(S["sw_s"], u + 1)
                nc.vector.reduce_max(sw_mx_, s_, AX.X).then_inc(S["sw_mx"], 1)
                dve.wait_ge(S["sw_mx"], u + 1)
                TTO(sw_mx_, sw_mx_, sinkb[:, 2 * c:2 * c + 2], ALU.max).then_inc(S["sw_m"], 1)
                dve.wait_ge(S["sw_m"], u + 1)
                TS(sw_ng_, sw_mx_, -1.0, None, ALU.mult).then_inc(S["sw_neg"], 1)
                TTO(sw_es_, sinkb[:, 2 * c:2 * c + 2], sw_mx_, ALU.subtract).then_inc(S["sw_es"], 1)
                dve.wait_ge(S["sw_e"], 3 * u + 3)
                TTO(sw_es_, sw_es_, sw_z_, ALU.add).then_inc(S["sw_den"], 1)
                dve.wait_ge(S["sw_den"], u + 1)
                nc.vector.reciprocal(sw_r_, sw_es_).then_inc(S["sw_rd"], 1)
                dve.wait_ge(S["sw_rd"], u + 1)
                TTO(s_, s_, sw_r_.unsqueeze(2).to_broadcast([P, 2, 256 - off]), ALU.mult).then_inc(S["sw_p"], 1)
                if qb == 3:
                    dve.wait_ge(S["sw_hi"], c + 1)
                    TTO(s_lo[:, c, :], M[c % 2][:], s_hi[:, c, :].bitcast(f32), ALU.subtract).then_inc(S["sw_lo"], 1)
            resid(N_SOUT)
            norm_add(8)
            norm_apply(8, 8, h, "ln_mlp_2", 8, f_hi, f_lo)
            mlp(N_MLP3, 2)
            norm_add(9)
            norm_final(9, "ln_final_2")
            for i in range(2 * TT):
                dve.wait_ge(S["fin_tr"], i + 1)
                nc.vector.tensor_copy(ytm[:, i, :], X[2 + i % 2][:]).then_inc(S["fin_ev"], 1)


INPUTS = ["x", "mem", "norm_mix_w", "w_in", "mu_shift", "w_decay0", "w_decay_up", "a0", "a_up", "g_up", "k_k", "k_a", "r_k",
          "lnx_w", "lnx_b", "lam_q1", "lam_k1", "lam_q2", "lam_k2", "subln_w", "w_out", "norm_mem_w", "norm_src_w", "w_mq",
          "w_mk", "w_mv", "w_mo", "norm_mlp_w", "w_up", "w_down", "norm_final_w", "a_w_in_2", "a_w_gk2_2", "a_b_gk_2",
          "a_onorm_2", "a_w_out_2", "kv_norm_2", "w_kv_2", "b_w_q_2", "b_sinks_2", "b_w_out_2", "rel_table_2", "ln_mix_2",
          "ln_mlp_2", "w_up_2", "w_down_2", "ln_final_2"]


def kernel(**inputs):
    import concourse.bacc as _bacc
    from concourse.bass_utils import run_bass_kernel_spmd as _run

    nc = _bacc.Bacc("TRN2", target_bir_lowering=False, num_devices=1)
    given = {name: np.ascontiguousarray(inputs[name]) for name in INPUTS}
    given["consts"] = constants()
    given["onehot"] = bucket_onehot()
    arrays, aps = {}, {}
    for name, a in given.items():
        arrays[f"in_{name}_dram"] = a
        aps[name] = nc.dram_tensor(f"in_{name}_dram", a.shape, mybir.dt.from_np(a.dtype), kind="ExternalInput").ap()
    out = nc.dram_tensor("out_0_dram", (1, T, D), mybir.dt.float32, kind="ExternalOutput").ap()
    program(nc, aps, out)
    r = _run(nc, [arrays], core_ids=[0])
    return r.results[0]["out_0_dram"]
```

```python
import math
from contextlib import ExitStack

import numpy as np

import concourse.bass as bass
from concourse import mybir

P = 128
T = 512
D = 1024
KT = D // P
BW = 256
TT = T // P
MEM = 256
RW_COLS, RW_W, DIFF_W = 1792, 512, 512
FF = 4 * D
LAM_INIT = 0.8 - 0.6 * math.exp(-0.3 * 0)
C0 = math.exp(-0.5)
NEG = -1e30

VECS = [("norm_mix_w", 8), ("norm_src_w", 8), ("norm_mem_w", 8), ("norm_mlp_w", 8), ("norm_final_w", 8),
        ("mu_shift", 14), ("w_decay0", 4), ("a0", 4), ("k_k", 4), ("k_a", 4), ("r_k", 4), ("lnx_w", 4),
        ("lnx_b", 4), ("subln_w", 1), ("a_b_gk_2", 4), ("a_onorm_2", 2), ("kv_norm_2", 8), ("ln_mix_2", 16),
        ("ln_mlp_2", 16), ("ln_final_2", 8)]
VEC_ROW, _r = {}, 0
for _n, _k in VECS:
    VEC_ROW[_n] = _r
    _r += _k
VEC_ROWS = _r

CONST, _c = {}, 0
for _n, _k in [("ident", 128), ("ones", 128), ("blk64", 128), ("seg", 512), ("lower", 64), ("upper", 64),
               ("upper_in", 64), ("low16", 64), ("up16", 64), ("low32", 64), ("low64", 64), ("eye64", 64),
               ("gla", 128), ("sel0", 128), ("sel1", 128), ("plusminus", 128), ("eps5", 1), ("eps6", 1),
               ("epsgn", 1), ("kkb", 1), ("one", 1), ("zero", 1), ("pad", 2)]:
    CONST[_n] = (_c, _k)
    _c += _k
CONST_COLS = _c


def constants():
    out = np.zeros((P, CONST_COLS), np.float32)

    def put(name, value):
        at, n = CONST[name]
        out[:, at:at + n] = value

    p = np.arange(P)[:, None]
    f = np.arange(P)[None, :]
    a, b = p % 64, np.arange(64)[None, :]
    put("ident", p == f)
    put("ones", 1.0)
    put("blk64", p // 64 == f // 64)
    put("seg", (np.arange(T) % 64 != 0)[None, :])
    put("lower", b < a)
    put("upper", a < b)
    put("upper_in", a <= b)
    put("low16", (b < a) & (a // 16 == b // 16))
    put("up16", (a < b) & (a // 16 == b // 16))
    put("low32", (a // 32 == b // 32) & (a // 16 > b // 16))
    put("low64", a // 32 > b // 32)
    put("eye64", a == b)
    put("gla", (p // 64 == f // 64) & (p <= f))
    put("sel0", p == f % 64)
    put("sel1", p == 64 + f % 64)
    put("plusminus", np.where(p == 0, 1.0, np.where(p == 1, -1.0, 0.0)))
    put("eps5", 1e-5)
    put("eps6", 1e-6)
    put("epsgn", 64e-5)
    put("kkb", 10.0 * math.log(2.0))
    put("one", 1.0)
    return out


def bucket_onehot():
    dist = 255 - np.arange(384)
    n = np.maximum(dist, 0)
    large = 16 + (np.log(np.maximum(n, 1) / 16) / np.log(128 / 16) * 16).astype(np.int32)
    bucket = np.where(n < 16, n, np.minimum(large, 31))
    valid = (dist >= 0) & (dist < 128)
    hot = (bucket[None, :] == np.arange(32)[:, None]) & valid[None, :]
    out = np.zeros((33, 384), np.float32)
    out[:32] = hot
    out[32] = np.where(valid, 0.0, NEG)
    return out


N_DQ, N_DK, N_DV, N_RW = 0, 2, 4, 6
N_WOUT, N_MK, N_MV, N_MQ, N_MO, N_MLP1 = 13, 17, 21, 25, 29, 33
N_GLR, N_GQK, N_GV, N_GG, N_GOUT, N_MLP2 = 65, 66, 70, 74, 78, 82
N_KV, N_WQ, N_SOUT, N_MLP3 = 114, 115, 119, 123
N_END = 155


def acc_before(n):
    return 2 * n - 16 * sum(n >= m + 32 for m in (N_MLP1, N_MLP2, N_MLP3))


RW_STEPS = (["kk2", "bonus", "tA", "tBd", "tKd", "tV", "L", "LT", "RBT", "AKT", "RKT", "X", "P2", "PT2", "TT2", "P4",
             "PT4", "TT3", "P8", "TT4", "T4", "Z", "TT5", "T5", "Z2", "TT6", "W", "G", "MT", "N", "RT"]
            + [f"S{c}" for c in range(1, 7)] + ["Y", "mean", "var", "gate"])
RW_SEQ = []
for _g in range(2):
    RW_SEQ += [(st, hp) for st in ["zw", "za"] + RW_STEPS for hp in (2 * _g, 2 * _g + 1)]
RW_NO = {x: i for i, x in enumerate(RW_SEQ)}


def program(nc, A, out):
    f32, f32r, i32 = mybir.dt.float32, mybir.dt.float32r, mybir.dt.int32
    ALU, ACT, AX = mybir.AluOpType, mybir.ActivationFunctionType, mybir.AxisListType
    ds = bass.ds
    ctx = ExitStack()
    with ctx:
        sem_names = """ld_const ld_vec ld_small ld_lora ld_x0 ld_x1 ld_x2 ld_x3 ld_mem ld_gk ld_bias ld_rel st_bias st_out raw_lo
            w_hi_ready w_lo_ready acc_done acc_evac vec_tr vec_ready xt_tr xt_ev bias_mm bias_ev
            norm_sq norm_add norm_ss norm_ln norm_rstd x_hi x_lo h_final
            mn_sq mn_add mn_ss mn_ln mn_rstd mx_hi mx_lo
            lam_mul lam_e lam_mm lam_ready
            da_score da_fill da_max da_neg da_exp da_rz da_c2 da_e1 da_attn da_tr da_at da_pv da_o
            da_sq da_ss da_ln da_rstd da_y
            rw_zero rw_shift rw_p rw_act rw_dve rw_half rw_mm rw_ev rw_exp y_hi y_lo
            mt_tr mt_ev ma_score ma_max ma_neg ma_exp ma_rz ma_p ma_tr ma_pt ma_pv ma_hi ma_lo
            up_sq up_hi up_lo
            g_gk g_ab g_ln g_act g_dve g_sc g_at g_kt g_ktev g_n g_s g_o g_oev g_sq g_ss g_rl g_rstd g_hi g_lo g_zero g_o1 g_cs g_gate
            sw_dup sw_dupev sw_score sw_s sw_mx sw_m sw_neg sw_e sw_es sw_den sw_rd sw_p sw_tr sw_pt sw_pv sw_hi sw_lo
            fin_tr fin_ev dve_link act_link""".split()
        S = {n: ctx.enter_context(nc.semaphore(n)) for n in sem_names}
        w_arrived = [ctx.enter_context(nc.semaphore(f"w_arrived{i}")) for i in range(4)]

        def at(off, name, shape, dt=f32):
            nbytes = 4 * int(np.prod(shape[1:]))
            t = nc.alloc_sbuf_tensor_at(name, shape, dt, offset=off[0])
            off[0] += (nbytes + 31) // 32 * 32
            return t

        o = [16512]
        h = at(o, "h", [P, KT, T])
        raw = at(o, "raw", [P, 4, KT, BW])
        w_hi = at(o, "w_hi", [P, 2, KT, BW], f32r)
        w_lo = at(o, "w_lo", [P, 2, KT, BW], f32r)
        cst = at(o, "cst", [P, CONST_COLS])
        vec = at(o, "vec", [P, VEC_ROWS])
        rstd = at(o, "rstd", [P, T])
        nt = [at(o, f"nt{i}", [P, T]) for i in range(3)]
        rcol = at(o, "rcol", [P, TT])
        small = at(o, "small", [P, 128])
        arena = o[0]
        KB = 1024

        o = [arena]
        y_diff = at(o, "y_diff", [P, 4, T])
        p_rw = at(o, "p_rw", [P, 14, T + 1])
        lora = at(o, "lora", [P, RW_W])
        g_up = at(o, "g_up", [P, RW_W])
        mixing = o[0]
        xm_hi, xm_lo = at(o, "xm_hi", [P, KT, T], f32r), at(o, "xm_lo", [P, KT, T], f32r)
        dq, dk = at(o, "dq", [P, 4, T]), at(o, "dk", [P, 4, T])
        dv = at(o, "dv", [P, TT, DIFF_W])
        de_sq, da_rs = nt[0], nt[1]
        de = [at(o, f"de{i}", [P, T]) for i in range(2)]
        da_t = at(o, "da_t", [P, TT, P])
        da_out = at(o, "da_out", [P, T])
        top1 = o[0]
        o = [mixing + 2 * 4 * KT * T]
        xt = at(o, "xt", [P, TT, D])
        vrow = at(o, "vrow", [P, 2, P])
        lamv = at(o, "lamv", [2, 2, 64])
        o = [mixing]
        tm = [[at(o, f"tm{b}_{i}", [P, 4, P]) for i in range(4)] for b in range(2)]
        mt = [[at(o, f"mt{b}_{i}", [P, T]) for i in range(11)] for b in range(2)]
        bon = [at(o, f"bon{b}", [P, T]) for b in range(2)]
        top2 = o[0]
        o = [arena]
        x2_hi, x2_lo = at(o, "x2_hi", [P, KT, T], f32r), at(o, "x2_lo", [P, KT, T], f32r)
        me = [at(o, f"me{i}", [P, 4, MEM]) for i in range(2)]
        assert o[0] <= mixing
        o = [mixing]
        y_hi, y_lo = at(o, "yy_hi", [P, KT, T], f32r), at(o, "yy_lo", [P, KT, T], f32r)
        mrow = at(o, "mrow", [P, 2, D])
        memT = at(o, "memT", [P, KT, MEM])
        m_hi, m_lo = at(o, "m_hi", [P, KT, MEM], f32r), at(o, "m_lo", [P, KT, MEM], f32r)
        mnt = [at(o, f"mnt{i}", [P, MEM]) for i in range(3)]
        rstdm = at(o, "rstdm", [P, MEM])
        rcolm = at(o, "rcolm", [P, 2])
        top3 = o[0]
        o = [mixing]
        mk = at(o, "mk", [P, KT, MEM])
        mv = at(o, "mv", [P, 2, D])
        mq = at(o, "mq", [P, KT, T])
        o_hi, o_lo = at(o, "o_hi", [P, KT, T], f32r), at(o, "o_lo", [P, KT, T], f32r)
        o = [top3]
        onehot = at(o, "onehot_sb", [33, 384])
        relx = at(o, "relx", [33, 16])
        top3 = o[0]
        o = [mixing + 64 * KB]
        biasrow = [at(o, f"biasrow{i}", [P, 384]) for i in range(2)]
        mpt = [nt[i][:, 0:MEM].rearrange("p (a n) -> p a n", a=2) for i in range(2)]
        def mlp_memory(nth, fo, uo, vo):
            f = [at([arena + fo * KB + 16 * KB * i], f"f{nth}_{i}", [P, KT, T], f32r) for i in range(2)]
            u = [at([arena + a * KB], f"u{nth}_{i}", [P, 16, T], f32r) for i, a in enumerate((uo, vo))]
            return f + u

        mem_of = [mlp_memory(0, 0, 32, 64), mlp_memory(1, 32, 0, 64), mlp_memory(2, 0, 32, 64)]
        o = [arena + 96 * KB]
        ut, us = [at(o, f"ut{i}", [P, T]) for i in range(2)], [nt[0], nt[1]]
        top4 = o[0]
        o = [arena]
        g_hi, g_lo_ = at(o, "gx_hi", [P, KT, T], f32r), at(o, "gx_lo", [P, KT, T], f32r)
        gq, gk, gb = (at(o, n, [P, 4, T]) for n in ("gq", "gk", "gb"))
        gv = at(o, "gv", [P, TT, D])
        gg = at(o, "gg", [P, KT, T])
        gs = [at(o, f"gs{i}", [P, 4, 256]) for i in range(2)]
        gat = [at(o, f"gat{i}", [P, 4, P]) for i in range(2)]
        gkt = at(o, "gkt", [P, 4, P])
        glr = at(o, "glr", [16, T])
        w_gk2 = at(o, "w_gk2", [16, 512])
        top5 = o[0]
        o = [arena]
        sx_hi, sx_lo = at(o, "sx_hi", [P, KT, T], f32r), at(o, "sx_lo", [P, KT, T], f32r)
        kx_hi, kx_lo = at(o, "kx_hi", [P, KT, T], f32r), at(o, "kx_lo", [P, KT, T], f32r)
        s_hi, s_lo = at([arena + 32 * KB], "so_hi", [P, KT, T], f32r), at([arena + 48 * KB], "so_lo", [P, KT, T], f32r)
        kf = nt[2]
        kd = [at(o, f"kd{i}", [P, T]) for i in range(2)]
        sv = at(o, "sv", [P, TT, P])
        sq = at(o, "sq", [P, KT, T])
        bias = at(o, "bias", [P, 16, 256])
        sc = [at(o, f"sc{i}", [P, 2, 256]) for i in range(2)]
        spt = [at(o, f"spt{i}", [P, 4, P]) for i in range(2)]
        top6 = o[0]
        ytm = sq
        assert max(top1, top2, top3, top4, top5, top6) <= 16481 + 212863, (top1, top2, top3, top4, top5, top6)

        Mall = ctx.enter_context(nc.psum_tensor("M", [P, 4, T], f32))
        Xall = ctx.enter_context(nc.psum_tensor("X", [P, 4, T], f32))
        M, X = [Mall[:, i, :] for i in range(4)], [Xall[:, i, :] for i in range(4)]
        RB = X + M

        def sw_banks(u):
            return (Xall[:, 0:2, :], Mall[:, 2:4, :])[u % 2]

        bias_rows = nc.dram_tensor("bias_rows", [16, P, 384], f32, kind="Internal").ap()

        def ytm_view(t):
            return ytm[:, 2 * t:2 * t + 2, :].rearrange("p a n -> p (a n)")

        def C(name, rows=slice(0, P)):
            a, n = CONST[name]
            return cst[rows, a:a + n]

        def V(name, i, rows=slice(0, P)):
            return vec[rows, VEC_ROW[name] + i:VEC_ROW[name] + i + 1]

        lamneg, lame = small[:, 0:1], small[0:2, 1:2]
        lamd, onec = small[0:2, 2:3], small[:, 3:4]
        da_mx, da_ng, da_z, da_r, da_c = (small[:, 4 + 2 * i:6 + 2 * i] for i in range(5))
        sub_w = small[:, 14:15]
        ma_mx, ma_ng, ma_z, ma_r = (small[:, 16 + i:17 + i] for i in range(4))
        sinkb = small[:, 32:48]
        sw_mx_, sw_ng_, sw_z_, sw_es_, sw_r_ = (small[:, 48 + 2 * i:50 + 2 * i] for i in range(5))
        g_el = small[:, 64:96]
        rw_dc = [small[:, 96:104], small[:, 104:112]]
        seg = C("seg")

        def W(ap):
            return ap.rearrange("(k p) n -> p k n", p=P)

        w_in, a_in = W(A["w_in"][0]), W(A["a_w_in_2"][0])
        plain = [(N_DQ, 2, w_in, RW_COLS), (N_DK, 2, w_in, RW_COLS + 512), (N_DV, 2, w_in, RW_COLS + 1024),
                 (N_RW, 7, w_in, 0), (N_WOUT, 4, W(A["w_out"][0]), 0), (N_MK, 4, W(A["w_mk"][0]), 0),
                 (N_MV, 4, W(A["w_mv"][0]), 0), (N_MQ, 4, W(A["w_mq"][0]), 0), (N_MO, 4, W(A["w_mo"][0]), 0),
                 (N_GLR, 1, a_in, 3072), (N_GQK, 4, a_in, 0), (N_GV, 4, a_in, 1024), (N_GG, 4, a_in, 2048),
                 (N_GOUT, 4, W(A["a_w_out_2"][0]), 0), (N_KV, 1, W(A["w_kv_2"]), 0), (N_WQ, 4, W(A["b_w_q_2"][0]), 0),
                 (N_SOUT, 4, W(A["b_w_out_2"][0]), 0)]
        mlps = {N_MLP1: (W(A["w_up"][0]), W(A["w_down"][0])), N_MLP2: (W(A["w_up_2"][0]), W(A["w_down_2"][0])),
                N_MLP3: (W(A["w_up_2"][1]), W(A["w_down_2"][1]))}
        GLR = 16

        HF = 8 * 2
        LAST = N_END
        bias_skewed = lambda: bass.AP(bias_rows.tensor, P - 1, [[384 - 1, P], [P * 384, 16], [1, 256]])
        block = ctx.enter_context(nc.Block())

        SLOT = dict(P=0, Bd=1, B=2, Kd=3, PT=4, O32=5, O64=6, RBT=7, AKT=8, RKT=9, A=10,
                    P2=1, PT2=3, TT=2, P4=0, PT4=4, P8=1, T=3, Z=4, W=0, G=1, MT=5, N=6, RT=8, X=10, S=3, Y=4,
                    cs=5, sw=6, ex=0, inc=4, neg=7, dec=8, a=9, kk=10, t=1, d=2, dsq=5, rs=7)
        RW_ACT = ["sigw", "siga", "ex", "inc", "neg", "dec", "dc", "sq", "ln", "rn", "dsq", "gln", "grs"]
        RW_DVE = ["csx", "dl", "kkraw", "kmod", "kk", "rk", "beta", "K", "Kd", "R", "B", "Bd", "A", "yb", "yc"]
        pairs = [(0, 1), (2, 3)]
        ACT_NO = {x: i + 3 for i, x in enumerate((op, hp) for g in pairs for op in RW_ACT for hp in g)}
        DVE_NO = {x: i + 1 for i, x in enumerate((op, hp) for g in pairs for op in RW_DVE for hp in g)}

        def ev(st, hp):
            return RW_NO[(st, hp)] + 1

        def sl(name, hp):
            return mt[hp % 2][SLOT[name]]

        def rkv(i, hp, lo_=1):
            return p_rw[:, 4 * i + hp, lo_:lo_ + T]

        def rwkv_pe(pe, mm, wait):
            def blk(t, hh, cp, cpar):
                return t[64 * cpar:64 * cpar + 64, (4 * hh + cp) * 64:(4 * hh + cp) * 64 + 64]

            def fm(t, hh, c):
                return t[64 * hh:64 * hh + 64, 64 * c:64 * c + 64]

            def tmv(i, hp, hh, cp, cpar):
                return tm[hp % 2][i][64 * cpar:64 * cpar + 64, cp, 64 * hh:64 * hh + 64]

            mats = dict(X=("AKT", "V"), P2=("PT", "P"), PT2=("P", "PT"), TT2=("P2", "TT"), P4=("PT2", "P2"),
                        PT4=("P2", "PT2"), TT3=("P4", "TT"), P8=("PT4", "P4"), TT4=("P8", "TT"), T4=("TT", "eye"),
                        Z=("O32", "TT"), TT5=("T", "Z"), T5=("Z", "T"), Z2=("O64", "TT"), TT6=("T", "Z"),
                        W=("TT", "Atm"), G=("TT", "X"))
            feats = dict(L=("A", "B"), LT=("B", "A"), RBT=("B", "R"), AKT=("K", "A"), RKT=("K", "R"))
            tms = dict(Atm=0, Bdtm=1, Kdtm=2, V=3)
            after = dict(L=("dve", "A"), LT=("dve", "A"), RBT=("dve", "A"), AKT=("dve", "A"), RKT=("dve", "A"),
                         tA=("dve", "A"), tBd=("dve", "A"), tKd=("dve", "A"), tV=("dve", "A"), kk2=("act", "sq"),
                         bonus=("dve", "rk"), X="AKT", P2="RBT", PT2="RBT", TT2="P2", P4="PT2", PT4="PT2", TT3="P4",
                         P8="PT4", TT4="P8", T4="TT4", Z="TT4", TT5="Z", T5="TT5", Z2="TT5", TT6="Z2", W="TT6", G="TT6",
                         MT="W", N="G", RT="W", S1="N", Y="S6", mean="Y", var=("act", "dsq"), gate="mean")
            for i in range(2, 7):
                after[f"S{i}"] = f"S{i - 1}"

            def operand(name, hp, hh, cp, cpar):
                if name == "eye":
                    return C("eye64", slice(64 * cpar, 64 * cpar + 64))
                if name in tms:
                    return tmv(tms[name], hp, hh, cp, cpar)
                return blk(sl(name, hp), hh, cp, cpar)

            halves = [0]

            def half_done(ins):
                ins.then_inc(S["rw_half"], 1)
                halves[0] += 1
                wait("rw_half", halves[0])

            for (st, hp), no in RW_NO.items():
                bank = RB[no % 8]
                if no >= 8:
                    wait("rw_ev", no - 7)
                dep = after.get(st)
                if isinstance(dep, tuple):
                    wait("rw_act" if dep[0] == "act" else "rw_dve", (ACT_NO if dep[0] == "act" else DVE_NO)[(dep[1], hp)])
                elif dep:
                    wait("rw_ev", ev(dep, hp))
                fs = slice(hp * P, hp * P + P)
                if st == "zw":
                    wait("ld_lora", 48)
                    last = mm(bank[:], lora[0:64, fs], p_rw[0:64, 12, 1:T + 1], start=True, stop=True)
                elif st == "za":
                    last = mm(bank[:], lora[64:128, fs], p_rw[64:128, 12, 1:T + 1], start=True, stop=True)
                elif st == "gate":
                    last = mm(bank[:], g_up[:, fs], p_rw[:, 13, 1:T + 1], start=True, stop=True)
                elif st in ("kk2", "bonus"):
                    last = mm(bank[:], C("blk64"), nt[hp % 2][:], start=True, stop=True)
                elif st in ("mean", "var"):
                    last = mm(bank[:], C("blk64"), sl("Y" if st == "mean" else "dsq", hp)[:], start=True, stop=True)
                elif st in ("tA", "tBd", "tKd", "tV"):
                    src = rkv(2, hp) if st == "tV" else sl(st[1:], hp)[:]
                    for cp in range(4):
                        last = nc.tensor.transpose(bank[:, cp * P:cp * P + P], src[:, cp * P:cp * P + P], C("ident"))
                elif st in feats:
                    a_, b_ = (rkv(0 if n == "R" else 1, hp) if n in "RK" else sl(n, hp) for n in feats[st])
                    for hh in range(2):
                        if hh:
                            half_done(last)
                        for cp in range(4):
                            for cpar in range(2):
                                c = 2 * cp + cpar
                                last = mm(blk(bank, hh, cp, cpar), fm(a_, hh, c), fm(b_, hh, c), start=True, stop=True)
                elif st in mats:
                    for hh in range(2):
                        for cp in range(4):
                            for cpar in range(2):
                                a_, b_ = (operand(n, hp, hh, cp, cpar) for n in mats[st])
                                last = mm(blk(bank, hh, cp, cpar), a_, b_, start=True, stop=True)
                elif st[0] == "S":
                    c = int(st[1:])
                    for hh in range(2):
                        last = mm(bank[64 * hh:64 * hh + 64, 0:64], fm(sl("MT", hp), hh, c), fm(sl("S", hp), hh, c),
                                  start=True, stop=True)
                elif st != "Y":
                    for turn in range(2):
                        if turn:
                            half_done(last)
                        for cp in range(4):
                            for cpar in range(2):
                                hh = cpar ^ turn
                                o_ = fm(bank, hh, 2 * cp + cpar)
                                if st == "MT":
                                    last = mm(o_, blk(sl("W", hp), hh, cp, cpar), tmv(1, hp, hh, cp, cpar), start=True, stop=True)
                                elif st == "RT":
                                    last = mm(o_, blk(sl("W", hp), hh, cp, cpar), blk(sl("RBT", hp), hh, cp, cpar), start=True, stop=True)
                                else:
                                    mm(o_, tmv(1, hp, hh, cp, cpar), blk(sl("G", hp), hh, cp, cpar), start=True, stop=False)
                                    last = mm(o_, tmv(2, hp, hh, cp, cpar), tmv(3, hp, hh, cp, cpar), start=False, stop=True)
                else:
                    for turn in range(2):
                        if turn:
                            half_done(last)
                        for cp in range(4):
                            for cpar in range(2):
                                hh = cpar ^ turn
                                o_ = fm(bank, hh, 2 * cp + cpar)
                                mm(o_, blk(sl("G", hp), hh, cp, cpar), blk(sl("RBT", hp), hh, cp, cpar),
                                   start=turn == 0 and cp == 0, stop=False, skip_group_check=True)
                                last = mm(o_, tmv(3, hp, hh, cp, cpar), blk(sl("RKT", hp), hh, cp, cpar), start=False,
                                          stop=False, skip_group_check=True)
                    half_done(last)
                    for c in range(1, 8):
                        for hh in range(2):
                            last = mm(fm(bank, hh, c), fm(sl("S", hp), hh, c), fm(sl("RT", hp), hh, c), start=False,
                                      stop=c == 7, skip_group_check=True)
                last.then_inc(S["rw_mm"], 1)

        def rwkv_act(act):
            def go(op, hp, out_, in_, func, **kw):
                nc.scalar.activation(out_, in_, func, **kw).then_inc(S["rw_act"], 1)

            def dve(op, hp):
                act.wait_ge(S["rw_dve"], DVE_NO[(op, hp)])

            def own(op, hp):
                act.wait_ge(S["rw_act"], ACT_NO[(op, hp)])

            for g in pairs:
                for hp in g:
                    act.wait_ge(S["rw_mm"], ev("zw", hp))
                    if hp >= 2:
                        act.wait_ge(S["rw_ev"], ev("gate", hp - 2))
                    go("sigw", hp, sl("sw", hp)[:], RB[RW_NO[("zw", hp)] % 8][:], ACT.Sigmoid, bias=V("w_decay0", hp))
                for hp in g:
                    act.wait_ge(S["rw_mm"], ev("za", hp))
                    go("siga", hp, sl("a", hp)[:], RB[RW_NO[("za", hp)] % 8][:], ACT.Sigmoid, bias=V("a0", hp))
                nc.scalar.preload_act_table_set("natural_log_exp_and_others")
                for hp in g:
                    dve("csx", hp)
                    go("ex", hp, sl("ex", hp)[:], sl("sw", hp)[:], ACT.Exp, scale=-C0)
                for hp in g:
                    go("inc", hp, sl("inc", hp)[:], sl("cs", hp)[:], ACT.Exp, scale=-C0)
                for hp in g:
                    go("neg", hp, sl("neg", hp)[:], sl("cs", hp)[:], ACT.Exp, scale=C0)
                for hp in g:
                    dve("dl", hp)
                    go("dec", hp, sl("dec", hp)[:], sl("dec", hp)[:], ACT.Exp, scale=-C0)
                for hp in g:
                    go("dc", hp, rw_dc[hp % 2], sl("cs", hp)[:].rearrange("p (c t) -> p c t", t=64)[:, :, 63], ACT.Exp,
                       scale=-C0)
                for hp in g:
                    dve("kkraw", hp)
                    go("sq", hp, nt[hp % 2][:], sl("kk", hp)[:], ACT.Square)
                for hp in g:
                    act.wait_ge(S["rw_ev"], ev("kk2", hp))
                    go("ln", hp, nt[hp % 2][:], nt[hp % 2][:], ACT.Ln, scale=float(2 ** 20))
                for hp in g:
                    own("ln", hp)
                    go("rn", hp, nt[hp % 2][:], nt[hp % 2][:], ACT.Exp, scale=-0.5, bias=C("kkb"))
                for hp in g:
                    act.wait_ge(S["rw_ev"], ev("mean", hp))
                    go("dsq", hp, sl("dsq", hp)[:], sl("d", hp)[:], ACT.Square)
                for hp in g:
                    act.wait_ge(S["rw_mm"], ev("var", hp))
                    go("gln", hp, sl("rs", hp)[:], RB[RW_NO[("var", hp)] % 8][:], ACT.Ln, scale=1.0 / 64, bias=C("epsgn"))
                for hp in g:
                    own("gln", hp)
                    go("grs", hp, sl("rs", hp)[:], sl("rs", hp)[:], ACT.Exp, scale=-0.5)

        def rwkv_dve(dve):
            TTO, TS, STT = nc.vector.tensor_tensor, nc.vector.tensor_scalar, nc.vector.scalar_tensor_tensor

            def a8(ap):
                return ap.rearrange("p (c t) -> p c t", t=64)

            def bank(st, hp):
                return RB[RW_NO[(st, hp)] % 8]

            def mm_done(st, hp):
                dve.wait_ge(S["rw_mm"], ev(st, hp))

            def evd(ins):
                ins.then_inc(S["rw_ev"], 1)

            def own(op, hp):
                dve.wait_ge(S["rw_dve"], DVE_NO[(op, hp)])

            def own_ev(st, hp):
                dve.wait_ge(S["rw_ev"], ev(st, hp))

            def act(op, hp):
                dve.wait_ge(S["rw_act"], ACT_NO[(op, hp)])

            def go(ins):
                ins.then_inc(S["rw_dve"], 1)

            def mask(name):
                return C(name).unsqueeze(1).to_broadcast([P, 8, 64])

            for g in pairs:
                for hp in g:
                    act("sigw", hp)
                    evd(nc.vector.tensor_tensor_scan(sl("cs", hp)[:], seg, sl("sw", hp)[:], 0.0, ALU.mult, ALU.add))
                for hp in g:
                    act("siga", hp)
                    evd(TS(sl("t", hp)[:], sl("a", hp)[:], -1.0, V("k_a", hp), ALU.add, ALU.mult))
                for hp in g:
                    own_ev("zw", hp)
                    go(TTO(sl("sw", hp)[:], sl("cs", hp)[:], sl("sw", hp)[:], ALU.subtract))
                for hp in g:
                    cs8 = a8(sl("cs", hp)[:])
                    go(TTO(a8(sl("dec", hp)[:]), cs8[:, :, 63:64].to_broadcast([P, 8, 64]), cs8, ALU.subtract))
                for hp in g:
                    go(TS(sl("kk", hp)[:], rkv(1, hp), V("k_k", hp), None, ALU.mult))
                for hp in g:
                    own_ev("za", hp)
                    go(STT(sl("t", hp)[:], sl("t", hp)[:], 1.0, rkv(1, hp), ALU.add, ALU.mult))
                for hp in g:
                    mm_done("kk2", hp)
                    evd(nc.vector.tensor_scalar_max(nt[hp % 2][:], bank("kk2", hp)[:], 1e-24))
                for hp in g:
                    act("rn", hp)
                    go(TTO(sl("kk", hp)[:], sl("kk", hp)[:], nt[hp % 2][:], ALU.mult))
                for hp in g:
                    own("kmod", hp)
                    own("kk", hp)
                    go(STT(nt[hp % 2][:], rkv(0, hp), V("r_k", hp), sl("t", hp)[:], ALU.mult, ALU.mult))
                for hp in g:
                    mm_done("bonus", hp)
                    evd(TTO(bon[hp % 2][:], bank("bonus", hp)[:], rkv(2, hp), ALU.mult))
                for hp in g:
                    go(TTO(sl("a", hp)[:], sl("kk", hp)[:], sl("a", hp)[:], ALU.mult))
                for hp in g:
                    act("dc", hp)
                    go(TTO(rkv(1, hp), sl("t", hp)[:], sl("neg", hp)[:], ALU.mult))
                for hp in g:
                    go(TTO(sl("Kd", hp)[:], sl("t", hp)[:], sl("dec", hp)[:], ALU.mult))
                for hp in g:
                    go(TTO(rkv(0, hp), rkv(0, hp), sl("inc", hp)[:], ALU.mult))
                for hp in g:
                    own("beta", hp)
                    go(TTO(sl("B", hp)[:], sl("a", hp)[:], sl("neg", hp)[:], ALU.mult))
                for hp in g:
                    own("Kd", hp)
                    go(TTO(sl("Bd", hp)[:], sl("a", hp)[:], sl("dec", hp)[:], ALU.mult))
                for hp in g:
                    go(STT(sl("A", hp)[:], sl("kk", hp)[:], -1.0, sl("ex", hp)[:], ALU.mult, ALU.mult))
                for i, st in enumerate(("tA", "tBd", "tKd", "tV")):
                    for hp in g:
                        mm_done(st, hp)
                        evd(nc.vector.tensor_copy(tm[hp % 2][i][:].rearrange("p c f -> p (c f)"), bank(st, hp)[:]))
                for hp in g:
                    mm_done("L", hp)
                    for name, m in (("P", "low16"), ("O32", "low32"), ("O64", "low64")):
                        last = TTO(a8(sl(name, hp)[:]), a8(bank("L", hp)[:]), mask(m), ALU.mult)
                    evd(last)
                for st, name, m in (("LT", "PT", "up16"), ("RBT", "RBT", "upper_in"), ("AKT", "AKT", "upper"),
                                    ("RKT", "RKT", "upper_in")):
                    for hp in g:
                        mm_done(st, hp)
                        if st == "RBT":
                            own_ev("LT", hp)
                            TTO(a8(sl("TT", hp)[:]), a8(sl("PT", hp)[:]), mask("eye64"), ALU.add)
                        evd(TTO(a8(sl(name, hp)[:]), a8(bank(st, hp)[:]), mask(m), ALU.mult))
                for st, name, add in (("X", "X", 0), ("P2", "P2", 0), ("PT2", "PT2", 0), ("TT2", "TT", 1), ("P4", "P4", 0),
                                      ("PT4", "PT4", 0), ("TT3", "TT", 1), ("P8", "P8", 0), ("TT4", "TT", 1), ("T4", "T", 0),
                                      ("Z", "Z", 0), ("TT5", "TT", 1), ("T5", "T", 1), ("Z2", "Z", 0), ("TT6", "TT", 1),
                                      ("W", "W", 0), ("G", "G", 0)):
                    for hp in g:
                        mm_done(st, hp)
                        if add:
                            evd(TTO(sl(name, hp)[:], bank(st, hp)[:], sl(name, hp)[:], ALU.add))
                        else:
                            evd(nc.vector.tensor_copy(sl(name, hp)[:], bank(st, hp)[:]))
                for hp in g:
                    mm_done("MT", hp)
                    go_diag = TTO(a8(sl("MT", hp)[:]), mask("eye64"),
                                  rw_dc[hp % 2].unsqueeze(2).to_broadcast([P, 8, 64]), ALU.mult)
                    go_diag.then_inc(S["dve_link"], 1)
                    dve.wait_ge(S["dve_link"], hp + 1)
                    evd(TTO(sl("MT", hp)[:], bank("MT", hp)[:], sl("MT", hp)[:], ALU.add))
                for hp in g:
                    mm_done("N", hp)
                    nc.vector.tensor_copy(sl("S", hp)[:, 64:128], bank("N", hp)[:, 0:64])
                    evd(nc.vector.tensor_copy(sl("N", hp)[:], bank("N", hp)[:]))
                for hp in g:
                    mm_done("RT", hp)
                    evd(TTO(sl("RT", hp)[:], bank("RT", hp)[:], rkv(0, hp), ALU.add))
                for c in range(1, 7):
                    for hp in g:
                        mm_done(f"S{c}", hp)
                        evd(TTO(sl("S", hp)[:, 64 * (c + 1):64 * (c + 2)], bank(f"S{c}", hp)[:, 0:64],
                                sl("N", hp)[:, 64 * c:64 * c + 64], ALU.add))
                for hp in g:
                    mm_done("Y", hp)
                    evd(nc.vector.tensor_copy(sl("Y", hp)[:], bank("Y", hp)[:]))
                for hp in g:
                    mm_done("mean", hp)
                    evd(STT(sl("d", hp)[:], bank("mean", hp)[:], -1.0 / 64, sl("Y", hp)[:], ALU.mult, ALU.add))
                for hp in g:
                    act("grs", hp)
                    evd(TTO(sl("d", hp)[:], sl("d", hp)[:], sl("rs", hp)[:], ALU.mult))
                for hp in g:
                    own_ev("var", hp)
                    go(TS(sl("d", hp)[:], sl("d", hp)[:], V("lnx_w", hp), V("lnx_b", hp), ALU.mult, ALU.add))
                for hp in g:
                    own("yb", hp)
                    go(TTO(sl("d", hp)[:], sl("d", hp)[:], bon[hp % 2][:], ALU.add))
                for hp in g:
                    mm_done("gate", hp)
                    own("yc", hp)
                    evd(TTO(rkv(0, hp), bank("gate", hp)[:], sl("d", hp)[:], ALU.mult))

        def gla_pe(pe, mm, wait, chunk, blocks, block_tm):
            chunk(N_GLR, 0, g_hi, g_lo_, first=24, cols=GLR, inc=2)
            blocks(N_GQK, 1, g_hi, g_lo_)
            wait("acc_evac", acc_before(N_GQK))
            wait("ld_gk", 16)
            wait("norm_rstd", 5)
            for c in range(4):
                mm(X[c][:], w_gk2[:, c * P:c * P + P], glr[:], start=True, stop=True).then_inc(S["g_gk"], 1)
            blocks(N_GQK + 1, 3, g_hi, g_lo_)
            for b in range(4):
                block_tm(N_GV + b, g_hi, g_lo_, TT, 2)
            blocks(N_GG, 4, g_hi, g_lo_)
            wait("acc_evac", acc_before(N_GOUT))
            wait("g_gate", KT)
            wait("g_sc", 4 * 6)
            wait("g_zero", 2)
            for cp in range(4):
                if cp:
                    wait("g_at", cp)
                tok = slice(cp * P, cp * P + P)
                for hd in range(4):
                    last = mm(X[0][:, hd * P:hd * P + P], gb[:, hd, tok], gq[:, hd, tok], start=True, stop=True)
                last.then_inc(S["g_kt"], 1)
                if cp:
                    wait("g_rl", cp)
                for hd in range(4):
                    last = nc.tensor.transpose(X[1][:, hd * P:hd * P + P], gk[:, hd, tok], C("ident"))
                last.then_inc(S["g_kt"], 1)
                if cp >= 2:
                    wait("g_oev", 4 * (cp - 1))
                wait("g_at", cp + 1)
                wait("g_ktev", cp + 1)
                ob = [M[2 * (cp % 2)], M[2 * (cp % 2) + 1]]
                for hd in range(4):
                    for vc in range(2):
                        a_ = (2 * (hd % 2) + vc) * P
                        mm(ob[hd // 2][:, a_:a_ + P], gv[:, cp, hd * 256 + vc * P:hd * 256 + vc * P + P], gat[cp % 2][:, hd, :],
                           start=hd % 2 == 0 and vc == 0, stop=False, skip_group_check=True)
                for c2 in range(2):
                    c = 2 * cp + c2
                    if c:
                        wait("g_s", c)
                        for hd in range(4):
                            for vc in range(2):
                                a_ = (2 * (hd % 2) + vc) * P + 64 * c2
                                last = mm(ob[hd // 2][:, a_:a_ + 64], gs[c % 2][:, hd, vc * P:vc * P + P],
                                          gq[:, hd, 64 * c:64 * c + 64], start=False, stop=c2 == 1, skip_group_check=True)
                    if c2:
                        last.then_inc(S["g_o"], 1)
                    if c < 7:
                        r = slice(64 * c2, 64 * c2 + 64)
                        for hd in range(4):
                            last = mm(X[2 + hd // 2][:, (hd % 2) * 256:(hd % 2) * 256 + 256], gkt[r, hd, :],
                                      gv[r, cp, hd * 256:hd * 256 + 256], start=True, stop=True)
                        last.then_inc(S["g_n"], 1)
                wait("g_sq", 2 * (cp + 1))
                for hd in range(4):
                    for vc in range(2):
                        a_ = (2 * (hd % 2) + vc) * P
                        last = mm(X[1][:, hd * P:hd * P + P], C("ones"), nt[hd // 2][:, a_:a_ + P], start=vc == 0, stop=vc == 1)
                last.then_inc(S["g_ss"], 1)
            wait("g_lo", 8)
            blocks(N_GOUT, 4, g_hi, g_lo_)

        def cs(c):
            return gs[c // 2][:].rearrange("p a n -> p (a n)")[:, (c % 2) * T:(c % 2) * T + T]

        def gla_act(act, hi):
            hi(N_GQK)
            hi(N_GQK + 1)
            for c in range(4):
                act.wait_ge(S["g_gk"], c + 1)
                nc.scalar.activation(cs(c), X[c][:], ACT.Abs, bias=V("a_b_gk_2", c)).then_inc(S["g_ab"], 1)
            for c in range(4):
                act.wait_ge(S["g_ab"], c + 1)
                nc.scalar.activation(cs(c), cs(c), ACT.Exp, scale=-1.0).then_inc(S["g_ab"], 1)
            for c in range(4):
                act.wait_ge(S["g_ab"], 4 + c + 1)
                nc.scalar.activation(cs(c), cs(c), ACT.Ln, bias=C("one")).then_inc(S["g_ln"], 1)
            hi(N_GQK + 2)
            hi(N_GQK + 3)
            hi(N_GV)
            for c in range(4):
                act.wait_ge(S["g_cs"], c + 1)
                if c:
                    act.wait_ge(S["g_sc"], 6 * c)
                nc.scalar.activation(nt[0][:], cs(c), ACT.Exp, scale=1 / 16).then_inc(S["g_act"], 1)
                nc.scalar.activation(gb[:, c, :], cs(c), ACT.Exp, scale=-1 / 16).then_inc(S["g_act"], 1)
                nc.scalar.activation(g_el[:, 8 * c:8 * c + 8], cs(c).rearrange("p (c t) -> p c t", t=64)[:, :, 63],
                                     ACT.Exp, scale=1 / 16).then_inc(S["g_act"], 1)
                act.wait_ge(S["g_dve"], c + 1)
                nc.scalar.activation(nt[1][:], nt[2][:], ACT.Exp, scale=1 / 16).then_inc(S["g_act"], 1)
            for b in range(4):
                hi(N_GV + b + 1)
            for b in range(4):
                hi(N_GG + b + 1)
                for c in range(2):
                    k = 2 * b + c
                    act.wait_ge(S["acc_evac"], acc_before(N_GG) + k + 1)
                    if k >= 2:
                        act.wait_ge(S["g_gate"], k - 1)
                    nc.scalar.activation(nt[c][:], gg[:, k, :], ACT.Sigmoid).then_inc(S["g_act"], 1)
            nc.scalar.preload_act_table_set("natural_log_exp_and_others")
            for cp in range(4):
                act.wait_ge(S["g_kt"], 2 * cp + 2)
                nc.scalar.activation(gkt[:].rearrange("p a n -> p (a n)"), X[1][:], ACT.Copy).then_inc(S["g_ktev"], 1)
                act.wait_ge(S["g_o"], cp + 1)
                if cp:
                    act.wait_ge(S["g_ss"], cp)
                else:
                    act.wait_ge(S["g_gate"], KT)
                for i in range(2):
                    nc.scalar.activation(nt[i][:], M[2 * (cp % 2) + i][:], ACT.Square).then_inc(S["g_sq"], 1)
                act.wait_ge(S["g_ss"], cp + 1)
                if cp:
                    act.wait_ge(S["g_oev"], 4 * cp)
                nc.scalar.activation(rstd[:], X[1][:], ACT.Ln, scale=1.0 / 256, bias=C("eps6")).then_inc(S["g_rl"], 1)
                act.wait_ge(S["g_rl"], cp + 1)
                nc.scalar.activation(rstd[:], rstd[:], ACT.Exp, scale=-0.5).then_inc(S["g_rstd"], 1)
                for i in range(2):
                    act.wait_ge(S["g_oev"], 4 * cp + 3 + i)
                    tok = slice(cp * P, cp * P + P)
                    nc.scalar.activation(g_hi[:, 4 * i:4 * i + 4, tok], gg[:, 4 * i:4 * i + 4, tok], ACT.Copy).then_inc(S["g_hi"], 1)

        def gla_dve(dve, lo, evac, evac_tm, resid):
            TTO, TS, STT = nc.vector.tensor_tensor, nc.vector.tensor_scalar, nc.vector.scalar_tensor_tensor
            for i in range(2):
                nc.vector.memset(gat[i][:], 0.0).then_inc(S["g_zero"], 1)
            lo(N_GQK)
            dve.wait_ge(S["acc_done"], 2 * N_GLR + 2)
            dve.wait_ge(S["norm_rstd"], 5)
            TTO(glr[:], M[acc_before(N_GLR) % 4][0:GLR, :], rstd[0:GLR, :], ALU.mult).then_inc(S["acc_evac"], 2)

            def qk(b):
                lo(N_GQK + b + 1)
                for c in range(2):
                    j = 2 * b + c
                    evac(N_GQK + b, c, (gq if j < 4 else gk)[:, j % 4, :])

            qk(0)
            for c in range(4):
                dve.wait_ge(S["g_ab"], c + 1)
                TS(gb[:, c, :], X[c][:], V("a_b_gk_2", c), 0.0, ALU.add, ALU.min).then_inc(S["g_o1"], 1)
            for c in range(4):
                dve.wait_ge(S["g_ln"], c + 1)
                dve.wait_ge(S["g_o1"], c + 1)
                TTO(gb[:, c, :], gb[:, c, :], cs(c), ALU.subtract).then_inc(S["g_o1"], 1)
            for c in range(4):
                dve.wait_ge(S["g_o1"], 4 + c + 1)
                nc.vector.tensor_tensor_scan(cs(c), seg, gb[:, c, :], 0.0, ALU.mult, ALU.add).then_inc(S["g_cs"], 1)
            qk(1)
            qk(2)
            qk(3)
            for c in range(4):
                dve.wait_ge(S["g_cs"], c + 1)
                c8 = cs(c).rearrange("p (c t) -> p c t", t=64)
                TTO(nt[2][:].rearrange("p (c t) -> p c t", t=64), c8[:, :, 63:64].to_broadcast([P, 8, 64]), c8,
                    ALU.subtract).then_inc(S["g_dve"], 1)
                dve.wait_ge(S["g_act"], 4 * c + 4)
                STT(gq[:, c, :], gq[:, c, :], float(P) ** -0.5, nt[0][:], ALU.mult, ALU.mult).then_inc(S["g_sc"], 2)
                TTO(gb[:, c, :], gk[:, c, :], gb[:, c, :], ALU.mult).then_inc(S["g_sc"], 2)
                TTO(gk[:, c, :], gk[:, c, :], nt[1][:], ALU.mult).then_inc(S["g_sc"], 2)
            for b in range(4):
                lo(N_GV + b + 1)
                for i in range(2):
                    evac_tm(N_GV + b, i, gv[:, 2 * i:2 * i + 2, b * BW:b * BW + BW], rcol[:, 2 * i:2 * i + 2])
            for b in range(4):
                lo(N_GG + b + 1)
                for c in range(2):
                    k = 2 * b + c
                    evac(N_GG + b, c, gg[:, k, :])
                    dve.wait_ge(S["g_act"], 16 + k + 1)
                    STT(gg[:, k, :], gg[:, k, :], V("a_onorm_2", c), nt[c][:], ALU.mult,
                        ALU.mult).then_inc(S["g_gate"], 1)
            for cp in range(4):
                dve.wait_ge(S["g_kt"], 2 * cp + 1)
                nc.vector.copy_predicated(gat[cp % 2][:], C("gla").bitcast(i32).unsqueeze(1).to_broadcast([P, 4, P]),
                                          X[0][:].rearrange("p (h n) -> p h n", h=4)).then_inc(S["g_at"], 1)
                for c2 in range(2):
                    c = 2 * cp + c2
                    if c < 7:
                        dve.wait_ge(S["g_n"], c + 1)
                        if c:
                            dve.wait_ge(S["g_s"], c)
                        for hd in range(4):
                            n_ = X[2 + hd // 2][:, (hd % 2) * 256:(hd % 2) * 256 + 256]
                            if c == 0:
                                last = nc.vector.tensor_copy(gs[1][:, hd, :], n_)
                            else:
                                last = STT(gs[(c + 1) % 2][:, hd, :], gs[c % 2][:, hd, :],
                                           g_el[:, 8 * hd + c:8 * hd + c + 1], n_, ALU.mult, ALU.add)
                        last.then_inc(S["g_s"], 1)
                tok = slice(cp * P, cp * P + P)
                dve.wait_ge(S["g_o"], cp + 1)
                for i in range(2):
                    dve.wait_ge(S["g_sq"], 2 * cp + i + 1)
                    g_ = gg[:, 4 * i:4 * i + 4, tok]
                    TTO(g_, M[2 * (cp % 2) + i][:].rearrange("p (c n) -> p c n", c=4), g_, ALU.mult).then_inc(S["g_oev"], 1)
                dve.wait_ge(S["g_rstd"], cp + 1)
                for i in range(2):
                    dve.wait_ge(S["g_oev"], 4 * cp + 1 + i)
                    g_ = gg[:, 4 * i:4 * i + 4, tok].rearrange("p (h v) n -> p h v n", h=2)
                    r_ = rstd[:, 2 * i * P:(2 * i + 2) * P].rearrange("p (h n) -> p h n", h=2).unsqueeze(2).to_broadcast([P, 2, 2, P])
                    TTO(g_, g_, r_, ALU.mult).then_inc(S["g_oev"], 1)
                for i in range(2):
                    dve.wait_ge(S["g_hi"], 2 * cp + i + 1)
                    TTO(g_lo_[:, 4 * i:4 * i + 4, tok], gg[:, 4 * i:4 * i + 4, tok],
                        g_hi[:, 4 * i:4 * i + 4, tok].bitcast(f32), ALU.subtract).then_inc(S["g_lo"], 1)
            resid(N_GOUT, 5, 4, "ln_mlp_2", 0, *mem_of[1][0:2])

        @block.sync
        def _(sp):
            def load(n, src, cols=BW, r=0):
                if n >= 4:
                    sp.wait_ge(S["w_lo_ready"], n - 3 + r)
                sp.dma_start(raw[:, n % 4, :, 0:cols], src).then_inc(w_arrived[n % 4], 16)

            def load_plain(first):
                _, count, w, col = next(x for x in plain if x[0] == first)
                cols = GLR if first == N_GLR else BW
                for j in range(count):
                    load(first + j, w[:, :, col + BW * j:col + BW * j + cols], cols)

            def load_mlp(n):
                up, down = mlps[n]
                with sp.Fori(0, 2) as half:
                    with sp.Fori(0, 2) as j:
                        for b in range(4):
                            load(n + b, up[:, :, ds(half * 2048 + j * 1024 + b * BW, BW)], r=half * 16 + j * 4)
                    with sp.Fori(0, 2) as q:
                        for b in range(4):
                            kg, cg = b // 2, b % 2
                            load(n + 8 + b, down[:, ds(half * 16 + kg * 8, 8), ds(q * 512 + cg * BW, BW)],
                                 r=half * 16 + q * 4)

            sp.dma_start(cst[:], A["consts"]).then_inc(S["ld_const"], 16)
            for g in range(4):
                sp.dma_start(xt[:, :, g * 256:g * 256 + 256],
                             A["x"][0].rearrange("(t p) n -> p t n", p=P)[:, :, g * 256:g * 256 + 256]).then_inc(S[f"ld_x{g}"], 16)
            for n in (N_DQ, N_DK, N_DV, N_RW):
                load_plain(n)
            for n in (N_WOUT, N_MK, N_MV, N_MQ, N_MO):
                load_plain(n)
            load_mlp(N_MLP1)
            for n in (N_GLR, N_GQK, N_GV, N_GG, N_GOUT):
                load_plain(n)
            load_mlp(N_MLP2)
            for n in (N_KV, N_WQ, N_SOUT):
                load_plain(n)
            load_mlp(N_MLP3)
            load(LAST, w_in[:, :, 0:BW])
            for t in range(TT):
                sp.wait_ge(S["fin_ev"], 2 * (t + 1))
                sp.dma_start(out[0].rearrange("(t p) n -> p t n", p=P)[:, t, :], ytm_view(t)).then_inc(S["st_out"], 16)
            sp.wait_ge(S["st_out"], 16 * TT)

        @block.gpsimd
        def _(pool):
            pool.dma_start(vrow[:, 0, :], A["vecs"][0:P]).then_inc(S["ld_vec"], 16)
            pool.dma_start(vrow[0:VEC_ROWS - P, 1, :], A["vecs"][P:VEC_ROWS]).then_inc(S["ld_vec"], 16)
            for i, name in enumerate(("lam_q1", "lam_q2")):
                pool.dma_start(lamv[i:i + 1, 0, :], A[name]).then_inc(S["ld_small"], 16)
            for i, name in enumerate(("lam_k1", "lam_k2")):
                pool.dma_start(lamv[i:i + 1, 1, :], A[name]).then_inc(S["ld_small"], 16)
            pool.dma_start(sinkb, A["b_sinks_2"].broadcast_to([P, 16])).then_inc(S["ld_small"], 16)
            pool.dma_start(lora[0:64, :], A["w_decay_up"][0]).then_inc(S["ld_lora"], 16)
            pool.dma_start(lora[64:128, :], A["a_up"][0]).then_inc(S["ld_lora"], 16)
            pool.dma_start(g_up[:], A["g_up"][0]).then_inc(S["ld_lora"], 16)
            pool.wait_ge(S["rw_ev"], len(RW_SEQ))
            pool.dma_start(mrow[:], A["mem"][0].rearrange("(t p) n -> p t n", p=P)).then_inc(S["ld_mem"], 16)
            pool.wait_ge(S["acc_evac"], acc_before(N_MQ))
            pool.dma_start(onehot[:], A["onehot"]).then_inc(S["ld_rel"], 16)
            pool.dma_start(relx[0:32, :], A["rel_table_2"]).then_inc(S["ld_rel"], 16)
            pool.dma_start(relx[32:33, :], A["consts"][0:1, CONST["ones"][0]:CONST["ones"][0] + 16]).then_inc(S["ld_rel"], 16)
            for hd in range(16):
                pool.wait_ge(S["bias_ev"], hd + 1)
                pool.dma_start(bias_rows[hd], biasrow[hd % 2][:]).then_inc(S["st_bias"], 16)
                pool.wait_ge(S["st_bias"], 16 * (hd + 1))
            pool.wait_ge(S["acc_evac"], acc_before(N_GLR))
            pool.dma_start(w_gk2[:], A["a_w_gk2_2"][0]).then_inc(S["ld_gk"], 16)
            pool.wait_ge(S["acc_evac"], acc_before(N_KV))
            pool.dma_start(bias[:], bias_skewed()).then_inc(S["ld_bias"], 16)

        @block.tensor
        def _(pe):
            mm = nc.tensor.matmul

            def wait(name, v):
                pe.wait_ge(S[name], v)

            def bank_free(k, r=None):
                if k >= 4:
                    pe.wait_ge(S["acc_evac"], k - 3 if r is None else k - 3 + r)
                return M[k % 4]

            def block_ready(n, r=None):
                pe.wait_ge(S["w_lo_ready"], n + 1 if r is None else n + 1 + r)

            def exact3(dst, wh, wl, xh, xl, start, stop):
                mm(dst, wh, xh, start=start, stop=False)
                mm(dst, wl, xh, start=False, stop=False)
                return mm(dst, wh, xl, start=False, stop=stop)

            def chunk(n, c, hi, lo, first=None, cols=P, tok=T, inc=1, lo_sem="x_lo"):
                if c == 0:
                    block_ready(n)
                k = acc_before(n) + c
                dst = bank_free(k)
                for kt in range(KT):
                    if first is not None:
                        wait(lo_sem, first + kt + 1)
                    ws = slice(c * P, c * P + cols)
                    last = exact3(dst[0:cols, 0:tok], w_hi[:, n % 2, kt, ws], w_lo[:, n % 2, kt, ws],
                                  hi[:, kt, 0:tok], lo[:, kt, 0:tok], kt == 0, kt == KT - 1)
                last.then_inc(S["acc_done"], inc)

            def blocks(n, count, hi, lo, first=None, tok=T, lo_sem="x_lo"):
                for b in range(count):
                    for c in range(2):
                        chunk(n + b, c, hi, lo, first if b == 0 and c == 0 else None, tok=tok, lo_sem=lo_sem)

            def block_tm(n, hi, lo, tiles, per, width=BW, at=0, base=None):
                block_ready(n)
                k = acc_before(n) if base is None else base
                for t in range(tiles):
                    if t % per == 0:
                        dst = bank_free(k + t // per)
                    for kt in range(KT):
                        ts_, cs = slice(t * P, t * P + P), slice(at, at + width)
                        o_ = dst[:, (t % per) * width:(t % per + 1) * width]
                        mm(o_, hi[:, kt, ts_], w_hi[:, n % 2, kt, cs], start=kt == 0, stop=False)
                        mm(o_, hi[:, kt, ts_], w_lo[:, n % 2, kt, cs], start=False, stop=False)
                        last = mm(o_, lo[:, kt, ts_], w_hi[:, n % 2, kt, cs], start=False, stop=kt == KT - 1)
                    if t % per == per - 1:
                        last.then_inc(S["acc_done"], 2 // (tiles // per) if base is None else 1)

            def norm_stat(i, cols=False, tok=T, acc=nt[2], add="norm_add", ss="norm_ss"):
                wait(add, 7 * (i + 1))
                last = mm(X[0][:, 0:tok], C("ones"), acc[:, 0:tok], start=True, stop=True)
                if cols:
                    for t in range(tok // P):
                        last = mm(X[1][:, t:t + 1], acc[:, t * P:t * P + P], C("one"), start=True, stop=True)
                last.then_inc(S[ss], 1)

            def mlp(n, first, nth):
                f_hi, f_lo, u_hi, u_lo = mem_of[nth]
                k = acc_before(n)
                with pe.Fori(0, 2) as half:
                    with pe.Fori(0, 2) as j:
                        for b in range(4):
                            block_ready(n + b, half * 16 + j * 4)
                            for c in range(2):
                                dst = bank_free(k + 2 * b + c, half * 24 + j * 8)
                                for kt in range(KT):
                                    if b == 0 and c == 0:
                                        wait("x_lo", first + kt + 1)
                                    ws = slice(c * P, c * P + P)
                                    last = exact3(dst[:], w_hi[:, (n + b) % 2, kt, ws], w_lo[:, (n + b) % 2, kt, ws],
                                                  f_hi[:, kt, :], f_lo[:, kt, :], kt == 0, kt == KT - 1)
                                last.then_inc(S["acc_done"], 1)
                    with pe.Fori(0, 2) as q:
                        for b in range(4):
                            kg = b // 2
                            m = n + 8 + b
                            block_ready(m, half * 16 + q * 4)
                            pe.wait_ge(S["up_lo"], 32 * nth + 8 * kg + 8 + half * 16)
                            for c in range(2):
                                kk = k + 16 + 2 * (b % 2) + c
                                dst = M[kk % 4] if kg else bank_free(kk, half * 24 + q * 4)
                                for kt in range(KT):
                                    ws = slice(c * P, c * P + P)
                                    last = exact3(dst[:], w_hi[:, m % 2, kt, ws], w_lo[:, m % 2, kt, ws],
                                                  u_hi[:, kg * 8 + kt, :], u_lo[:, kg * 8 + kt, :],
                                                  kg == 0 and kt == 0, kg == 1 and kt == KT - 1)
                                last.then_inc(S["acc_done"], 1)

            wait("ld_const", 16)
            for g in range(4):
                wait(f"ld_x{g}", 16)
                for c in (2 * g, 2 * g + 1):
                    if c >= 4:
                        wait("xt_ev", c - 3)
                    for t in range(TT):
                        last = nc.tensor.transpose(X[c % 4][:, t * P:t * P + P], xt[:, t, c * P:c * P + P], C("ident"))
                    last.then_inc(S["xt_tr"], 1)
                if g == 0:
                    wait("ld_vec", 32)
                    nc.tensor.transpose(M[0][:, 0:P], vrow[:, 0, :], C("ident"))
                    nc.tensor.transpose(M[0][:, P:VEC_ROWS], vrow[0:VEC_ROWS - P, 1, :],
                                        C("ident", slice(0, VEC_ROWS - P))[:, 0:VEC_ROWS - P]).then_inc(S["vec_tr"], 1)
            wait("xt_ev", KT)
            norm_stat(0, cols=True)

            blocks(N_DQ, 2, xm_hi, xm_lo, first=0)
            blocks(N_DK, 2, xm_hi, xm_lo)
            wait("lam_e", 1)
            mm(X[3][:, 0:1], C("plusminus", slice(0, 2)), lame, start=True, stop=True).then_inc(S["lam_mm"], 1)
            for b in range(2):
                block_tm(N_DV + b, xm_hi, xm_lo, TT, 2)
            wait("acc_evac", acc_before(N_RW))
            wait("lam_ready", 1)

            def diff_norm(hd):
                wait("da_sq", hd + 1)
                mm(X[2][:], C("ones"), de_sq[:], start=True, stop=True).then_inc(S["da_ss"], 1)

            for u in range(16):
                hd, qb = u // 4, u % 4
                nk = (qb + 1) * P
                if u:
                    wait("da_exp", 2 * u)
                for m in range(2):
                    r = slice(64 * m, 64 * m + 64)
                    last = mm(X[m][:, 0:nk], dq[r, hd, qb * P:qb * P + P], dk[r, hd, 0:nk], start=True, stop=True)
                last.then_inc(S["da_score"], 1)
                if u < 14:
                    chunk(N_RW + u // 2, u % 2, xm_hi, xm_lo)
                if qb == 0 and hd:
                    wait("da_at", u)
                    diff_norm(hd - 1)
                wait("da_attn", u + 1)
                if u:
                    wait("da_at", u)
                if qb == 0 and hd:
                    wait("da_ln", hd)
                for kb in range(qb + 1):
                    last = nc.tensor.transpose(X[2][:, kb * P:kb * P + P], de[1][:, kb * P:kb * P + P], C("ident"))
                last.then_inc(S["da_tr"], 1)
                wait("da_at", u + 1)
                if qb == 0 and hd:
                    wait("da_o", hd)
                for kb in range(qb + 1):
                    last = mm(X[3][:, qb * P:qb * P + P], dv[:, kb, hd * P:hd * P + P], da_t[:, kb, :],
                              start=kb == 0, stop=kb == qb)
                last.then_inc(S["da_pv"], 1)
            diff_norm(3)
            wait("da_y", 4)

            wait("rw_act", 2)
            rwkv_pe(pe, mm, wait)

            wait("y_lo", KT)
            blocks(N_WOUT, 1, y_hi, y_lo)
            wait("ld_mem", 16)
            for g in range(4):
                for i in range(2):
                    for t in range(2):
                        c = 2 * g + i
                        last = nc.tensor.transpose(X[g][:, i * MEM + t * P:i * MEM + t * P + P],
                                                   mrow[:, t, c * P:c * P + P], C("ident"))
                last.then_inc(S["mt_tr"], 1)
            blocks(N_WOUT + 1, 1, y_hi, y_lo)
            wait("mt_ev", 4)
            norm_stat(0, True, MEM, mnt[2], "mn_add", "mn_ss")
            blocks(N_WOUT + 2, 2, y_hi, y_lo)
            blocks(N_MK, 4, m_hi, m_lo, first=0, tok=MEM, lo_sem="mx_lo")
            for b in range(4):
                block_tm(N_MV + b, m_hi, m_lo, 2, 1)
            wait("mn_ln", 1)
            norm_stat(1)
            blocks(N_MQ, 4, x2_hi, x2_lo, first=8)
            wait("acc_evac", acc_before(N_MO))

            def mem_score(u):
                hd, qb = u // 4, u % 4
                if u >= 2:
                    wait("ma_exp", u - 1)
                for i in range(2):
                    last = mm(X[u % 2][:, 0:MEM], mq[:, 2 * hd + i, qb * P:qb * P + P], mk[:, 2 * hd + i, :],
                              start=i == 0, stop=i == 1)
                last.then_inc(S["ma_score"], 1)

            mem_score(0)
            for u in range(16):
                hd, qb = u // 4, u % 4
                if u < 15:
                    mem_score(u + 1)
                wait("ma_p", u + 1)
                if u:
                    wait("ma_pt", u)
                for t in range(2):
                    last = nc.tensor.transpose(X[2][:, t * P:t * P + P], me[u % 2][:, 0, t * P:t * P + P], C("ident"))
                last.then_inc(S["ma_tr"], 1)
                if u:
                    wait("bias_ev", u)
                else:
                    wait("ld_rel", 48)
                mm(X[3][:, 0:384], relx[:, u:u + 1].to_broadcast([33, P]), onehot[:], start=True,
                   stop=True).then_inc(S["bias_mm"], 1)
                wait("ma_pt", u + 1)
                if qb == 0 and hd >= 2:
                    wait("ma_lo", 2 * (hd - 1))
                for i in range(2):
                    for t in range(2):
                        f = (2 * hd + i) * P
                        last = mm(M[2 * (hd % 2) + i][:, qb * P:qb * P + P], mv[:, t, f:f + P],
                                  mpt[u % 2][:, t, :], start=t == 0, stop=t == 1)
                last.then_inc(S["ma_pv"], 1)
            wait("ma_lo", KT)
            blocks(N_MO, 4, o_hi, o_lo)

            norm_stat(2)
            mlp(N_MLP1, 16, 0)
            norm_stat(3)

            norm_stat(4, cols=True)
            gla_pe(pe, mm, wait, chunk, blocks, block_tm)
            norm_stat(5)
            mlp(N_MLP2, 32, 1)

            norm_stat(6, cols=True)
            chunk(N_KV, 0, kx_hi, kx_lo, first=40)
            block_tm(N_KV, kx_hi, kx_lo, TT, TT, width=P, at=P, base=acc_before(N_KV) + 1)
            wait("acc_evac", acc_before(N_KV) + 2)
            for i in range(2):
                mm(X[1 + i][:], C(f"sel{i}"), kf[:], start=True, stop=True).then_inc(S["sw_dup"], 1)
            blocks(N_WQ, 4, sx_hi, sx_lo, first=48)
            wait("acc_evac", acc_before(N_SOUT))
            wait("sw_dupev", 2)

            def sw_score(u):
                c, qb = u // 4, u % 4
                if u >= 2:
                    wait("sw_s", u - 1)
                lo_ = max(qb - 1, 0) * P
                n = (qb + 1) * P - lo_
                for i in range(2):
                    r = slice(64 * i, 64 * i + 64)
                    last = mm(sw_banks(u)[:, i, 256 - n:256], sq[r, c, qb * P:qb * P + P],
                              kd[c // 4][r, lo_:lo_ + n], start=True, stop=True)
                last.then_inc(S["sw_score"], 1)

            sw_score(0)
            for u in range(32):
                c, qb = u // 4, u % 4
                if u < 31:
                    sw_score(u + 1)
                wait("sw_p", u + 1)
                if u:
                    wait("sw_pt", u)
                kbs = (0, 1) if qb else (1,)
                for i in range(2):
                    for kb in kbs:
                        last = nc.tensor.transpose(X[2][:, (2 * i + kb) * P:(2 * i + kb + 1) * P],
                                                   sc[u % 2][:, i, kb * P:kb * P + P], C("ident"))
                last.then_inc(S["sw_tr"], 1)
                wait("sw_pt", u + 1)
                if qb == 0 and c >= 2:
                    wait("sw_lo", c - 1)
                for i in range(2):
                    for kb in kbs:
                        last = mm(M[c % 2][64 * i:64 * i + 64, qb * P:qb * P + P],
                                  sv[:, qb - 1 + kb, (c // 4) * 64:(c // 4) * 64 + 64],
                                  spt[u % 2][:, 2 * i + kb, :], start=kb == kbs[0], stop=kb == 1)
                last.then_inc(S["sw_pv"], 1)
            wait("sw_lo", KT)
            blocks(N_SOUT, 4, s_hi, s_lo)
            norm_stat(7)
            mlp(N_MLP3, 56, 2)
            norm_stat(8)

            wait("acc_evac", acc_before(LAST))
            wait("h_final", HF)
            for t in range(TT):
                for half in range(2):
                    i = 2 * t + half
                    if i >= 2:
                        wait("fin_ev", i - 1)
                    for c in range(4):
                        last = nc.tensor.transpose(X[2 + i % 2][:, c * P:c * P + P], h[:, 4 * half + c, t * P:t * P + P],
                                                   C("ident"))
                    last.then_inc(S["fin_tr"], 1)

        @block.scalar
        def _(act):
            def hi(n, r=None):
                if n >= 2:
                    act.wait_ge(S["acc_done"], 2 * (n - 1) if r is None else 2 * (n - 1) + 2 * r)
                act.wait_ge(w_arrived[n % 4], 16 * (n // 4 + 1) if r is None else 16 * (n // 4 + 1) + 4 * r)
                cols = GLR if n == N_GLR else BW
                nc.scalar.activation(w_hi[:, n % 2, :, 0:cols], raw[:, n % 4, :, 0:cols], ACT.Copy).then_inc(S["w_hi_ready"], 1)

            def norm_chunk(i, c, src, ready=None, x=None, tok=T, sem=("norm_sq", "norm_add", "x_hi")):
                if ready is not None:
                    act.wait_ge(S[ready[0]], ready[1])
                if c >= 2:
                    act.wait_ge(S[sem[1]], 7 * i + max(1, c - 2))
                b_ = (nt if tok == T else mnt)[c % 2]
                nc.scalar.activation(b_[:, 0:tok], src, ACT.Square).then_inc(S[sem[0]], 1)
                if x is not None:
                    nc.scalar.activation(x[1][:, c, :], src, ACT.Copy, scale=x[0]).then_inc(S[sem[2]], 1)

            def norm_rsqrt(i, eps, cols=0, tok=T, rs=rstd, rc=rcol, sem=("norm_ss", "norm_ln", "norm_rstd")):
                act.wait_ge(S[sem[0]], i + 1)
                if cols:
                    nc.scalar.activation(rc[:, 0:cols], X[1][:, 0:cols], ACT.Ln, scale=1.0 / D, bias=C(eps))
                nc.scalar.activation(rs[:, 0:tok], X[0][:, 0:tok], ACT.Ln, scale=1.0 / D, bias=C(eps)).then_inc(S[sem[1]], 1)
                act.wait_ge(S[sem[1]], i + 1)
                if cols:
                    nc.scalar.activation(rc[:, 0:cols], rc[:, 0:cols], ACT.Exp, scale=-0.5)
                nc.scalar.activation(rs[:, 0:tok], rs[:, 0:tok], ACT.Exp, scale=-0.5).then_inc(S[sem[2]], 1)

            def resid_norm(n, i, x=None):
                for b in range(4):
                    hi(n + b + 1)
                    for c in range(2):
                        c_ = 2 * b + c
                        norm_chunk(i, c_, h[:, c_, :], ("acc_evac", acc_before(n) + c_ + 1), x and (V(x[0], x[1] + c_), x[2]))

            def mlp(n, nth, i_, x=None):
                u_hi = mem_of[nth][2]
                k = acc_before(n)
                for half in range(2):
                    with act.Fori(0, 2) as j:
                        for b in range(4):
                            hi(n + b + 1, half * 16 + j * 4)
                            for c in range(2):
                                i = 2 * b + c
                                act.wait_ge(S["acc_evac"], k + i + 1 + half * 24 + j * 8)
                                nc.scalar.activation(us[c][:], ut[c][:], ACT.Square).then_inc(S["up_sq"], 1)
                                act.wait_ge(S["up_sq"], 32 * nth + i + 1 + half * 16 + j * 8)
                                nc.scalar.activation(u_hi[:, ds(j * 8 + i, 1), :], us[c][:].unsqueeze(1), ACT.Copy).then_inc(S["up_hi"], 1)
                    if half == 0:
                        with act.Fori(0, 2) as q:
                            for b in range(4):
                                hi(n + 9 + b, q * 4)
                for q in range(2):
                    for b in range(4):
                        if n + 25 + 4 * q + b < N_END:
                            hi(n + 25 + 4 * q + b)
                        if b >= 2:
                            for c in range(2):
                                c_ = 4 * q + 2 * (b % 2) + c
                                norm_chunk(i_, c_, h[:, c_, :], ("acc_evac", k + 40 + c_ + 1), x and (V(x[0], x[1] + c_), x[2]))

            nc.scalar.preload_act_table_set("natural_log_exp_and_others")
            act.wait_ge(S["lam_mul"], 3)
            nc.scalar.activation(lame, lamd, ACT.Exp).then_inc(S["lam_e"], 1)
            for c in range(KT):
                norm_chunk(0, c, h[:, c, :], ("xt_ev", c + 1), (V("norm_mix_w", c), xm_hi))
            hi(0)
            norm_rsqrt(0, "eps5", cols=TT)
            for n in range(N_RW):
                hi(n + 1)
            for u in range(16):
                hd, qb = u // 4, u % 4
                nk = (qb + 1) * P
                act.wait_ge(S["da_neg"], u + 1)
                for m in range(2):
                    nc.scalar.activation(de[m][:, 0:nk], X[m][:, 0:nk], ACT.Exp, bias=da_ng[:, m:m + 1], scale=0.125,
                                         accum_out=da_z[:, m:m + 1]).then_inc(S["da_exp"], 1)
                if u % 2 == 0 and u < 14:
                    hi(N_RW + u // 2 + 1)
                if qb == 0 and hd:
                    act.wait_ge(S["da_ss"], hd)
                    nc.scalar.activation(da_rs[:], X[2][:], ACT.Ln, scale=1.0 / P, bias=C("eps5")).then_inc(S["da_ln"], 1)
                    act.wait_ge(S["da_ln"], hd)
                    nc.scalar.activation(da_rs[:], da_rs[:], ACT.Exp, scale=-0.5).then_inc(S["da_rstd"], 1)
                act.wait_ge(S["da_tr"], u + 1)
                nc.scalar.activation(da_t[:, 0:qb + 1, :], X[2][:, 0:nk].rearrange("p (k n) -> p k n", n=P), ACT.Copy).then_inc(S["da_at"], 1)
                if qb == 3:
                    act.wait_ge(S["da_o"], hd + 1)
                    if hd:
                        act.wait_ge(S["da_ss"], hd)
                    nc.scalar.activation(de_sq[:], da_out[:], ACT.Square).then_inc(S["da_sq"], 1)
            act.wait_ge(S["da_ss"], 4)
            nc.scalar.activation(da_rs[:], X[2][:], ACT.Ln, scale=1.0 / P, bias=C("eps5")).then_inc(S["da_ln"], 1)
            act.wait_ge(S["da_ln"], 4)
            nc.scalar.activation(da_rs[:], da_rs[:], ACT.Exp, scale=-0.5).then_inc(S["da_rstd"], 1)
            act.wait_ge(S["rw_p"], 14)
            nc.scalar.activation(p_rw[0:64, 12, 1:T + 1], p_rw[0:64, 12, 1:T + 1], ACT.Tanh).then_inc(S["rw_act"], 1)
            nc.scalar.activation(p_rw[:, 13, 1:T + 1], p_rw[:, 13, 1:T + 1], ACT.Sigmoid).then_inc(S["rw_act"], 1)
            rwkv_act(act)
            for c in range(KT):
                act.wait_ge(S["rw_ev"], ev("gate", min(c, 3)))
                nc.scalar.activation(y_hi[:, c, :], rkv(0, c) if c < 4 else y_diff[:, c - 4, :], ACT.Copy).then_inc(S["y_hi"], 1)
            def out_chunk(c):
                norm_chunk(1, c, h[:, c, :], ("acc_evac", acc_before(N_WOUT) + c + 1), (V("norm_mem_w", c), x2_hi))

            hi(N_WOUT + 1)
            out_chunk(0)
            out_chunk(1)
            for c in range(KT):
                norm_chunk(0, c, memT[:, c, :], ("mt_ev", c // 2 + 1), (V("norm_src_w", c), m_hi), MEM,
                           ("mn_sq", "mn_add", "mx_hi"))
            hi(N_WOUT + 2)
            out_chunk(2)
            out_chunk(3)
            norm_rsqrt(0, "eps5", 2, MEM, rstdm, rcolm, ("mn_ss", "mn_ln", "mn_rstd"))
            hi(N_WOUT + 3)
            out_chunk(4)
            out_chunk(5)
            hi(N_MK)
            out_chunk(6)
            out_chunk(7)
            for n in range(N_MK, N_MQ):
                hi(n + 1)
            norm_rsqrt(1, "eps5")
            for n in range(N_MQ, N_MO):
                hi(n + 1)
            for u in range(16):
                hd, qb = u // 4, u % 4
                act.wait_ge(S["ma_neg"], u + 1)
                if u >= 2:
                    act.wait_ge(S["ma_tr"], u - 1)
                nc.scalar.activation(me[u % 2][:, 0, :], X[u % 2][:, 0:MEM], ACT.Exp, bias=ma_ng, scale=1.0 / 16,
                                     accum_out=ma_z).then_inc(S["ma_exp"], 1)
                act.wait_ge(S["bias_mm"], u + 1)
                if u >= 2:
                    act.wait_ge(S["st_bias"], 16 * (u - 1))
                nc.scalar.activation(biasrow[u % 2][:], X[3][:, 0:384], ACT.Copy).then_inc(S["bias_ev"], 1)
                act.wait_ge(S["ma_tr"], u + 1)
                nc.scalar.activation(nt[u % 2][:, 0:MEM], X[2][:, 0:MEM], ACT.Copy).then_inc(S["ma_pt"], 1)
                if qb == 3:
                    act.wait_ge(S["ma_pv"], u + 1)
                    for i in range(2):
                        nc.scalar.activation(o_hi[:, 2 * hd + i, :], M[2 * (hd % 2) + i][:], ACT.Copy).then_inc(S["ma_hi"], 1)
            resid_norm(N_MO, 2, ("norm_mlp_w", 0, mem_of[0][0]))
            norm_rsqrt(2, "eps5")
            mlp(N_MLP1, 0, 3)
            norm_rsqrt(3, "eps5")
            for c in range(KT):
                norm_chunk(4, c, h[:, c, :], ("h_final", c + 1), (V("ln_mix_2", c), g_hi))
            norm_rsqrt(4, "eps6", cols=TT)
            gla_act(act, hi)
            resid_norm(N_GOUT, 5, ("ln_mlp_2", 0, mem_of[1][0]))
            norm_rsqrt(5, "eps6")
            mlp(N_MLP2, 1, 6, ("kv_norm_2", 0, kx_hi))
            for c in range(KT):
                nc.scalar.activation(sx_hi[:, c, :], h[:, c, :], ACT.Copy, scale=V("ln_mix_2", 8 + c)).then_inc(S["x_hi"], 1)
            norm_rsqrt(6, "eps6", cols=TT)
            hi(N_WQ)
            for n in range(N_WQ, N_SOUT):
                hi(n + 1)
            for u in range(32):
                c, qb = u // 4, u % 4
                off = 0 if qb else P
                act.wait_ge(S["sw_neg"], u + 1)
                for i in range(2):
                    nc.scalar.activation(sc[u % 2][:, i, off:256], sc[u % 2][:, i, off:256], ACT.Exp, bias=sw_ng_[:, i:i + 1],
                                         accum_out=sw_z_[:, i:i + 1]).then_inc(S["sw_e"], 1)
                act.wait_ge(S["sw_es"], u + 1)
                nc.scalar.activation(sw_es_, sw_es_, ACT.Exp).then_inc(S["sw_e"], 1)
                act.wait_ge(S["sw_tr"], u + 1)
                o4 = slice(0 if qb else 1, 2)
                nc.scalar.activation(spt[u % 2][:].rearrange("p (i k) n -> p i k n", i=2)[:, :, o4, :],
                                     X[2][:].rearrange("p (i k n) -> p i k n", i=2, k=2)[:, :, o4, :], ACT.Copy).then_inc(S["sw_pt"], 1)
                if qb == 3:
                    act.wait_ge(S["sw_pv"], u + 1)
                    nc.scalar.activation(s_hi[:, c, :], M[c % 2][:], ACT.Copy).then_inc(S["sw_hi"], 1)
            resid_norm(N_SOUT, 7, ("ln_mlp_2", 8, mem_of[2][0]))
            norm_rsqrt(7, "eps6")
            mlp(N_MLP3, 2, 8)
            norm_rsqrt(8, "eps6")

        @block.vector
        def _(dve):
            TTO, TS, STT = nc.vector.tensor_tensor, nc.vector.tensor_scalar, nc.vector.scalar_tensor_tensor

            def lo(n, r=None):
                dve.wait_ge(S["w_hi_ready"], n + 1 if r is None else n + 1 + r)
                cols = GLR if n == N_GLR else BW
                TTO(w_lo[:, n % 2, :, 0:cols], raw[:, n % 4, :, 0:cols], w_hi[:, n % 2, :, 0:cols].bitcast(f32),
                    ALU.subtract).then_inc(S["w_lo_ready"], 1)

            def evac_copy(n, c, dst, two=False):
                dve.wait_ge(S["acc_done"], 2 * n + c + 1)
                src = M[(acc_before(n) + c) % 4][:]
                nc.vector.tensor_copy(dst, src.rearrange("p (t n) -> p t n", t=2) if two else src).then_inc(S["acc_evac"], 1)

            def evac(n, c, dst):
                dve.wait_ge(S["acc_done"], 2 * n + c + 1)
                TTO(dst, M[(acc_before(n) + c) % 4], rstd[:], ALU.mult).then_inc(S["acc_evac"], 1)

            def evac_tm(n, c, dst, rc):
                _, t_, f_ = dst.shape
                dve.wait_ge(S["acc_done"], 2 * n + c + 1)
                src = M[(acc_before(n) + c) % 4][:, 0:t_ * f_].rearrange("p (t n) -> p t n", t=t_)
                TTO(dst, src, rc.unsqueeze(2).to_broadcast([P, t_, f_]), ALU.mult).then_inc(S["acc_evac"], 1)

            def resid_chunk(n, b, c):
                i = 2 * b + c
                dve.wait_ge(S["acc_done"], 2 * n + i + 1)
                TTO(h[:, i, :], h[:, i, :], M[(acc_before(n) + i) % 4], ALU.add).then_inc(S["acc_evac"], 1)

            def norm_step(i, c, j, src, w, lo_, hi_, tok=T, sem=("norm_sq", "norm_add", "x_hi", "x_lo")):
                b_ = nt if tok == T else mnt
                if c:
                    dve.wait_ge(S[sem[0]], 8 * i + c + 1)
                    if c > 1:
                        dve.wait_ge(S[sem[1]], 7 * i + c - 1)
                    TTO(b_[2][:, 0:tok], (b_[0] if c == 1 else b_[2])[:, 0:tok], b_[c % 2][:, 0:tok],
                        ALU.add).then_inc(S[sem[1]], 1)
                if w is not None:
                    dve.wait_ge(S[sem[2]], 8 * j + c + 1)
                    STT(lo_[:, c, :], src, w, hi_[:, c, :].bitcast(f32), ALU.mult, ALU.subtract).then_inc(S[sem[3]], 1)

            def resid(n, i, j, wname, woff, hi_, lo_):
                dve.wait_ge(S["acc_evac"], acc_before(n))
                for b in range(4):
                    lo(n + b + 1)
                    for c in range(2):
                        resid_chunk(n, b, c)
                        if 2 * b + c:
                            c_ = 2 * b + c - 1
                            norm_step(i, c_, j, h[:, c_, :], V(wname, woff + c_), lo_, hi_)
                norm_step(i, 7, j, h[:, 7, :], V(wname, woff + 7), lo_, hi_)

            def norm_final(i, wname, i2=None, j2=None, w2=None, hi_=None, lo_=None):
                dve.wait_ge(S["norm_rstd"], i + 1)
                for c in range(KT):
                    STT(h[:, c, :], h[:, c, :], V(wname, c), rstd[:], ALU.mult, ALU.mult).then_inc(S["h_final"], 1)
                    if c and w2:
                        norm_step(i2, c - 1, j2, h[:, c - 1, :], V(w2, c - 1), lo_, hi_)
                if w2:
                    norm_step(i2, 7, j2, h[:, 7, :], V(w2, 7), lo_, hi_)

            def mlp(n, nth, i_, j_, wname=None, woff=0, hi_=None, lo_=None):
                u_hi, u_lo = mem_of[nth][2:4]
                k = acc_before(n)
                for half in range(2):
                    with dve.Fori(0, 2) as j:
                        for b in range(4):
                            lo(n + b + 1, half * 16 + j * 4)
                            for c in range(2):
                                i = 2 * b + c
                                dve.wait_ge(S["acc_done"], 2 * n + i + 1 + half * 32 + j * 8)
                                STT(ut[c][:], M[(k + i) % 4], 0.0, rstd[:], ALU.max, ALU.mult).then_inc(S["acc_evac"], 1)
                                dve.wait_ge(S["up_hi"], 32 * nth + i + 1 + half * 16 + j * 8)
                                u_ = ds(j * 8 + i, 1)
                                TTO(u_lo[:, u_, :], us[c][:].unsqueeze(1), u_hi[:, u_, :].bitcast(f32),
                                    ALU.subtract).then_inc(S["up_lo"], 1)
                    if half == 0:
                        with dve.Fori(0, 2) as q:
                            for b in range(4):
                                lo(n + 9 + b, q * 4)
                                if b >= 2:
                                    for c in range(2):
                                        i = 2 * (b % 2) + c
                                        dve.wait_ge(S["acc_done"], 2 * (n + 8 + b) + c + 1 + q * 8)
                                        dve.wait_ge(S["acc_evac"], k + 16 + i + q * 4)
                                        h_ = h[:, ds(q * 4 + i, 1), :]
                                        TTO(h_, h_, M[(k + i) % 4].unsqueeze(1), ALU.add).then_inc(S["acc_evac"], 1)
                for q in range(2):
                    for b in range(4):
                        if n + 25 + 4 * q + b < N_END:
                            lo(n + 25 + 4 * q + b)
                        if b >= 2:
                            for c in range(2):
                                i = 4 * q + 2 * (b % 2) + c
                                dve.wait_ge(S["acc_done"], 2 * (n + 24 + 4 * q + b) + c + 1)
                                TTO(h[:, i, :], h[:, i, :], M[(k + i) % 4], ALU.add).then_inc(S["acc_evac"], 1)
                                if i:
                                    norm_step(i_, i - 1, j_, h[:, i - 1, :], wname and V(wname, woff + i - 1), lo_, hi_)
                norm_step(i_, 7, j_, h[:, 7, :], wname and V(wname, woff + 7), lo_, hi_)

            nc.vector.memset(p_rw[:, :, 0:1], 0.0).then_inc(S["rw_zero"], 1)
            dve.wait_ge(S["vec_tr"], 1)
            nc.vector.tensor_copy(vec[:], M[0][:, 0:VEC_ROWS]).then_inc(S["vec_ready"], 1)
            dve.wait_ge(S["ld_small"], 16 * 5)
            TTO(lamv[:, 0, :], lamv[:, 0, :], lamv[:, 1, :], ALU.mult).then_inc(S["lam_mul"], 1)
            dve.wait_ge(S["lam_mul"], 1)
            nc.vector.reduce_sum(lamd, lamv[:, 0, :], AX.X).then_inc(S["lam_mul"], 2)
            dve.wait_ge(S["vec_ready"], 1)
            nc.vector.tensor_scalar(sub_w, V("subln_w", 0), 1.0 - LAM_INIT, None, ALU.mult).then_inc(S["vec_ready"], 1)
            for c in range(KT):
                dve.wait_ge(S["xt_tr"], c + 1)
                nc.vector.tensor_copy(h[:, c, :], X[c % 4]).then_inc(S["xt_ev"], 1)
                if c:
                    norm_step(0, c - 1, 0, h[:, c - 1, :], V("norm_mix_w", c - 1), xm_lo, xm_hi)
            norm_step(0, 7, 0, h[:, 7, :], V("norm_mix_w", 7), xm_lo, xm_hi)
            lo(0)
            dve.wait_ge(S["norm_rstd"], 1)
            for b in range(4):
                lo(b + 1)
                for c in range(2):
                    i = 2 * b + c
                    evac(b, c, (dq if i < 4 else dk)[:, i % 4, :])
            dve.wait_ge(S["lam_mm"], 1)
            TS(lamneg, X[3][:, 0:1], -1.0, -LAM_INIT, ALU.mult, ALU.add).then_inc(S["lam_ready"], 1)
            for b in range(2):
                lo(N_DV + b + 1)
                for i in range(2):
                    evac_tm(N_DV + b, i, dv[:, 2 * i:2 * i + 2, b * BW:b * BW + BW], rcol[:, 2 * i:2 * i + 2])
            def diff_y(hd):
                dve.wait_ge(S["da_rstd"], hd + 1)
                STT(y_diff[:, hd, :], da_out[:], sub_w, da_rs[:], ALU.mult, ALU.mult).then_inc(S["da_y"], 1)

            for u in range(16):
                hd, qb = u // 4, u % 4
                nk = (qb + 1) * P
                dve.wait_ge(S["da_score"], u + 1)
                for m in range(2):
                    nc.vector.memset(X[m][0:64, nk - 64:nk], NEG).then_inc(S["da_fill"], 1)
                dve.wait_ge(S["da_fill"], 2 * u + 2)
                for m in range(2):
                    nc.vector.reduce_max(da_mx[:, m:m + 1], X[m][:, 0:nk], AX.X).then_inc(S["da_max"], 1)
                dve.wait_ge(S["da_max"], 2 * u + 2)
                TS(da_ng, da_mx, -0.125, None, ALU.mult).then_inc(S["da_neg"], 1)
                dve.wait_ge(S["da_exp"], 2 * u + 2)
                nc.vector.reciprocal(da_r, da_z).then_inc(S["da_rz"], 1)
                dve.wait_ge(S["da_rz"], u + 1)
                TS(da_c[:, 0:1], da_r[:, 1:2], lamneg, None, ALU.mult).then_inc(S["da_c2"], 1)
                TS(de[0][:, 0:nk], de[0][:, 0:nk], da_r[:, 0:1], None, ALU.mult).then_inc(S["da_c2"], 1)
                dve.wait_ge(S["da_c2"], 2 * u + 2)
                STT(de[1][:, 0:nk], de[1][:, 0:nk], da_c[:, 0:1], de[0][:, 0:nk], ALU.mult, ALU.add).then_inc(S["da_attn"], 1)
                if u < 14:
                    n, c = N_RW + u // 2, u % 2
                    if c == 0:
                        lo(n + 1)
                    evac(n, c, p_rw[:, 2 * (n - N_RW) + c, 1:T + 1])
                if qb == 0 and hd:
                    diff_y(hd - 1)
                if qb == 3:
                    dve.wait_ge(S["da_pv"], u + 1)
                    nc.vector.tensor_copy(da_out[:], X[3][:]).then_inc(S["da_o"], 1)
            diff_y(3)
            for c in range(14):
                if c == 0:
                    dve.wait_ge(S["acc_evac"], acc_before(N_WOUT))
                    dve.wait_ge(S["da_y"], 4)
                if c >= 2:
                    dve.wait_ge(S["rw_p"], c - 1)
                TTO(nt[c % 2][:], p_rw[:, c, 0:T], p_rw[:, c, 1:T + 1], ALU.subtract).then_inc(S["rw_shift"], 1)
                dve.wait_ge(S["rw_shift"], c + 1)
                STT(p_rw[:, c, 1:T + 1], nt[c % 2][:], V("mu_shift", c), p_rw[:, c, 1:T + 1], ALU.mult,
                    ALU.add).then_inc(S["rw_p"], 1)
            rwkv_dve(dve)
            for c in range(KT):
                dve.wait_ge(S["y_hi"], c + 1)
                TTO(y_lo[:, c, :], rkv(0, c) if c < 4 else y_diff[:, c - 4, :], y_hi[:, c, :].bitcast(f32),
                    ALU.subtract).then_inc(S["y_lo"], 1)
            def out_step(c):
                norm_step(1, c, 1, h[:, c, :], V("norm_mem_w", c), x2_lo, x2_hi)

            lo(N_WOUT + 1)
            resid_chunk(N_WOUT, 0, 0)
            resid_chunk(N_WOUT, 0, 1)
            out_step(0)
            out_step(1)
            for c in range(KT):
                if c % 2 == 0:
                    dve.wait_ge(S["mt_tr"], c // 2 + 1)
                    nc.vector.tensor_copy(memT[:, c:c + 2, :], X[c // 2].rearrange("p (a n) -> p a n", a=2)).then_inc(S["mt_ev"], 1)
                norm_step(0, c, 0, memT[:, c, :], V("norm_src_w", c), m_lo, m_hi, MEM, ("mn_sq", "mn_add", "mx_hi", "mx_lo"))
            for b in range(1, 4):
                lo(N_WOUT + b + 1)
                for c in range(2):
                    resid_chunk(N_WOUT, b, c)
                    if b > 1 or c:
                        out_step(2 * b + c - 1)
            out_step(7)
            dve.wait_ge(S["mn_rstd"], 1)
            for b in range(4):
                lo(N_MK + b + 1)
                for c in range(2):
                    dve.wait_ge(S["acc_done"], 2 * (N_MK + b) + c + 1)
                    TTO(mk[:, 2 * b + c, :], M[(acc_before(N_MK + b) + c) % 4][:, 0:MEM], rstdm[:], ALU.mult).then_inc(S["acc_evac"], 1)
            for b in range(4):
                lo(N_MV + b + 1)
                for t in range(2):
                    evac_tm(N_MV + b, t, mv[:, t:t + 1, b * BW:b * BW + BW], rcolm[:, t:t + 1])
            dve.wait_ge(S["norm_rstd"], 2)
            for b in range(4):
                lo(N_MQ + b + 1)
                for c in range(2):
                    evac(N_MQ + b, c, mq[:, 2 * b + c, :])
            for u in range(16):
                hd, qb = u // 4, u % 4
                dve.wait_ge(S["ma_score"], u + 1)
                nc.vector.reduce_max(ma_mx, X[u % 2][:, 0:MEM], AX.X).then_inc(S["ma_max"], 1)
                dve.wait_ge(S["ma_max"], u + 1)
                TS(ma_ng, ma_mx, -1.0 / 16, None, ALU.mult).then_inc(S["ma_neg"], 1)
                dve.wait_ge(S["ma_exp"], u + 1)
                nc.vector.reciprocal(ma_r, ma_z).then_inc(S["ma_rz"], 1)
                dve.wait_ge(S["ma_rz"], u + 1)
                TS(me[u % 2][:, 0, :], me[u % 2][:, 0, :], ma_r, None, ALU.mult).then_inc(S["ma_p"], 1)
                if qb == 3:
                    for i in range(2):
                        dve.wait_ge(S["ma_hi"], 2 * hd + i + 1)
                        TTO(o_lo[:, 2 * hd + i, :], M[2 * (hd % 2) + i], o_hi[:, 2 * hd + i, :].bitcast(f32),
                            ALU.subtract).then_inc(S["ma_lo"], 1)
            resid(N_MO, 2, 2, "norm_mlp_w", 0, *mem_of[0][0:2])
            dve.wait_ge(S["st_bias"], 16 * 16)
            dve.wait_ge(S["norm_rstd"], 3)
            mlp(N_MLP1, 0, 3, None)
            norm_final(3, "norm_final_w", 4, 3, "ln_mix_2", g_hi, g_lo_)
            gla_dve(dve, lo, evac, evac_tm, resid)
            dve.wait_ge(S["norm_rstd"], 6)
            mlp(N_MLP2, 1, 6, 5, "kv_norm_2", 0, kx_hi, kx_lo)
            for c in range(KT):
                dve.wait_ge(S["x_hi"], 48 + c + 1)
                STT(sx_lo[:, c, :], h[:, c, :], V("ln_mix_2", 8 + c), sx_hi[:, c, :].bitcast(f32), ALU.mult,
                    ALU.subtract).then_inc(S["x_lo"], 1)
            lo(N_WQ)
            dve.wait_ge(S["norm_rstd"], 7)
            evac(N_KV, 0, kf[:])
            evac_tm(N_KV, 1, sv[:], rcol[:])
            for i in range(2):
                dve.wait_ge(S["sw_dup"], i + 1)
                nc.vector.tensor_copy(kd[i][:], X[1 + i]).then_inc(S["sw_dupev"], 1)
            for b in range(4):
                lo(N_WQ + b + 1)
                for c in range(2):
                    evac(N_WQ + b, c, sq[:, 2 * b + c, :])
            dve.wait_ge(S["ld_bias"], 16)
            for u in range(32):
                c, qb = u // 4, u % 4
                off = 0 if qb else P
                dve.wait_ge(S["sw_score"], u + 1)
                if u >= 2:
                    dve.wait_ge(S["sw_tr"], u - 1)
                s_ = sc[u % 2][:, :, off:256]
                STT(s_, sw_banks(u)[:, :, off:256], 0.125, bias[:, 2 * c:2 * c + 2, off:256],
                    ALU.mult, ALU.add).then_inc(S["sw_s"], 1)
                dve.wait_ge(S["sw_s"], u + 1)
                nc.vector.reduce_max(sw_mx_, s_, AX.X).then_inc(S["sw_mx"], 1)
                dve.wait_ge(S["sw_mx"], u + 1)
                TTO(sw_mx_, sw_mx_, sinkb[:, 2 * c:2 * c + 2], ALU.max).then_inc(S["sw_m"], 1)
                dve.wait_ge(S["sw_m"], u + 1)
                TS(sw_ng_, sw_mx_, -1.0, None, ALU.mult).then_inc(S["sw_neg"], 1)
                TTO(sw_es_, sinkb[:, 2 * c:2 * c + 2], sw_mx_, ALU.subtract).then_inc(S["sw_es"], 1)
                dve.wait_ge(S["sw_e"], 3 * u + 3)
                TTO(sw_es_, sw_es_, sw_z_, ALU.add).then_inc(S["sw_den"], 1)
                dve.wait_ge(S["sw_den"], u + 1)
                nc.vector.reciprocal(sw_r_, sw_es_).then_inc(S["sw_rd"], 1)
                dve.wait_ge(S["sw_rd"], u + 1)
                TTO(s_, s_, sw_r_.unsqueeze(2).to_broadcast([P, 2, 256 - off]), ALU.mult).then_inc(S["sw_p"], 1)
                if qb == 3:
                    dve.wait_ge(S["sw_hi"], c + 1)
                    TTO(s_lo[:, c, :], M[c % 2][:], s_hi[:, c, :].bitcast(f32), ALU.subtract).then_inc(S["sw_lo"], 1)
            resid(N_SOUT, 7, 7, "ln_mlp_2", 8, *mem_of[2][0:2])
            dve.wait_ge(S["norm_rstd"], 8)
            mlp(N_MLP3, 2, 8, None)
            norm_final(8, "ln_final_2")
            for i in range(2 * TT):
                dve.wait_ge(S["fin_tr"], i + 1)
                nc.vector.tensor_copy(ytm[:, i, :], X[2 + i % 2][:]).then_inc(S["fin_ev"], 1)


INPUTS = ["x", "mem", "norm_mix_w", "w_in", "mu_shift", "w_decay0", "w_decay_up", "a0", "a_up", "g_up", "k_k", "k_a", "r_k",
          "lnx_w", "lnx_b", "lam_q1", "lam_k1", "lam_q2", "lam_k2", "subln_w", "w_out", "norm_mem_w", "norm_src_w", "w_mq",
          "w_mk", "w_mv", "w_mo", "norm_mlp_w", "w_up", "w_down", "norm_final_w", "a_w_in_2", "a_w_gk2_2", "a_b_gk_2",
          "a_onorm_2", "a_w_out_2", "kv_norm_2", "w_kv_2", "b_w_q_2", "b_sinks_2", "b_w_out_2", "rel_table_2", "ln_mix_2",
          "ln_mlp_2", "w_up_2", "w_down_2", "ln_final_2"]


def kernel(**inputs):
    import concourse.bacc as _bacc
    from concourse.bass_utils import run_bass_kernel_spmd as _run

    nc = _bacc.Bacc("TRN2", target_bir_lowering=False, num_devices=1)
    given = {name: np.ascontiguousarray(inputs[name]) for name in INPUTS}
    given["vecs"] = np.concatenate([given.pop(name).reshape(-1, P) for name, _ in VECS])
    given["consts"] = constants()
    given["onehot"] = bucket_onehot()
    arrays, aps = {}, {}
    for name, a in given.items():
        arrays[f"in_{name}_dram"] = a
        aps[name] = nc.dram_tensor(f"in_{name}_dram", a.shape, mybir.dt.from_np(a.dtype), kind="ExternalInput").ap()
    out = nc.dram_tensor("out_0_dram", (1, T, D), mybir.dt.float32, kind="ExternalOutput").ap()
    program(nc, aps, out)
    r = _run(nc, [arrays], core_ids=[0])
    return r.results[0]["out_0_dram"]
```

```python
import math
from contextlib import ExitStack

import numpy as np

import concourse.bass as bass
from concourse import mybir

P = 128
T = 512
D = 1024
KT = D // P
BW = 256
TT = T // P
MEM = 256
RW_COLS, RW_W, DIFF_W = 1792, 512, 512
FF = 4 * D
LAM_INIT = 0.8 - 0.6 * math.exp(-0.3 * 0)
C0 = math.exp(-0.5)
NEG = -1e30

VECS = [("norm_mix_w", 8), ("norm_src_w", 8), ("norm_mem_w", 8), ("norm_mlp_w", 8), ("norm_final_w", 8),
        ("mu_shift", 14), ("w_decay0", 4), ("a0", 4), ("k_k", 4), ("k_a", 4), ("r_k", 4), ("lnx_w", 4),
        ("lnx_b", 4), ("subln_w", 1), ("a_b_gk_2", 4), ("a_onorm_2", 2), ("kv_norm_2", 8), ("ln_mix_2", 16),
        ("ln_mlp_2", 16), ("ln_final_2", 8)]
VEC_ROW, _r = {}, 0
for _n, _k in VECS:
    VEC_ROW[_n] = _r
    _r += _k
VEC_ROWS = _r

CONST, _c = {}, 0
for _n, _k in [("ident", 128), ("ones", 128), ("blk64", 128), ("seg", 512), ("lower", 64), ("upper", 64),
               ("upper_in", 64), ("low16", 64), ("up16", 64), ("low32", 64), ("low64", 64), ("eye64", 64),
               ("gla", 128), ("sel0", 128), ("sel1", 128), ("plusminus", 128), ("eps5", 1), ("eps6", 1),
               ("epsgn", 1), ("kkb", 1), ("one", 1), ("zero", 1), ("pad", 2)]:
    CONST[_n] = (_c, _k)
    _c += _k
CONST_COLS = _c


def constants():
    out = np.zeros((P, CONST_COLS), np.float32)

    def put(name, value):
        at, n = CONST[name]
        out[:, at:at + n] = value

    p = np.arange(P)[:, None]
    f = np.arange(P)[None, :]
    a, b = p % 64, np.arange(64)[None, :]
    put("ident", p == f)
    put("ones", 1.0)
    put("blk64", p // 64 == f // 64)
    put("seg", (np.arange(T) % 64 != 0)[None, :])
    put("lower", b < a)
    put("upper", a < b)
    put("upper_in", a <= b)
    put("low16", (b < a) & (a // 16 == b // 16))
    put("up16", (a < b) & (a // 16 == b // 16))
    put("low32", (a // 32 == b // 32) & (a // 16 > b // 16))
    put("low64", a // 32 > b // 32)
    put("eye64", a == b)
    put("gla", (p // 64 == f // 64) & (p <= f))
    put("sel0", p == f % 64)
    put("sel1", p == 64 + f % 64)
    put("plusminus", np.where(p == 0, 1.0, np.where(p == 1, -1.0, 0.0)))
    put("eps5", 1e-5)
    put("eps6", 1e-6)
    put("epsgn", 64e-5)
    put("kkb", 10.0 * math.log(2.0))
    put("one", 1.0)
    return out


def bucket_onehot():
    dist = 255 - np.arange(384)
    n = np.maximum(dist, 0)
    large = 16 + (np.log(np.maximum(n, 1) / 16) / np.log(128 / 16) * 16).astype(np.int32)
    bucket = np.where(n < 16, n, np.minimum(large, 31))
    valid = (dist >= 0) & (dist < 128)
    hot = (bucket[None, :] == np.arange(32)[:, None]) & valid[None, :]
    out = np.zeros((33, 384), np.float32)
    out[:32] = hot
    out[32] = np.where(valid, 0.0, NEG)
    return out


N_DQ, N_DK, N_DV, N_RW = 0, 2, 4, 6
N_WOUT, N_MK, N_MV, N_MQ, N_MO, N_MLP1 = 13, 17, 21, 25, 29, 33
N_GLR, N_GQK, N_GV, N_GG, N_GOUT, N_MLP2 = 65, 66, 70, 74, 78, 82
N_KV, N_WQ, N_SOUT, N_MLP3 = 114, 115, 119, 123
N_END = 155


def acc_before(n):
    return 2 * n - 16 * sum(n >= m + 32 for m in (N_MLP1, N_MLP2, N_MLP3))


RW_STREAM = """d.cs a.sq d.t p.kk2 p.tV d.kk2 d.csx a.ln d.dl a.tV d.kmod a.rn a.ex d.kk a.inc d.rk a.dc a.dec d.beta
    p.bonus a.neg d.A d.R p.tA d.B d.K p.L a.tA d.Kd d.Bd d.bonus p.LT d.L p.tBd d.LT p.tKd a.tBd p.RBT a.tKd
    p.AKT d.RBT p.RKT d.AKT p.P2 d.RKT p.PT2 a.P2 p.X a.PT2 p.TT2 a.X p.P4 d.TT2 p.PT4 a.P4 p.TT3 a.PT4 p.P8
    d.TT3 a.P8 p.TT4 d.TT4 p.T4 p.Z a.T4 a.Z p.TT5 p.T5 d.TT5 p.Z2 d.T5 a.Z2 p.TT6 d.TT6 p.W p.G a.W p.MT a.G
    p.N d.MT p.RT a.N p.S1 d.RT d.S1 p.S2 d.S2 p.S3 d.S3 p.S4 d.S4 p.S5 d.S5 p.S6 d.S6 p.Y p.gate a.Y p.mean
    d.mean a.dsq p.var a.var a.grs d.var d.yb d.yc d.gate""".split()
RW_STEPS = [x[2:] for x in RW_STREAM if x[0] == "p"]
RW_SKEW = (len(RW_STREAM) + 1) // 2
RW_ORDER = [f"{e}.{st}".split(".") + [hp] for st in ("zw", "za") for e in "pa" for hp in range(4)]
RW_ORDER += [x.split(".") + [hp] for _, hp, x in sorted((i + RW_SKEW * hp, hp, x) for i, x in enumerate(RW_STREAM)
                                                        for hp in range(4))]
RW_OPS = {e: [(op, hp) for e_, op, hp in RW_ORDER if e_ == e] for e in "pad"}
RW_NO = {e: {x: i + 1 for i, x in enumerate(ops)} for e, ops in RW_OPS.items()}


def program(nc, A, out):
    f32, f32r, i32 = mybir.dt.float32, mybir.dt.float32r, mybir.dt.int32
    ALU, ACT, AX = mybir.AluOpType, mybir.ActivationFunctionType, mybir.AxisListType
    ds = bass.ds
    ctx = ExitStack()
    with ctx:
        sem_names = """ld_const ld_vec ld_small ld_lora ld_x0 ld_x1 ld_x2 ld_x3 ld_mem ld_gk ld_bias ld_rel st_bias st_out raw_lo
            w_hi_ready w_lo_ready acc_done acc_evac vec_tr vec_ready xt_tr xt_ev bias_mm bias_ev
            norm_sq norm_add norm_ss norm_ln norm_rstd x_hi x_lo h_final
            mn_sq mn_add mn_ss mn_ln mn_rstd mx_hi mx_lo
            lam_mul lam_e lam_mm lam_ready
            da_score da_fill da_max da_neg da_exp da_rz da_c2 da_e1 da_attn da_tr da_at da_pv da_o
            da_sq da_ss da_ln da_rstd da_y
            rw_zero rw_shift rw_p rw_lora rw_act rw_dve rw_half rw_mm y_hi y_lo
            mt_tr mt_ev ms_hi ms_lo ma_score ma_max ma_neg ma_exp ma_rz ma_p ma_tr ma_pt_hi ma_pt_lo ma_pv ma_hi ma_lo
            up_sq up_hi up_lo
            g_gk g_ab g_ln g_act g_dve g_sc g_at g_kt g_ktev g_n g_s g_o g_oev g_sq g_ss g_rl g_rstd g_hi g_lo g_zero g_o1 g_cs g_gate
            sw_dup sw_dup_hi sw_dupev sq_split_hi sq_split_lo sw_score sw_fill sw_s sw_mx sw_m sw_neg sw_e sw_es sw_den sw_rd sw_p sw_tr sw_pt sw_pv sw_hi sw_lo
            fin_tr fin_ev dve_link act_link""".split()
        S = {n: ctx.enter_context(nc.semaphore(n)) for n in sem_names}
        w_arrived = [ctx.enter_context(nc.semaphore(f"w_arrived{i}")) for i in range(4)]

        def at(off, name, shape, dt=f32):
            nbytes = 4 * int(np.prod(shape[1:]))
            t = nc.alloc_sbuf_tensor_at(name, shape, dt, offset=off[0])
            off[0] += (nbytes + 31) // 32 * 32
            return t

        o = [16512]
        h = at(o, "h", [P, KT, T])
        raw = at(o, "raw", [P, 4, KT, BW])
        w_hi = at(o, "w_hi", [P, 2, KT, BW], f32r)
        w_lo = at(o, "w_lo", [P, 2, KT, BW], f32r)
        cst = at(o, "cst", [P, CONST_COLS])
        vec = at(o, "vec", [P, VEC_ROWS])
        rstd = at(o, "rstd", [P, T])
        nt_at = o[0]
        nt = [at(o, f"nt{i}", [P, T]) for i in range(3)]
        rcol = at(o, "rcol", [P, TT])
        small = at(o, "small", [P, 128])
        arena = o[0]
        KB = 1024

        o = [arena]
        y_diff = at(o, "y_diff", [P, 4, T])
        p_rw = at(o, "p_rw", [P, 14, T + 1])
        lora = at(o, "lora", [P, RW_W])
        g_up = at(o, "g_up", [P, RW_W])
        mixing = o[0]
        xm_hi, xm_lo = at(o, "xm_hi", [P, KT, T], f32r), at(o, "xm_lo", [P, KT, T], f32r)
        dq, dk = at(o, "dq", [P, 4, T]), at(o, "dk", [P, 4, T])
        dv = at(o, "dv", [P, TT, DIFF_W])
        de_sq, da_rs = nt[0], nt[1]
        de = [at(o, f"de{i}", [P, T]) for i in range(2)]
        da_t = at(o, "da_t", [P, TT, P])
        da_out = at(o, "da_out", [P, T])
        shift = [at(o, f"shift{i}", [P, T]) for i in range(2)]
        top1 = o[0]
        o = [mixing + 2 * 4 * KT * T]
        xt = at(o, "xt", [P, TT, D])
        vrow = at(o, "vrow", [P, 2, P])
        lamv = at(o, "lamv", [2, 2, 64])
        o = [mixing]
        tm = [[at(o, f"tm{b}_{i}", [P, 4, P]) for i in range(4)] for b in range(2)]
        mt = [[at(o, f"mt{b}_{i}", [P, T]) for i in range(11)] for b in range(2)]
        bon = [at(o, f"bon{b}", [P, T]) for b in range(2)]
        rw_sig = [[at(o, f"sig{i}", [P, T]) for i in range(2)], [at(o, "sig2", [P, T]), nt[2]]]
        top2 = o[0]
        o = [arena]
        x2_hi, x2_lo = at(o, "x2_hi", [P, KT, T], f32r), at(o, "x2_lo", [P, KT, T], f32r)
        me = [at(o, f"me{i}", [P, 4, MEM]) for i in range(2)]
        assert o[0] <= mixing
        o = [mixing]
        y_hi, y_lo = at(o, "yy_hi", [P, KT, T], f32r), at(o, "yy_lo", [P, KT, T], f32r)
        mrow = at(o, "mrow", [P, 2, D])
        memT = at(o, "memT", [P, KT, MEM])
        m_hi, m_lo = at(o, "m_hi", [P, KT, MEM], f32r), at(o, "m_lo", [P, KT, MEM], f32r)
        mnt = [at(o, f"mnt{i}", [P, MEM]) for i in range(3)]
        rstdm = at(o, "rstdm", [P, MEM])
        rcolm = at(o, "rcolm", [P, 2])
        top3 = o[0]
        o = [mixing]
        mk_hi, mk_lo = at(o, "mk_hi", [P, KT, MEM], f32r), at(o, "mk_lo", [P, KT, MEM], f32r)
        mv_hi, mv_lo = at(o, "mv_hi", [P, 2, D], f32r), at(o, "mv_lo", [P, 2, D], f32r)
        mq_hi, mq_lo = at(o, "mq_hi", [P, KT, T], f32r), at(o, "mq_lo", [P, KT, T], f32r)
        o = [arena]
        o_hi, o_lo = at(o, "o_hi", [P, KT, T], f32r), at(o, "o_lo", [P, KT, T], f32r)
        o = [nt_at + 2 * 4 * T]
        onehot = at(o, "onehot_sb", [33, 384])
        relx = at(o, "relx", [33, 16])
        pt_hi = at([nt_at], "pt_hi", [P, 2, T], f32r)
        top3 = o[0]
        o = [mixing + 64 * KB]
        biasrow = at(o, "biasrow", [16, 384])
        pt_lo = at(o, "pt_lo", [P, 2, T], f32r)

        def ms_tmp(s):
            t_ = me[s // 2 % 2][:, 2 * (s % 2):2 * (s % 2) + 2, :].rearrange("p a n -> p (a n)")
            return t_ if s >= 16 else t_[:, 0:MEM]

        def ms_part(s, k, v, q):
            return k[:, s, :] if s < 8 else q[:, s - 16, :] if s >= 16 else v[:, s % 2, (s - 8) // 2 * BW:(s - 8) // 2 * BW + BW]

        def mlp_memory(nth, fo, uo, vo):
            f = [at([arena + fo * KB + 16 * KB * i], f"f{nth}_{i}", [P, KT, T], f32r) for i in range(2)]
            u = [at([arena + a * KB], f"u{nth}_{i}", [P, 16, T], f32r) for i, a in enumerate((uo, vo))]
            return f + u

        mem_of = [mlp_memory(0, 32, 0, 64), mlp_memory(1, 32, 0, 64), mlp_memory(2, 0, 32, 64)]
        o = [arena + 96 * KB]
        ut, us = [at(o, f"ut{i}", [P, T]) for i in range(2)], [nt[0], nt[1]]
        top4 = o[0]
        o = [arena]
        g_hi, g_lo_ = at(o, "gx_hi", [P, KT, T], f32r), at(o, "gx_lo", [P, KT, T], f32r)
        gq, gk, gb = (at(o, n, [P, 4, T]) for n in ("gq", "gk", "gb"))
        gv = at(o, "gv", [P, TT, D])
        gg = at(o, "gg", [P, KT, T])
        gs = [at(o, f"gs{i}", [P, 4, 256]) for i in range(2)]
        gat = [at(o, f"gat{i}", [P, 4, P]) for i in range(2)]
        gkt = [at(o, "gkt0", [P, 4, P]), at([o[0]], "gkt1", [P, 4, P])]
        glr = at(o, "glr", [16, T])
        w_gk2 = at(o, "w_gk2", [16, 512])
        top5 = o[0]
        o = [arena]
        sx_hi, sx_lo = at(o, "sx_hi", [P, KT, T], f32r), at(o, "sx_lo", [P, KT, T], f32r)
        kx_hi, kx_lo = at(o, "kx_hi", [P, KT, T], f32r), at(o, "kx_lo", [P, KT, T], f32r)
        s_hi, s_lo = at([arena + 32 * KB], "so_hi", [P, KT, T], f32r), at([arena + 48 * KB], "so_lo", [P, KT, T], f32r)
        kf = nt[2]
        kd_hi, kd_lo = ([at(o, f"kd_{n}{i}", [P, T], f32r) for i in range(2)] for n in ("hi", "lo"))
        sv = at(o, "sv", [P, TT, P])
        sq_tmp = [at(o, f"sq_tmp{i}", [P, T]) for i in range(4)]
        sq_hi = at([arena + 32 * KB], "sq_hi", [P, KT, T], f32r)
        sq_lo = at([arena + 48 * KB], "sq_lo", [P, KT, T], f32r)
        bias = at(o, "bias", [P, 16, 256])
        spt = [at(o, f"spt{i}", [P, 4, P]) for i in range(2)]
        top6 = o[0]
        o = [arena]
        sc = [at(o, f"sc{i}", [P, 4, 2, 256]) for i in range(3)]
        ytm = at([arena], "ytm", [P, KT, T])
        assert max(top1, top2, top3, top4, top5, top6) <= 16481 + 212863, (top1, top2, top3, top4, top5, top6)

        Mall = ctx.enter_context(nc.psum_tensor("M", [P, 4, T], f32))
        Xall = ctx.enter_context(nc.psum_tensor("X", [P, 4, T], f32))
        M, X = [Mall[:, i, :] for i in range(4)], [Xall[:, i, :] for i in range(4)]
        RB = X + M

        def mem_banks(hd):
            return (Xall[:, 0:2, :], Mall[:, 2:4, :])[hd % 2]

        def sw_banks(u):
            return (Xall[:, 0:2, :], Mall[:, 2:4, :])[u % 2]

        bias_rows = nc.dram_tensor("bias_rows", [16, P, 384], f32, kind="Internal").ap()

        def ytm_view(t):
            return ytm[:, 2 * t:2 * t + 2, :].rearrange("p a n -> p (a n)")

        def C(name, rows=slice(0, P)):
            a, n = CONST[name]
            return cst[rows, a:a + n]

        def V(name, i, rows=slice(0, P)):
            return vec[rows, VEC_ROW[name] + i:VEC_ROW[name] + i + 1]

        MIXED = (4, 5, 6, 7, 0, 1, 2, 3)
        lamneg, lame = small[:, 0:1], small[0:2, 1:2]
        lamd, onec = small[0:2, 2:3], small[:, 3:4]
        da_mx, da_ng, da_z, da_r, da_c = (small[:, 4 + 2 * i:6 + 2 * i] for i in range(5))
        sub_w = small[:, 14:15]
        ma_small = [[small[:, 64 + 16 * j + 4 * i:68 + 16 * j + 4 * i] for i in range(4)] for j in range(2)]
        sinkb = small[:, 32:48]
        sw_small = [[small[:, 48 + 40 * j + 8 * i:56 + 40 * j + 8 * i] for i in range(5)] for j in range(2)]
        g_el = small[:, 64:96]
        rw_dc = [small[:, 96:104], small[:, 104:112]]
        seg = C("seg")

        def W(ap):
            return ap.rearrange("(k p) n -> p k n", p=P)

        w_in, a_in = W(A["w_in"][0]), W(A["a_w_in_2"][0])
        plain = [(N_DQ, 2, w_in, RW_COLS), (N_DK, 2, w_in, RW_COLS + 512), (N_DV, 2, w_in, RW_COLS + 1024),
                 (N_RW, 1, w_in, 12 * P), (N_RW + 1, 6, w_in, 0), (N_WOUT, 4, W(A["w_out"][0]), 0), (N_MK, 4, W(A["w_mk"][0]), 0),
                 (N_MV, 4, W(A["w_mv"][0]), 0), (N_MQ, 4, W(A["w_mq"][0]), 0), (N_MO, 4, W(A["w_mo"][0]), 0),
                 (N_GLR, 1, a_in, 3072), (N_GQK, 4, a_in, 0), (N_GV, 4, a_in, 1024), (N_GG, 4, a_in, 2048),
                 (N_GOUT, 4, W(A["a_w_out_2"][0]), 0), (N_KV, 1, W(A["w_kv_2"]), 0), (N_WQ, 4, W(A["b_w_q_2"][0]), 0),
                 (N_SOUT, 4, W(A["b_w_out_2"][0]), 0)]
        mlps = {N_MLP1: (W(A["w_up"][0]), W(A["w_down"][0])), N_MLP2: (W(A["w_up_2"][0]), W(A["w_down_2"][0])),
                N_MLP3: (W(A["w_up_2"][1]), W(A["w_down_2"][1]))}
        GLR = 16

        HF = 8 * 2
        LAST = N_END
        bias_skewed = lambda: bass.AP(bias_rows.tensor, P - 1, [[384 - 1, P], [P * 384, 16], [1, 256]])
        block = ctx.enter_context(nc.Block())

        SLOT = dict(P=0, Bd=1, B=2, Kd=3, PT=4, O32=5, O64=6, RBT=7, AKT=8, RKT=9, A=10,
                    P2=1, PT2=3, TT=2, P4=0, PT4=4, P8=1, T=3, Z=4, W=0, G=1, MT=5, N=6, RT=8, X=10, S=3, Y=4,
                    cs=5, sw=6, ex=0, inc=4, neg=7, dec=8, a=9, kk=10, t=1, d=2, dsq=5, rs=7)

        def sl(name, hp):
            if hp >= 2 and name in ("sw", "a"):
                return rw_sig[name == "a"][hp % 2]
            return mt[hp % 2][SLOT[name]]

        def rkv(i, hp, lo_=1):
            return p_rw[:, 4 * i + hp, lo_:lo_ + T]

        def rwkv_pe(pe, mm, wait):
            def blk(t, hh, cp, cpar):
                return t[64 * cpar:64 * cpar + 64, (4 * hh + cp) * 64:(4 * hh + cp) * 64 + 64]

            def fm(t, hh, c):
                return t[64 * hh:64 * hh + 64, 64 * c:64 * c + 64]

            def tmv(i, hp, hh, cp, cpar):
                return tm[hp % 2][i][64 * cpar:64 * cpar + 64, cp, 64 * hh:64 * hh + 64]

            mats = dict(X=("AKT", "V"), P2=("PT", "P"), PT2=("P", "PT"), TT2=("P2", "TT"), P4=("PT2", "P2"),
                        PT4=("P2", "PT2"), TT3=("P4", "TT"), P8=("PT4", "P4"), TT4=("P8", "TT"), T4=("TT", "eye"),
                        Z=("O32", "TT"), TT5=("T", "Z"), T5=("Z", "T"), Z2=("O64", "TT"), TT6=("T", "Z"),
                        W=("TT", "Atm"), G=("TT", "X"))
            feats = dict(L=("A", "B"), LT=("B", "A"), RBT=("B", "R"), AKT=("K", "A"), RKT=("K", "R"))
            tms = dict(Atm=0, Bdtm=1, Kdtm=2, V=3)
            after = dict(zw=[], za=[], kk2=["a.sq"], bonus=["d.rk"], tV=[], tA=["d.A"], L=["d.B"], LT=["d.B"],
                         tBd=["d.Bd"], tKd=["d.Bd"], RBT=["d.Bd"], AKT=["d.Bd"], RKT=["d.Bd"], P2=["d.LT"], PT2=["d.LT"],
                         X=["d.AKT", "a.tV"], TT2=["a.P2", "d.RBT"], P4=["a.PT2"], PT4=["a.PT2"], TT3=["a.P4", "d.TT2"],
                         P8=["a.PT4"], TT4=["a.P8", "d.TT3"], T4=["d.TT4"], Z=["d.TT4"], TT5=["a.Z"], T5=["a.Z"],
                         Z2=["d.TT5"], TT6=["a.Z2", "d.T5"], W=["d.TT6", "a.tA"], G=["d.TT6", "a.X"], MT=["a.W", "a.tBd"],
                         N=["a.G", "a.tKd"], RT=["a.W", "d.RBT"], S1=["a.N", "d.MT"], Y=["d.S6", "d.RT", "d.RKT", "a.G"],
                         gate=[], mean=["a.Y"], var=["a.dsq"])
            for i in range(2, 7):
                after[f"S{i}"] = [f"d.S{i - 1}"]
            sem_of = dict(a="rw_act", d="rw_dve")

            def operand(name, hp, hh, cp, cpar):
                if name == "eye":
                    return C("eye64", slice(64 * cpar, 64 * cpar + 64))
                if name in tms:
                    return tmv(tms[name], hp, hh, cp, cpar)
                return blk(sl(name, hp), hh, cp, cpar)

            halves = [0]

            def half_done(ins):
                ins.then_inc(S["rw_half"], 1)
                halves[0] += 1
                wait("rw_half", halves[0])

            def out_of_psum(st, hp):
                e = "a" if (st, hp) in RW_NO["a"] else "d"
                wait(sem_of[e], RW_NO[e][(st, hp)])

            for st, hp in RW_OPS["p"]:
                bank = rw_bank(st, hp)
                if st in RW_STEPS and RW_STEPS.index(st) >= 4:
                    out_of_psum(RW_STEPS[RW_STEPS.index(st) - 4], hp)
                for x in after[st]:
                    wait(sem_of[x[0]], RW_NO[x[0]][(x[2:], hp)])
                fs = slice(hp * P, hp * P + P)
                if st == "zw":
                    wait("ld_lora", 48)
                    last = mm(bank[:], lora[0:64, fs], p_rw[0:64, 12, 1:T + 1], start=True, stop=True)
                elif st == "za":
                    last = mm(bank[:], lora[64:128, fs], p_rw[64:128, 12, 1:T + 1], start=True, stop=True)
                elif st == "gate":
                    last = mm(bank[:], g_up[:, fs], p_rw[:, 13, 1:T + 1], start=True, stop=True)
                elif st in ("kk2", "bonus"):
                    last = mm(bank[:], C("blk64"), nt[hp % 2][:], start=True, stop=True)
                elif st in ("mean", "var"):
                    last = mm(bank[:], C("blk64"), sl("Y" if st == "mean" else "dsq", hp)[:], start=True, stop=True)
                elif st in ("tA", "tBd", "tKd", "tV"):
                    src = rkv(2, hp) if st == "tV" else sl(st[1:], hp)[:]
                    for cp in range(4):
                        last = nc.tensor.transpose(bank[:, cp * P:cp * P + P], src[:, cp * P:cp * P + P], C("ident"))
                elif st in feats:
                    a_, b_ = (rkv(0 if n == "R" else 1, hp) if n in "RK" else sl(n, hp) for n in feats[st])
                    for hh in range(2):
                        if hh:
                            half_done(last)
                        for cp in range(4):
                            for cpar in range(2):
                                c = 2 * cp + cpar
                                last = mm(blk(bank, hh, cp, cpar), fm(a_, hh, c), fm(b_, hh, c), start=True, stop=True)
                elif st in mats:
                    for hh in range(2):
                        for cp in range(4):
                            for cpar in range(2):
                                a_, b_ = (operand(n, hp, hh, cp, cpar) for n in mats[st])
                                last = mm(blk(bank, hh, cp, cpar), a_, b_, start=True, stop=True)
                elif st[0] == "S":
                    c = int(st[1:])
                    for hh in range(2):
                        last = mm(bank[64 * hh:64 * hh + 64, 0:64], fm(sl("MT", hp), hh, c), fm(sl("S", hp), hh, c),
                                  start=True, stop=True)
                elif st != "Y":
                    for turn in range(2):
                        if turn:
                            half_done(last)
                        for cp in range(4):
                            for cpar in range(2):
                                hh = cpar ^ turn
                                o_ = fm(bank, hh, 2 * cp + cpar)
                                if st == "MT":
                                    last = mm(o_, blk(sl("W", hp), hh, cp, cpar), tmv(1, hp, hh, cp, cpar), start=True, stop=True)
                                elif st == "RT":
                                    last = mm(o_, blk(sl("W", hp), hh, cp, cpar), blk(sl("RBT", hp), hh, cp, cpar), start=True, stop=True)
                                else:
                                    mm(o_, tmv(1, hp, hh, cp, cpar), blk(sl("G", hp), hh, cp, cpar), start=True, stop=False)
                                    last = mm(o_, tmv(2, hp, hh, cp, cpar), tmv(3, hp, hh, cp, cpar), start=False, stop=True)
                else:
                    for turn in range(2):
                        if turn:
                            half_done(last)
                        for cp in range(4):
                            for cpar in range(2):
                                hh = cpar ^ turn
                                o_ = fm(bank, hh, 2 * cp + cpar)
                                mm(o_, blk(sl("G", hp), hh, cp, cpar), blk(sl("RBT", hp), hh, cp, cpar),
                                   start=turn == 0 and cp == 0, stop=False, skip_group_check=True)
                                last = mm(o_, tmv(3, hp, hh, cp, cpar), blk(sl("RKT", hp), hh, cp, cpar), start=False,
                                          stop=False, skip_group_check=True)
                    half_done(last)
                    for c in range(1, 8):
                        for hh in range(2):
                            last = mm(fm(bank, hh, c), fm(sl("S", hp), hh, c), fm(sl("RT", hp), hh, c), start=False,
                                      stop=c == 7, skip_group_check=True)
                last.then_inc(S["rw_mm"], 1)

        def rw_bank(st, hp):
            if st not in RW_STEPS:
                return RB[4 * (st == "za") + hp]
            return RB[4 * (hp % 2) + RW_STEPS.index(st) % 4]

        def rwkv_act(act):
            def go(out_, in_, func, **kw):
                nc.scalar.activation(out_, in_, func, **kw).then_inc(S["rw_act"], 1)

            def dve(op, hp):
                act.wait_ge(S["rw_dve"], RW_NO["d"][(op, hp)])

            def own(op, hp):
                act.wait_ge(S["rw_act"], RW_NO["a"][(op, hp)])

            def mm_done(st, hp):
                act.wait_ge(S["rw_mm"], RW_NO["p"][(st, hp)])

            def y_hi_part(c):
                if c < 4:
                    dve("gate", c)
                nc.scalar.activation(y_hi[:, c, :], rkv(0, c) if c < 4 else y_diff[:, c - 4, :], ACT.Copy).then_inc(S["y_hi"], 1)

            for op, hp in RW_OPS["a"]:
                n_ = nt[hp % 2][:]
                if op == "zw":
                    mm_done(op, hp)
                    go(sl("sw", hp)[:], rw_bank(op, hp)[:], ACT.Sigmoid, bias=V("w_decay0", hp))
                elif op == "za":
                    mm_done(op, hp)
                    go(sl("a", hp)[:], rw_bank(op, hp)[:], ACT.Sigmoid, bias=V("a0", hp))
                    if hp == 3:
                        nc.scalar.preload_act_table_set("natural_log_exp_and_others")
                elif op == "sq":
                    if hp >= 2:
                        dve("gate", hp - 2)
                    go(n_, rkv(1, hp), ACT.Square, scale=V("k_k", hp))
                elif op == "ln":
                    dve("kk2", hp)
                    go(n_, n_, ACT.Ln, scale=float(2 ** 20))
                elif op == "rn":
                    own("ln", hp)
                    go(n_, n_, ACT.Exp, scale=-0.5, bias=C("kkb"))
                elif op == "ex":
                    dve("csx", hp)
                    go(sl("ex", hp)[:], sl("sw", hp)[:], ACT.Exp, scale=-C0)
                elif op == "inc":
                    go(sl("inc", hp)[:], sl("cs", hp)[:], ACT.Exp, scale=-C0)
                elif op == "neg":
                    go(sl("neg", hp)[:], sl("cs", hp)[:], ACT.Exp, scale=C0)
                elif op == "dec":
                    dve("dl", hp)
                    go(sl("dec", hp)[:], sl("dec", hp)[:], ACT.Exp, scale=-C0)
                elif op == "dc":
                    go(rw_dc[hp % 2], sl("cs", hp)[:].rearrange("p (c t) -> p c t", t=64)[:, :, 63], ACT.Exp, scale=-C0)
                elif op in ("tV", "tA", "tBd", "tKd"):
                    mm_done(op, hp)
                    go(tm[hp % 2][("tA", "tBd", "tKd", "tV").index(op)][:].rearrange("p c f -> p (c f)"),
                       rw_bank(op, hp)[:], ACT.Copy)
                elif op == "N":
                    mm_done(op, hp)
                    nc.scalar.activation(sl("S", hp)[:, 64:128], rw_bank(op, hp)[:, 0:64], ACT.Copy)
                    go(sl("N", hp)[:], rw_bank(op, hp)[:], ACT.Copy)
                elif op == "dsq":
                    dve("mean", hp)
                    go(sl("dsq", hp)[:], sl("d", hp)[:], ACT.Square)
                elif op == "var":
                    mm_done(op, hp)
                    go(sl("rs", hp)[:], rw_bank(op, hp)[:], ACT.Ln, scale=1.0 / 64, bias=C("epsgn"))
                elif op == "grs":
                    own("var", hp)
                    go(sl("rs", hp)[:], sl("rs", hp)[:], ACT.Exp, scale=-0.5)
                    if hp == 3:
                        for c in MIXED[:7]:
                            y_hi_part(c)
                else:
                    mm_done(op, hp)
                    go(sl("T" if op == "T4" else op[0] if op == "Z2" else op, hp)[:], rw_bank(op, hp)[:], ACT.Copy)
            y_hi_part(3)

        def rwkv_dve(dve):
            TTO, TS, STT = nc.vector.tensor_tensor, nc.vector.tensor_scalar, nc.vector.scalar_tensor_tensor

            def a8(ap):
                return ap.rearrange("p (c t) -> p c t", t=64)

            def mm_done(st, hp):
                dve.wait_ge(S["rw_mm"], RW_NO["p"][(st, hp)])

            def own(op, hp):
                dve.wait_ge(S["rw_dve"], RW_NO["d"][(op, hp)])

            def act(op, hp):
                dve.wait_ge(S["rw_act"], RW_NO["a"][(op, hp)])

            def go(ins):
                ins.then_inc(S["rw_dve"], 1)

            def mask(name):
                return C(name).unsqueeze(1).to_broadcast([P, 8, 64])

            products = {"L", "LT", "RBT", "AKT", "RKT", "kk2", "bonus", "TT2", "TT3", "TT4", "TT5", "T5", "TT6", "MT", "RT",
                        "mean"} | {f"S{i}" for i in range(1, 7)}
            for op, hp in RW_OPS["d"]:
                def s_(name):
                    return sl(name, hp)[:]

                n_, cs8 = nt[hp % 2][:], a8(sl("cs", hp)[:])
                if op in products:
                    mm_done(op, hp)
                    b_ = rw_bank(op, hp)
                if op == "cs":
                    act("zw", hp)
                    if hp >= 2:
                        own("gate", hp - 2)
                    go(nc.vector.tensor_tensor_scan(s_("cs"), seg, s_("sw"), 0.0, ALU.mult, ALU.add))
                elif op == "t":
                    act("za", hp)
                    go(TS(s_("t"), s_("a"), -1.0, V("k_a", hp), ALU.add, ALU.mult))
                elif op == "csx":
                    own("cs", hp)
                    go(TTO(s_("sw"), s_("cs"), s_("sw"), ALU.subtract))
                elif op == "dl":
                    go(TTO(a8(s_("dec")), cs8[:, :, 63:64].to_broadcast([P, 8, 64]), cs8, ALU.subtract))
                elif op == "kmod":
                    own("t", hp)
                    go(STT(s_("t"), s_("t"), 1.0, rkv(1, hp), ALU.add, ALU.mult))
                elif op == "kk2":
                    go(nc.vector.tensor_scalar_max(n_, b_[:], 1e-24))
                elif op == "kk":
                    act("rn", hp)
                    go(STT(s_("kk"), rkv(1, hp), V("k_k", hp), n_, ALU.mult, ALU.mult))
                elif op == "rk":
                    own("kmod", hp)
                    own("kk", hp)
                    go(STT(n_, rkv(0, hp), V("r_k", hp), s_("t"), ALU.mult, ALU.mult))
                elif op == "bonus":
                    go(TTO(bon[hp % 2][:], b_[:], rkv(2, hp), ALU.mult))
                elif op == "beta":
                    go(TTO(s_("a"), s_("kk"), s_("a"), ALU.mult))
                elif op == "A":
                    act("ex", hp)
                    own("beta", hp)
                    go(STT(s_("A"), s_("kk"), -1.0, s_("ex"), ALU.mult, ALU.mult))
                elif op == "R":
                    act("inc", hp)
                    own("rk", hp)
                    go(TTO(rkv(0, hp), rkv(0, hp), s_("inc"), ALU.mult))
                elif op == "B":
                    act("neg", hp)
                    go(TTO(s_("B"), s_("a"), s_("neg"), ALU.mult))
                elif op == "K":
                    go(TTO(rkv(1, hp), s_("t"), s_("neg"), ALU.mult))
                elif op == "Kd":
                    go(TTO(s_("Kd"), s_("t"), s_("dec"), ALU.mult))
                elif op == "Bd":
                    own("Kd", hp)
                    go(TTO(s_("Bd"), s_("a"), s_("dec"), ALU.mult))
                elif op == "L":
                    for name, m in (("P", "low16"), ("O32", "low32"), ("O64", "low64")):
                        last = TTO(a8(s_(name)), a8(b_[:]), mask(m), ALU.mult)
                    go(last)
                elif op in ("LT", "RBT", "AKT", "RKT"):
                    if op == "RBT":
                        own("LT", hp)
                        TTO(a8(s_("TT")), a8(s_("PT")), mask("eye64"), ALU.add)
                    m = dict(LT="up16", RBT="upper_in", AKT="upper", RKT="upper_in")[op]
                    go(TTO(a8(s_("PT" if op == "LT" else op)), a8(b_[:]), mask(m), ALU.mult))
                elif op in ("TT2", "TT3", "TT4", "TT5", "T5", "TT6"):
                    name = op[:-1]
                    go(TTO(s_(name), b_[:], s_(name), ALU.add))
                elif op == "MT":
                    TTO(a8(s_("MT")), mask("eye64"), rw_dc[hp % 2].unsqueeze(2).to_broadcast([P, 8, 64]),
                        ALU.mult).then_inc(S["dve_link"], 1)
                    dve.wait_ge(S["dve_link"], hp + 1)
                    go(TTO(s_("MT"), b_[:], s_("MT"), ALU.add))
                elif op == "RT":
                    go(TTO(s_("RT"), b_[:], rkv(0, hp), ALU.add))
                elif op[0] == "S":
                    c = int(op[1:])
                    go(TTO(sl("S", hp)[:, 64 * (c + 1):64 * (c + 2)], b_[:, 0:64], sl("N", hp)[:, 64 * c:64 * c + 64], ALU.add))
                elif op == "mean":
                    go(STT(s_("d"), b_[:], -1.0 / 64, s_("Y"), ALU.mult, ALU.add))
                elif op == "var":
                    act("grs", hp)
                    go(TTO(s_("d"), s_("d"), s_("rs"), ALU.mult))
                elif op == "yb":
                    own("var", hp)
                    go(TS(s_("d"), s_("d"), V("lnx_w", hp), V("lnx_b", hp), ALU.mult, ALU.add))
                elif op == "yc":
                    own("yb", hp)
                    go(TTO(s_("d"), s_("d"), bon[hp % 2][:], ALU.add))
                elif op == "gate":
                    mm_done("gate", hp)
                    own("yc", hp)
                    go(TTO(rkv(0, hp), rw_bank("gate", hp)[:], s_("d"), ALU.mult))
        def gla_pe(pe, mm, wait, chunk, blocks, block_tm, norm_stat):
            chunk(N_GLR, 0, g_hi, g_lo_, first=24, cols=GLR, inc=2)
            norm_stat(4, cols=True)
            blocks(N_GQK, 1, g_hi, g_lo_)
            wait("acc_evac", acc_before(N_GQK))
            wait("ld_gk", 16)
            wait("norm_rstd", 5)
            for c in range(4):
                mm(X[c][:], w_gk2[:, c * P:c * P + P], glr[:], start=True, stop=True).then_inc(S["g_gk"], 1)
            blocks(N_GQK + 1, 3, g_hi, g_lo_)
            for b in range(4):
                block_tm(N_GV + b, g_hi, g_lo_, TT, 2)
            blocks(N_GG, 4, g_hi, g_lo_)
            wait("acc_evac", acc_before(N_GOUT))
            wait("g_gate", KT)
            wait("g_sc", 4 * 6)
            wait("g_zero", 2)

            def pair_scores(cp):
                tok = slice(cp * P, cp * P + P)
                if cp:
                    wait("g_at", cp)
                for hd in range(4):
                    last = mm(X[0][:, hd * P:hd * P + P], gb[:, hd, tok], gq[:, hd, tok], start=True, stop=True)
                last.then_inc(S["g_kt"], 1)
                if cp >= 2:
                    wait("g_rl", cp - 1)
                if cp:
                    wait("g_ktev", cp)
                for hd in range(4):
                    last = nc.tensor.transpose(X[1][:, hd * P:hd * P + P], gk[:, hd, tok], C("ident"))
                last.then_inc(S["g_kt"], 1)

            def pair_norm(cp):
                wait("g_sq", 2 * (cp + 1))
                wait("g_ktev", min(cp + 2, 4))
                for hd in range(4):
                    for vc in range(2):
                        a_ = (2 * (hd % 2) + vc) * P
                        last = mm(X[1][:, hd * P:hd * P + P], C("ones"), nt[hd // 2][:, a_:a_ + P], start=vc == 0, stop=vc == 1)
                last.then_inc(S["g_ss"], 1)

            pair_scores(0)
            for cp in range(4):
                if cp >= 2:
                    wait("g_oev", 4 * (cp - 1))
                wait("g_at", cp + 1)
                wait("g_ktev", cp + 1)
                ob = [M[2 * (cp % 2)], M[2 * (cp % 2) + 1]]
                for hd in range(4):
                    for vc in range(2):
                        a_ = (2 * (hd % 2) + vc) * P
                        mm(ob[hd // 2][:, a_:a_ + P], gv[:, cp, hd * 256 + vc * P:hd * 256 + vc * P + P], gat[cp % 2][:, hd, :],
                           start=hd % 2 == 0 and vc == 0, stop=False, skip_group_check=True)
                for c2 in range(2):
                    c = 2 * cp + c2
                    if c:
                        wait("g_s", c)
                        for hd in range(4):
                            for vc in range(2):
                                a_ = (2 * (hd % 2) + vc) * P + 64 * c2
                                last = mm(ob[hd // 2][:, a_:a_ + 64], gs[c % 2][:, hd, vc * P:vc * P + P],
                                          gq[:, hd, 64 * c:64 * c + 64], start=False, stop=c2 == 1, skip_group_check=True)
                    if c2:
                        last.then_inc(S["g_o"], 1)
                    if c < 7:
                        r = slice(64 * c2, 64 * c2 + 64)
                        for hd in range(4):
                            last = mm(X[2 + hd // 2][:, (hd % 2) * 256:(hd % 2) * 256 + 256], gkt[cp % 2][r, hd, :],
                                      gv[r, cp, hd * 256:hd * 256 + 256], start=True, stop=True)
                        last.then_inc(S["g_n"], 1)
                    if c2 == 0:
                        if cp:
                            pair_norm(cp - 1)
                        if cp < 3:
                            pair_scores(cp + 1)
            pair_norm(3)
            wait("g_lo", 8)
            blocks(N_GOUT, 4, g_hi, g_lo_)

        def cs(c):
            return gs[c // 2][:].rearrange("p a n -> p (a n)")[:, (c % 2) * T:(c % 2) * T + T]

        def gla_act(act, hi):
            hi(N_GQK + 1)
            for c in range(4):
                act.wait_ge(S["g_gk"], c + 1)
                nc.scalar.activation(cs(c), X[c][:], ACT.Abs, bias=V("a_b_gk_2", c)).then_inc(S["g_ab"], 1)
            for c in range(4):
                act.wait_ge(S["g_ab"], c + 1)
                nc.scalar.activation(cs(c), cs(c), ACT.Exp, scale=-1.0).then_inc(S["g_ab"], 1)
            for c in range(4):
                act.wait_ge(S["g_ab"], 4 + c + 1)
                nc.scalar.activation(cs(c), cs(c), ACT.Ln, bias=C("one")).then_inc(S["g_ln"], 1)
            hi(N_GQK + 2)
            hi(N_GQK + 3)
            hi(N_GV)
            for c in range(4):
                act.wait_ge(S["g_cs"], c + 1)
                if c:
                    act.wait_ge(S["g_sc"], 6 * c)
                nc.scalar.activation(nt[0][:], cs(c), ACT.Exp, scale=1 / 16).then_inc(S["g_act"], 1)
                nc.scalar.activation(gb[:, c, :], cs(c), ACT.Exp, scale=-1 / 16).then_inc(S["g_act"], 1)
                nc.scalar.activation(g_el[:, 8 * c:8 * c + 8], cs(c).rearrange("p (c t) -> p c t", t=64)[:, :, 63],
                                     ACT.Exp, scale=1 / 16).then_inc(S["g_act"], 1)
                act.wait_ge(S["g_dve"], c + 1)
                nc.scalar.activation(nt[1][:], nt[2][:], ACT.Exp, scale=1 / 16).then_inc(S["g_act"], 1)
            for b in range(4):
                hi(N_GV + b + 1)
            for b in range(4):
                hi(N_GG + b + 1)
                for c in range(2):
                    k = 2 * b + c
                    act.wait_ge(S["acc_evac"], acc_before(N_GG) + k + 1)
                    if k >= 2:
                        act.wait_ge(S["g_gate"], k - 1)
                    nc.scalar.activation(nt[c][:], gg[:, k, :], ACT.Sigmoid).then_inc(S["g_act"], 1)
            nc.scalar.preload_act_table_set("natural_log_exp_and_others")

            def keys_out(cp):
                act.wait_ge(S["g_kt"], 2 * cp + 2)
                nc.scalar.activation(gkt[cp % 2][:].rearrange("p a n -> p (a n)"), X[1][:], ACT.Copy).then_inc(S["g_ktev"], 1)

            def pair_norm(cp):
                act.wait_ge(S["g_ss"], cp + 1)
                if cp:
                    act.wait_ge(S["g_oev"], 4 * cp)
                nc.scalar.activation(rstd[:], X[1][:], ACT.Ln, scale=1.0 / 256, bias=C("eps6")).then_inc(S["g_rl"], 1)
                act.wait_ge(S["g_rl"], cp + 1)
                nc.scalar.activation(rstd[:], rstd[:], ACT.Exp, scale=-0.5).then_inc(S["g_rstd"], 1)

            def pair_hi(cp):
                for i in range(2):
                    act.wait_ge(S["g_oev"], 4 * cp + 3 + i)
                    tok = slice(cp * P, cp * P + P)
                    nc.scalar.activation(g_hi[:, 4 * i:4 * i + 4, tok], gg[:, 4 * i:4 * i + 4, tok], ACT.Copy).then_inc(S["g_hi"], 1)

            keys_out(0)
            for cp in range(4):
                if cp:
                    pair_norm(cp - 1)
                if cp < 3:
                    keys_out(cp + 1)
                if cp:
                    pair_hi(cp - 1)
                act.wait_ge(S["g_o"], cp + 1)
                if cp:
                    act.wait_ge(S["g_ss"], cp)
                else:
                    act.wait_ge(S["g_gate"], KT)
                for i in range(2):
                    nc.scalar.activation(nt[i][:], M[2 * (cp % 2) + i][:], ACT.Square).then_inc(S["g_sq"], 1)
            pair_norm(3)
            pair_hi(3)

        def gla_dve(dve, lo, evac, evac_tm, resid):
            TTO, TS, STT = nc.vector.tensor_tensor, nc.vector.tensor_scalar, nc.vector.scalar_tensor_tensor
            for i in range(2):
                nc.vector.memset(gat[i][:], 0.0).then_inc(S["g_zero"], 1)
            lo(N_GQK)
            dve.wait_ge(S["acc_done"], 2 * N_GLR + 2)
            dve.wait_ge(S["norm_rstd"], 5)
            TTO(glr[:], M[acc_before(N_GLR) % 4][0:GLR, :], rstd[0:GLR, :], ALU.mult).then_inc(S["acc_evac"], 2)

            def qk(b):
                lo(N_GQK + b + 1)
                for c in range(2):
                    j = 2 * b + c
                    evac(N_GQK + b, c, (gq if j < 4 else gk)[:, j % 4, :])

            qk(0)
            for c in range(4):
                dve.wait_ge(S["g_ab"], c + 1)
                TS(gb[:, c, :], X[c][:], V("a_b_gk_2", c), 0.0, ALU.add, ALU.min).then_inc(S["g_o1"], 1)
            for c in range(4):
                dve.wait_ge(S["g_ln"], c + 1)
                dve.wait_ge(S["g_o1"], c + 1)
                TTO(gb[:, c, :], gb[:, c, :], cs(c), ALU.subtract).then_inc(S["g_o1"], 1)
            for c in range(4):
                dve.wait_ge(S["g_o1"], 4 + c + 1)
                nc.vector.tensor_tensor_scan(cs(c), seg, gb[:, c, :], 0.0, ALU.mult, ALU.add).then_inc(S["g_cs"], 1)
            qk(1)
            qk(2)
            qk(3)
            for c in range(4):
                dve.wait_ge(S["g_cs"], c + 1)
                c8 = cs(c).rearrange("p (c t) -> p c t", t=64)
                TTO(nt[2][:].rearrange("p (c t) -> p c t", t=64), c8[:, :, 63:64].to_broadcast([P, 8, 64]), c8,
                    ALU.subtract).then_inc(S["g_dve"], 1)
                dve.wait_ge(S["g_act"], 4 * c + 4)
                STT(gq[:, c, :], gq[:, c, :], float(P) ** -0.5, nt[0][:], ALU.mult, ALU.mult).then_inc(S["g_sc"], 2)
                TTO(gb[:, c, :], gk[:, c, :], gb[:, c, :], ALU.mult).then_inc(S["g_sc"], 2)
                TTO(gk[:, c, :], gk[:, c, :], nt[1][:], ALU.mult).then_inc(S["g_sc"], 2)
            for b in range(4):
                lo(N_GV + b + 1)
                for i in range(2):
                    evac_tm(N_GV + b, i, gv[:, 2 * i:2 * i + 2, b * BW:b * BW + BW], rcol[:, 2 * i:2 * i + 2])
            for b in range(4):
                lo(N_GG + b + 1)
                for c in range(2):
                    k = 2 * b + c
                    evac(N_GG + b, c, gg[:, k, :])
                    dve.wait_ge(S["g_act"], 16 + k + 1)
                    STT(gg[:, k, :], gg[:, k, :], V("a_onorm_2", c), nt[c][:], ALU.mult,
                        ALU.mult).then_inc(S["g_gate"], 1)

            def pair_mask(cp):
                dve.wait_ge(S["g_kt"], 2 * cp + 1)
                nc.vector.copy_predicated(gat[cp % 2][:], C("gla").bitcast(i32).unsqueeze(1).to_broadcast([P, 4, P]),
                                          X[0][:].rearrange("p (h n) -> p h n", h=4)).then_inc(S["g_at"], 1)

            def state(c):
                dve.wait_ge(S["g_n"], c + 1)
                if c:
                    dve.wait_ge(S["g_s"], c)
                for hd in range(4):
                    n_ = X[2 + hd // 2][:, (hd % 2) * 256:(hd % 2) * 256 + 256]
                    if c == 0:
                        last = nc.vector.tensor_copy(gs[1][:, hd, :], n_)
                    else:
                        last = STT(gs[(c + 1) % 2][:, hd, :], gs[c % 2][:, hd, :],
                                   g_el[:, 8 * hd + c:8 * hd + c + 1], n_, ALU.mult, ALU.add)
                last.then_inc(S["g_s"], 1)

            def pair_result(cp):
                tok = slice(cp * P, cp * P + P)
                dve.wait_ge(S["g_rstd"], cp + 1)
                for i in range(2):
                    dve.wait_ge(S["g_oev"], 4 * cp + 1 + i)
                    g_ = gg[:, 4 * i:4 * i + 4, tok].rearrange("p (h v) n -> p h v n", h=2)
                    r_ = rstd[:, 2 * i * P:(2 * i + 2) * P].rearrange("p (h n) -> p h n", h=2).unsqueeze(2).to_broadcast([P, 2, 2, P])
                    TTO(g_, g_, r_, ALU.mult).then_inc(S["g_oev"], 1)

            def pair_lo(cp):
                tok = slice(cp * P, cp * P + P)
                for i in range(2):
                    dve.wait_ge(S["g_hi"], 2 * cp + i + 1)
                    TTO(g_lo_[:, 4 * i:4 * i + 4, tok], gg[:, 4 * i:4 * i + 4, tok],
                        g_hi[:, 4 * i:4 * i + 4, tok].bitcast(f32), ALU.subtract).then_inc(S["g_lo"], 1)

            pair_mask(0)
            for cp in range(4):
                state(2 * cp)
                if cp < 3:
                    pair_mask(cp + 1)
                if cp:
                    pair_result(cp - 1)
                if cp < 3:
                    state(2 * cp + 1)
                if cp:
                    pair_lo(cp - 1)
                tok = slice(cp * P, cp * P + P)
                dve.wait_ge(S["g_o"], cp + 1)
                for i in range(2):
                    dve.wait_ge(S["g_sq"], 2 * cp + i + 1)
                    g_ = gg[:, 4 * i:4 * i + 4, tok]
                    TTO(g_, M[2 * (cp % 2) + i][:].rearrange("p (c n) -> p c n", c=4), g_, ALU.mult).then_inc(S["g_oev"], 1)
            pair_result(3)
            pair_lo(3)
            resid(N_GOUT, 5, 4, "ln_mlp_2", 0, *mem_of[1][0:2])

        @block.sync
        def _(sp):
            def load(n, src, cols=BW, r=0):
                if n >= 4:
                    sp.wait_ge(S["w_lo_ready"], n - 3 + r)
                sp.dma_start(raw[:, n % 4, :, 0:cols], src).then_inc(w_arrived[n % 4], 16)

            def load_plain(first):
                _, count, w, col = next(x for x in plain if x[0] == first)
                cols = GLR if first == N_GLR else BW
                for j in range(count):
                    load(first + j, w[:, :, col + BW * j:col + BW * j + cols], cols)

            def load_mlp(n):
                up, down = mlps[n]
                with sp.Fori(0, 2) as half:
                    with sp.Fori(0, 2) as j:
                        for b in range(4):
                            load(n + b, up[:, :, ds(half * 2048 + j * 1024 + b * BW, BW)], r=half * 16 + j * 4)
                    with sp.Fori(0, 2) as q:
                        for b in range(4):
                            kg, cg = b // 2, b % 2
                            load(n + 8 + b, down[:, ds(half * 16 + kg * 8, 8), ds(q * 512 + cg * BW, BW)],
                                 r=half * 16 + q * 4)

            sp.dma_start(cst[:], A["consts"]).then_inc(S["ld_const"], 16)
            for g in range(4):
                sp.dma_start(xt[:, :, g * 256:g * 256 + 256],
                             A["x"][0].rearrange("(t p) n -> p t n", p=P)[:, :, g * 256:g * 256 + 256]).then_inc(S[f"ld_x{g}"], 16)
            for n in (N_DQ, N_DK, N_DV, N_RW, N_RW + 1):
                load_plain(n)
            for n in (N_WOUT, N_MK, N_MV, N_MQ, N_MO):
                load_plain(n)
            load_mlp(N_MLP1)
            for n in (N_GLR, N_GQK, N_GV, N_GG, N_GOUT):
                load_plain(n)
            load_mlp(N_MLP2)
            for n in (N_KV, N_WQ, N_SOUT):
                load_plain(n)
            load_mlp(N_MLP3)
            load(LAST, w_in[:, :, 0:BW])
            for t in range(TT):
                sp.wait_ge(S["fin_ev"], 2 * (t + 1))
                sp.dma_start(out[0].rearrange("(t p) n -> p t n", p=P)[:, t, :], ytm_view(t)).then_inc(S["st_out"], 16)
            sp.wait_ge(S["st_out"], 16 * TT)

        @block.gpsimd
        def _(pool):
            pool.dma_start(vrow[:, 0, :], A["vecs"][0:P]).then_inc(S["ld_vec"], 16)
            pool.dma_start(vrow[0:VEC_ROWS - P, 1, :], A["vecs"][P:VEC_ROWS]).then_inc(S["ld_vec"], 16)
            for i, name in enumerate(("lam_q1", "lam_q2")):
                pool.dma_start(lamv[i:i + 1, 0, :], A[name]).then_inc(S["ld_small"], 16)
            for i, name in enumerate(("lam_k1", "lam_k2")):
                pool.dma_start(lamv[i:i + 1, 1, :], A[name]).then_inc(S["ld_small"], 16)
            pool.dma_start(sinkb, A["b_sinks_2"].broadcast_to([P, 16])).then_inc(S["ld_small"], 16)
            pool.dma_start(lora[0:64, :], A["w_decay_up"][0]).then_inc(S["ld_lora"], 16)
            pool.dma_start(lora[64:128, :], A["a_up"][0]).then_inc(S["ld_lora"], 16)
            pool.dma_start(g_up[:], A["g_up"][0]).then_inc(S["ld_lora"], 16)
            def norm_sums(i):
                for c in range(1, KT):
                    pool.wait_ge(S["norm_sq"], 8 * i + c + 1)
                    if c > 1:
                        pool.wait_ge(S["norm_add"], 7 * i + c - 1)
                    nc.gpsimd.tensor_tensor(nt[2][:], (nt[0] if c == 1 else nt[2])[:], nt[c % 2][:], ALU.add).then_inc(S["norm_add"], 1)

            norm_sums(0)
            pool.wait_ge(S["vec_ready"], 1)
            pool.wait_ge(S["rw_zero"], 1)
            for k in range(14):
                c = (k + 12) % 14
                now, s_ = p_rw[:, c, 1:T + 1], shift[k % 2]
                pool.wait_ge(S["acc_evac"], acc_before(N_RW) + k + 1)
                if k >= 2:
                    pool.wait_ge(S["rw_p"], k - 1)
                nc.gpsimd.tensor_tensor(s_[:], p_rw[:, c, 0:T], now, ALU.subtract).then_inc(S["rw_shift"], 1)
                pool.wait_ge(S["rw_shift"], 2 * k + 1)
                nc.gpsimd.tensor_scalar(s_[:], s_[:], V("mu_shift", c), None, ALU.mult).then_inc(S["rw_shift"], 1)
                pool.wait_ge(S["rw_shift"], 2 * k + 2)
                nc.gpsimd.tensor_tensor(now, s_[:], now, ALU.add).then_inc(S["rw_p"], 1)
            pool.wait_ge(S["rw_dve"], len(RW_OPS["d"]))
            pool.dma_start(mrow[:], A["mem"][0].rearrange("(t p) n -> p t n", p=P)).then_inc(S["ld_mem"], 16)
            pool.wait_ge(S["acc_evac"], acc_before(N_MQ))
            pool.wait_ge(S["norm_ss"], 2)
            pool.dma_start(onehot[:], A["onehot"]).then_inc(S["ld_rel"], 16)
            pool.dma_start(relx[0:32, :], A["rel_table_2"]).then_inc(S["ld_rel"], 16)
            pool.dma_start(relx[32:33, :], A["consts"][0:1, CONST["ones"][0]:CONST["ones"][0] + 16]).then_inc(S["ld_rel"], 16)
            pool.wait_ge(S["bias_ev"], 1)
            pool.dma_start(bias_rows, biasrow[:].unsqueeze(1).to_broadcast([16, P, 384])).then_inc(S["st_bias"], 16)
            pool.wait_ge(S["st_bias"], 16)
            norm_sums(4)
            pool.wait_ge(S["acc_evac"], acc_before(N_GLR))
            pool.dma_start(w_gk2[:], A["a_w_gk2_2"][0]).then_inc(S["ld_gk"], 16)
            pool.wait_ge(S["acc_evac"], acc_before(N_KV))
            pool.dma_start(bias[:], bias_skewed()).then_inc(S["ld_bias"], 16)
            for c in range(KT):
                pool.wait_ge(S["sw_rd"], c + 1)
                s_ = sc[c % 3][:].rearrange("p a b n -> p (a b) n")
                nc.gpsimd.tensor_tensor(s_, s_, sw_small[c % 2][4].unsqueeze(2).to_broadcast([P, 8, 256]),
                                        ALU.mult).then_inc(S["sw_p"], 1)

        @block.tensor
        def _(pe):
            mm = nc.tensor.matmul

            def wait(name, v):
                pe.wait_ge(S[name], v)

            def bank_free(k, r=None):
                if k >= 4:
                    pe.wait_ge(S["acc_evac"], k - 3 if r is None else k - 3 + r)
                return M[k % 4]

            def block_ready(n, r=None):
                pe.wait_ge(S["w_lo_ready"], n + 1 if r is None else n + 1 + r)

            def exact3(dst, wh, wl, xh, xl, start, stop):
                mm(dst, wh, xh, start=start, stop=False)
                mm(dst, wl, xh, start=False, stop=False)
                return mm(dst, wh, xl, start=False, stop=stop)

            def chunk(n, c, hi, lo, first=None, cols=P, tok=T, inc=1, lo_sem="x_lo", order=range(KT)):
                if c == 0:
                    block_ready(n)
                k = acc_before(n) + c
                dst = bank_free(k)
                for i, kt in enumerate(order):
                    if first is not None:
                        wait(lo_sem, first + i + 1)
                    ws = slice(c * P, c * P + cols)
                    last = exact3(dst[0:cols, 0:tok], w_hi[:, n % 2, kt, ws], w_lo[:, n % 2, kt, ws],
                                  hi[:, kt, 0:tok], lo[:, kt, 0:tok], i == 0, i == KT - 1)
                last.then_inc(S["acc_done"], inc)

            def blocks(n, count, hi, lo, first=None, tok=T, lo_sem="x_lo"):
                for b in range(count):
                    for c in range(2):
                        chunk(n + b, c, hi, lo, first if b == 0 and c == 0 else None, tok=tok, lo_sem=lo_sem)

            def block_tm(n, hi, lo, tiles, per, width=BW, at=0, base=None):
                block_ready(n)
                k = acc_before(n) if base is None else base
                for t in range(tiles):
                    if t % per == 0:
                        dst = bank_free(k + t // per)
                    for kt in range(KT):
                        ts_, cs = slice(t * P, t * P + P), slice(at, at + width)
                        o_ = dst[:, (t % per) * width:(t % per + 1) * width]
                        mm(o_, hi[:, kt, ts_], w_hi[:, n % 2, kt, cs], start=kt == 0, stop=False)
                        mm(o_, hi[:, kt, ts_], w_lo[:, n % 2, kt, cs], start=False, stop=False)
                        last = mm(o_, lo[:, kt, ts_], w_hi[:, n % 2, kt, cs], start=False, stop=kt == KT - 1)
                    if t % per == per - 1:
                        last.then_inc(S["acc_done"], 2 // (tiles // per) if base is None else 1)

            def norm_stat(i, cols=False, tok=T, acc=nt[2], add="norm_add", ss="norm_ss"):
                wait(add, 7 * (i + 1))
                last = mm(X[0][:, 0:tok], C("ones"), acc[:, 0:tok], start=True, stop=True)
                if cols:
                    for t in range(tok // P):
                        last = mm(X[1][:, t:t + 1], acc[:, t * P:t * P + P], C("one"), start=True, stop=True)
                last.then_inc(S[ss], 1)

            def mlp(n, first, nth):
                f_hi, f_lo, u_hi, u_lo = mem_of[nth]
                k = acc_before(n)
                with pe.Fori(0, 2) as half:
                    with pe.Fori(0, 2) as j:
                        for b in range(4):
                            block_ready(n + b, half * 16 + j * 4)
                            for c in range(2):
                                dst = bank_free(k + 2 * b + c, half * 24 + j * 8)
                                for kt in range(KT):
                                    if b == 0 and c == 0:
                                        wait("x_lo", first + kt + 1)
                                    ws = slice(c * P, c * P + P)
                                    last = exact3(dst[:], w_hi[:, (n + b) % 2, kt, ws], w_lo[:, (n + b) % 2, kt, ws],
                                                  f_hi[:, kt, :], f_lo[:, kt, :], kt == 0, kt == KT - 1)
                                last.then_inc(S["acc_done"], 1)
                    with pe.Fori(0, 2) as q:
                        for b in range(4):
                            kg = b // 2
                            m = n + 8 + b
                            block_ready(m, half * 16 + q * 4)
                            pe.wait_ge(S["up_lo"], 32 * nth + 8 * kg + 8 + half * 16)
                            for c in range(2):
                                kk = k + 16 + 2 * (b % 2) + c
                                dst = M[kk % 4] if kg else bank_free(kk, half * 24 + q * 4)
                                for kt in range(KT):
                                    ws = slice(c * P, c * P + P)
                                    last = exact3(dst[:], w_hi[:, m % 2, kt, ws], w_lo[:, m % 2, kt, ws],
                                                  u_hi[:, kg * 8 + kt, :], u_lo[:, kg * 8 + kt, :],
                                                  kg == 0 and kt == 0, kg == 1 and kt == KT - 1)
                                last.then_inc(S["acc_done"], 1)

            wait("ld_const", 16)
            for g in range(4):
                wait(f"ld_x{g}", 16)
                for c in (2 * g, 2 * g + 1):
                    if c >= 4:
                        wait("xt_ev", c - 3)
                    for t in range(TT):
                        last = nc.tensor.transpose(X[c % 4][:, t * P:t * P + P], xt[:, t, c * P:c * P + P], C("ident"))
                    last.then_inc(S["xt_tr"], 1)
                if g == 0:
                    wait("ld_vec", 32)
                    nc.tensor.transpose(M[0][:, 0:P], vrow[:, 0, :], C("ident"))
                    nc.tensor.transpose(M[0][:, P:VEC_ROWS], vrow[0:VEC_ROWS - P, 1, :],
                                        C("ident", slice(0, VEC_ROWS - P))[:, 0:VEC_ROWS - P]).then_inc(S["vec_tr"], 1)
            wait("xt_ev", KT)

            chunk(N_DQ, 0, xm_hi, xm_lo, first=0)
            norm_stat(0, cols=True)
            chunk(N_DQ, 1, xm_hi, xm_lo)
            blocks(N_DQ + 1, 1, xm_hi, xm_lo)
            blocks(N_DK, 2, xm_hi, xm_lo)
            wait("lam_e", 1)
            mm(X[3][:, 0:1], C("plusminus", slice(0, 2)), lame, start=True, stop=True).then_inc(S["lam_mm"], 1)
            for b in range(2):
                block_tm(N_DV + b, xm_hi, xm_lo, TT, 2)
            wait("acc_evac", acc_before(N_RW))
            wait("lam_ready", 1)

            def diff_norm(hd):
                wait("da_sq", hd + 1)
                mm(X[2][:], C("ones"), de_sq[:], start=True, stop=True).then_inc(S["da_ss"], 1)

            for u in range(16):
                hd, qb = u // 4, u % 4
                nk = (qb + 1) * P
                if u:
                    wait("da_exp", 2 * u)
                for m in range(2):
                    r = slice(64 * m, 64 * m + 64)
                    last = mm(X[m][:, 0:nk], dq[r, hd, qb * P:qb * P + P], dk[r, hd, 0:nk], start=True, stop=True)
                last.then_inc(S["da_score"], 1)
                if u < 14:
                    chunk(N_RW + u // 2, u % 2, xm_hi, xm_lo)
                if qb == 0 and hd:
                    wait("da_at", u)
                    diff_norm(hd - 1)
                wait("da_attn", u + 1)
                if u:
                    wait("da_at", u)
                if qb == 0 and hd:
                    wait("da_ln", hd)
                for kb in range(qb + 1):
                    last = nc.tensor.transpose(X[2][:, kb * P:kb * P + P], de[1][:, kb * P:kb * P + P], C("ident"))
                last.then_inc(S["da_tr"], 1)
                wait("da_at", u + 1)
                if qb == 0 and hd:
                    wait("da_o", hd)
                for kb in range(qb + 1):
                    last = mm(X[3][:, qb * P:qb * P + P], dv[:, kb, hd * P:hd * P + P], da_t[:, kb, :],
                              start=kb == 0, stop=kb == qb)
                last.then_inc(S["da_pv"], 1)
            diff_norm(3)
            wait("da_y", 4)

            wait("rw_p", 14)
            wait("rw_lora", 2)
            rwkv_pe(pe, mm, wait)

            chunk(N_WOUT, 0, y_hi, y_lo, first=0, lo_sem="y_lo", order=MIXED)
            chunk(N_WOUT, 1, y_hi, y_lo)
            wait("ld_mem", 16)
            for g in range(4):
                for i in range(2):
                    for t in range(2):
                        c = 2 * g + i
                        last = nc.tensor.transpose(X[g][:, i * MEM + t * P:i * MEM + t * P + P],
                                                   mrow[:, t, c * P:c * P + P], C("ident"))
                last.then_inc(S["mt_tr"], 1)
            blocks(N_WOUT + 1, 1, y_hi, y_lo)
            wait("mt_ev", 4)
            norm_stat(0, True, MEM, mnt[2], "mn_add", "mn_ss")
            blocks(N_WOUT + 2, 2, y_hi, y_lo)
            blocks(N_MK, 4, m_hi, m_lo, first=0, tok=MEM, lo_sem="mx_lo")
            for b in range(4):
                block_tm(N_MV + b, m_hi, m_lo, 2, 1)
            wait("mn_ln", 1)
            norm_stat(1)
            blocks(N_MQ, 4, x2_hi, x2_lo, first=8)
            wait("acc_evac", acc_before(N_MO))
            wait("ms_lo", 24)

            def mem_scores(hd):
                if hd >= 2:
                    wait("ma_exp", hd - 1)
                for qb in range(4):
                    dst, q_ = mem_banks(hd)[:, qb // 2, qb % 2 * MEM:qb % 2 * MEM + MEM], slice(qb * P, qb * P + P)
                    for i in range(2):
                        k = 2 * hd + i
                        last = exact3(dst, mq_hi[:, k, q_], mq_lo[:, k, q_], mk_hi[:, k, :], mk_lo[:, k, :], i == 0, i == 1)
                last.then_inc(S["ma_score"], 1)

            mem_scores(0)
            mem_scores(1)
            wait("ld_rel", 48)
            mm(X[3][0:16, 0:384], relx[:], onehot[:], start=True, stop=True).then_inc(S["bias_mm"], 1)
            for hd in range(4):
                wait("ma_p", hd + 1)
                if hd:
                    wait("ma_pt_lo", 2 * hd)
                else:
                    wait("bias_ev", 1)
                for t in range(2):
                    for qb in range(4):
                        last = nc.tensor.transpose(X[2 + t][:, qb * P:qb * P + P], me[hd % 2][:, qb, t * P:t * P + P],
                                                   C("ident"))
                    last.then_inc(S["ma_tr"], 1)
                if hd < 2:
                    mem_scores(hd + 2)
                if hd:
                    wait("ma_lo", 2 * hd)
                for i in range(2):
                    for t in range(2):
                        wait("ma_pt_lo", 2 * hd + t + 1)
                        f = slice((2 * hd + i) * P, (2 * hd + i) * P + P)
                        last = exact3(M[i], mv_hi[:, t, f], mv_lo[:, t, f], pt_hi[:, t, :], pt_lo[:, t, :],
                                      t == 0, t == 1)
                last.then_inc(S["ma_pv"], 1)
            wait("ma_lo", KT)
            blocks(N_MO, 4, o_hi, o_lo)

            norm_stat(2)
            mlp(N_MLP1, 16, 0)
            norm_stat(3)

            gla_pe(pe, mm, wait, chunk, blocks, block_tm, norm_stat)
            norm_stat(5)
            mlp(N_MLP2, 32, 1)

            chunk(N_KV, 0, kx_hi, kx_lo, first=40)
            norm_stat(6, cols=True)
            block_tm(N_KV, kx_hi, kx_lo, TT, TT, width=P, at=P, base=acc_before(N_KV) + 1)
            wait("acc_evac", acc_before(N_KV) + 2)
            for i in range(2):
                mm(X[1 + i][:], C(f"sel{i}"), kf[:], start=True, stop=True).then_inc(S["sw_dup"], 1)
            blocks(N_WQ, 4, sx_hi, sx_lo, first=48)
            wait("acc_evac", acc_before(N_SOUT))
            wait("sw_dupev", 2)
            wait("sq_split_lo", KT)

            def sw_score(u):
                c, qb = u // 4, u % 4
                if u >= 2:
                    wait("sw_s", u - 1)
                lo_ = max(qb - 1, 0) * P
                n = (qb + 1) * P - lo_
                for i in range(2):
                    r = slice(64 * i, 64 * i + 64)
                    q_, k_ = slice(qb * P, qb * P + P), slice(lo_, lo_ + n)
                    last = exact3(sw_banks(u)[:, i, 256 - n:256], sq_hi[r, c, q_], sq_lo[r, c, q_],
                                  kd_hi[c // 4][r, k_], kd_lo[c // 4][r, k_], True, True)
                last.then_inc(S["sw_score"], 1)

            def sw_transposes(u):
                c, qb = u // 4, u % 4
                if u >= 2:
                    wait("sw_pt", u - 1)
                for i in range(2):
                    for kb in ((0, 1) if qb else (1,)):
                        last = nc.tensor.transpose(X[2 + u % 2][:, (2 * i + kb) * P:(2 * i + kb + 1) * P],
                                                   sc[c % 3][:, qb, i, kb * P:kb * P + P], C("ident"))
                last.then_inc(S["sw_tr"], 1)

            for u in range(8):
                sw_score(u)
            for c in range(KT):
                if c + 2 < KT:
                    for qb in range(4):
                        sw_score(4 * (c + 2) + qb)
                wait("sw_p", c + 1)
                sw_transposes(4 * c)
                for qb in range(4):
                    u = 4 * c + qb
                    if qb < 3:
                        sw_transposes(u + 1)
                    wait("sw_pt", u + 1)
                    if qb == 0 and c >= 2:
                        wait("sw_lo", c - 1)
                    kbs = (0, 1) if qb else (1,)
                    for i in range(2):
                        for kb in kbs:
                            last = mm(M[c % 2][64 * i:64 * i + 64, qb * P:qb * P + P],
                                      sv[:, qb - 1 + kb, (c // 4) * 64:(c // 4) * 64 + 64],
                                      spt[u % 2][:, 2 * i + kb, :], start=kb == kbs[0], stop=kb == 1)
                    last.then_inc(S["sw_pv"], 1)
            wait("sw_lo", KT)
            blocks(N_SOUT, 4, s_hi, s_lo)
            norm_stat(7)
            mlp(N_MLP3, 56, 2)
            norm_stat(8)

            wait("acc_evac", acc_before(LAST))
            wait("h_final", HF)
            for t in range(TT):
                for half in range(2):
                    i = 2 * t + half
                    if i >= 2:
                        wait("fin_ev", i - 1)
                    for c in range(4):
                        last = nc.tensor.transpose(X[2 + i % 2][:, c * P:c * P + P], h[:, 4 * half + c, t * P:t * P + P],
                                                   C("ident"))
                    last.then_inc(S["fin_tr"], 1)

        @block.scalar
        def _(act):
            def hi(n, r=None):
                if n >= 2:
                    act.wait_ge(S["acc_done"], 2 * (n - 1) if r is None else 2 * (n - 1) + 2 * r)
                act.wait_ge(w_arrived[n % 4], 16 * (n // 4 + 1) if r is None else 16 * (n // 4 + 1) + 4 * r)
                cols = GLR if n == N_GLR else BW
                nc.scalar.activation(w_hi[:, n % 2, :, 0:cols], raw[:, n % 4, :, 0:cols], ACT.Copy).then_inc(S["w_hi_ready"], 1)

            def norm_chunk(i, c, src, ready=None, x=None, tok=T, sem=("norm_sq", "norm_add", "x_hi")):
                if ready is not None:
                    act.wait_ge(S[ready[0]], ready[1])
                if c >= 2:
                    act.wait_ge(S[sem[1]], 7 * i + max(1, c - 2))
                b_ = (nt if tok == T else mnt)[c % 2]
                nc.scalar.activation(b_[:, 0:tok], src, ACT.Square).then_inc(S[sem[0]], 1)
                if x is not None:
                    nc.scalar.activation(x[1][:, c, :], src, ACT.Copy, scale=x[0]).then_inc(S[sem[2]], 1)

            def norm_rsqrt(i, eps, cols=0, tok=T, rs=rstd, rc=rcol, sem=("norm_ss", "norm_ln", "norm_rstd")):
                act.wait_ge(S[sem[0]], i + 1)
                if cols:
                    nc.scalar.activation(rc[:, 0:cols], X[1][:, 0:cols], ACT.Ln, scale=1.0 / D, bias=C(eps))
                nc.scalar.activation(rs[:, 0:tok], X[0][:, 0:tok], ACT.Ln, scale=1.0 / D, bias=C(eps)).then_inc(S[sem[1]], 1)
                act.wait_ge(S[sem[1]], i + 1)
                if cols:
                    nc.scalar.activation(rc[:, 0:cols], rc[:, 0:cols], ACT.Exp, scale=-0.5)
                nc.scalar.activation(rs[:, 0:tok], rs[:, 0:tok], ACT.Exp, scale=-0.5).then_inc(S[sem[2]], 1)

            def resid_norm(n, i, x=None):
                for b in range(4):
                    hi(n + b + 1)
                    for c in range(2):
                        c_ = 2 * b + c
                        norm_chunk(i, c_, h[:, c_, :], ("acc_evac", acc_before(n) + c_ + 1), x and (V(x[0], x[1] + c_), x[2]))

            def mlp(n, nth, i_, x=None):
                u_hi = mem_of[nth][2]
                k = acc_before(n)
                for half in range(2):
                    with act.Fori(0, 2) as j:
                        for b in range(4):
                            hi(n + b + 1, half * 16 + j * 4)
                            for c in range(2):
                                i = 2 * b + c
                                act.wait_ge(S["acc_evac"], k + i + 1 + half * 24 + j * 8)
                                nc.scalar.activation(us[c][:], ut[c][:], ACT.Square).then_inc(S["up_sq"], 1)
                                act.wait_ge(S["up_sq"], 32 * nth + i + 1 + half * 16 + j * 8)
                                nc.scalar.activation(u_hi[:, ds(j * 8 + i, 1), :], us[c][:].unsqueeze(1), ACT.Copy).then_inc(S["up_hi"], 1)
                    if half == 0:
                        with act.Fori(0, 2) as q:
                            for b in range(4):
                                hi(n + 9 + b, q * 4)
                for q in range(2):
                    for b in range(4):
                        if n + 25 + 4 * q + b < N_END:
                            hi(n + 25 + 4 * q + b)
                        if b >= 2:
                            for c in range(2):
                                c_ = 4 * q + 2 * (b % 2) + c
                                norm_chunk(i_, c_, h[:, c_, :], ("acc_evac", k + 40 + c_ + 1), x and (V(x[0], x[1] + c_), x[2]))

            nc.scalar.preload_act_table_set("natural_log_exp_and_others")
            for c in range(KT):
                norm_chunk(0, c, h[:, c, :], ("xt_ev", c + 1), (V("norm_mix_w", c), xm_hi))
            hi(0)
            hi(1)
            norm_rsqrt(0, "eps5", cols=TT)
            act.wait_ge(S["lam_mul"], 3)
            nc.scalar.activation(lame, lamd, ACT.Exp).then_inc(S["lam_e"], 1)
            for n in range(1, N_RW):
                hi(n + 1)
            for u in range(16):
                hd, qb = u // 4, u % 4
                nk = (qb + 1) * P
                act.wait_ge(S["da_neg"], u + 1)
                for m in range(2):
                    nc.scalar.activation(de[m][:, 0:nk], X[m][:, 0:nk], ACT.Exp, bias=da_ng[:, m:m + 1], scale=0.125,
                                         accum_out=da_z[:, m:m + 1]).then_inc(S["da_exp"], 1)
                if u % 2 == 0 and u < 14:
                    hi(N_RW + u // 2 + 1)
                if qb == 0 and hd:
                    act.wait_ge(S["da_ss"], hd)
                    nc.scalar.activation(da_rs[:], X[2][:], ACT.Ln, scale=1.0 / P, bias=C("eps5")).then_inc(S["da_ln"], 1)
                    act.wait_ge(S["da_ln"], hd)
                    nc.scalar.activation(da_rs[:], da_rs[:], ACT.Exp, scale=-0.5).then_inc(S["da_rstd"], 1)
                act.wait_ge(S["da_tr"], u + 1)
                nc.scalar.activation(da_t[:, 0:qb + 1, :], X[2][:, 0:nk].rearrange("p (k n) -> p k n", n=P), ACT.Copy).then_inc(S["da_at"], 1)
                if qb == 3:
                    act.wait_ge(S["da_o"], hd + 1)
                    if hd:
                        act.wait_ge(S["da_ss"], hd)
                    nc.scalar.activation(de_sq[:], da_out[:], ACT.Square).then_inc(S["da_sq"], 1)
            act.wait_ge(S["da_ss"], 4)
            nc.scalar.activation(da_rs[:], X[2][:], ACT.Ln, scale=1.0 / P, bias=C("eps5")).then_inc(S["da_ln"], 1)
            act.wait_ge(S["da_ln"], 4)
            nc.scalar.activation(da_rs[:], da_rs[:], ACT.Exp, scale=-0.5).then_inc(S["da_rstd"], 1)
            act.wait_ge(S["rw_p"], 14)
            nc.scalar.activation(p_rw[0:64, 12, 1:T + 1], p_rw[0:64, 12, 1:T + 1], ACT.Tanh).then_inc(S["rw_lora"], 1)
            nc.scalar.activation(p_rw[:, 13, 1:T + 1], p_rw[:, 13, 1:T + 1], ACT.Sigmoid).then_inc(S["rw_lora"], 1)
            rwkv_act(act)
            def out_chunk(c):
                norm_chunk(1, c, h[:, c, :], ("acc_evac", acc_before(N_WOUT) + c + 1), (V("norm_mem_w", c), x2_hi))

            hi(N_WOUT + 1)
            out_chunk(0)
            out_chunk(1)
            for c in range(KT):
                norm_chunk(0, c, memT[:, c, :], ("mt_ev", c // 2 + 1), (V("norm_src_w", c), m_hi), MEM,
                           ("mn_sq", "mn_add", "mx_hi"))
            hi(N_WOUT + 2)
            out_chunk(2)
            out_chunk(3)
            norm_rsqrt(0, "eps5", 2, MEM, rstdm, rcolm, ("mn_ss", "mn_ln", "mn_rstd"))
            hi(N_WOUT + 3)
            out_chunk(4)
            out_chunk(5)
            hi(N_MK)
            out_chunk(6)
            out_chunk(7)
            for n in range(N_MK, N_MO):
                if n == N_MQ:
                    norm_rsqrt(1, "eps5")
                hi(n + 1)
                for s in (2 * (n - N_MK), 2 * (n - N_MK) + 1):
                    act.wait_ge(S["acc_evac"], acc_before(N_MK) + s + 1)
                    nc.scalar.activation(ms_part(s, mk_hi, mv_hi, mq_hi), ms_tmp(s), ACT.Copy).then_inc(S["ms_hi"], 1)

            def mem_exps(hd):
                _, ma_ng, ma_z, _ = ma_small[hd % 2]
                act.wait_ge(S["ma_neg"], hd + 1)
                if hd >= 2:
                    act.wait_ge(S["ma_tr"], 2 * (hd - 1))
                for qb in range(4):
                    last = nc.scalar.activation(me[hd % 2][:, qb, :], mem_banks(hd)[:, qb // 2, qb % 2 * MEM:qb % 2 * MEM + MEM], ACT.Exp,
                                                bias=ma_ng[:, qb:qb + 1], scale=1.0 / 16, accum_out=ma_z[:, qb:qb + 1])
                last.then_inc(S["ma_exp"], 1)

            act.wait_ge(S["ms_lo"], 24)
            mem_exps(0)
            mem_exps(1)
            act.wait_ge(S["bias_mm"], 1)
            nc.scalar.activation(biasrow[:], X[3][0:16, 0:384], ACT.Copy).then_inc(S["bias_ev"], 1)
            for hd in range(4):
                for t in range(2):
                    act.wait_ge(S["ma_tr"], 2 * hd + t + 1)
                    if hd:
                        act.wait_ge(S["ma_pv"], hd)
                    nc.scalar.activation(pt_hi[:, t, :], X[2 + t], ACT.Copy).then_inc(S["ma_pt_hi"], 1)
                if hd < 2:
                    mem_exps(hd + 2)
                act.wait_ge(S["ma_pv"], hd + 1)
                for i in range(2):
                    nc.scalar.activation(o_hi[:, 2 * hd + i, :], M[i][:], ACT.Copy).then_inc(S["ma_hi"], 1)
            resid_norm(N_MO, 2, ("norm_mlp_w", 0, mem_of[0][0]))
            norm_rsqrt(2, "eps5")
            mlp(N_MLP1, 0, 3)
            norm_rsqrt(3, "eps5")
            for c in range(KT):
                norm_chunk(4, c, h[:, c, :], ("h_final", c + 1), (V("ln_mix_2", c), g_hi))
            hi(N_GQK)
            norm_rsqrt(4, "eps6", cols=TT)
            gla_act(act, hi)
            resid_norm(N_GOUT, 5, ("ln_mlp_2", 0, mem_of[1][0]))
            norm_rsqrt(5, "eps6")
            mlp(N_MLP2, 1, 6, ("kv_norm_2", 0, kx_hi))
            for c in range(KT):
                nc.scalar.activation(sx_hi[:, c, :], h[:, c, :], ACT.Copy, scale=V("ln_mix_2", 8 + c)).then_inc(S["x_hi"], 1)
            norm_rsqrt(6, "eps6", cols=TT)
            hi(N_WQ)
            for i in range(2):
                act.wait_ge(S["sw_dup"], i + 1)
                nc.scalar.activation(kd_hi[i][:], X[1 + i], ACT.Copy).then_inc(S["sw_dup_hi"], 1)
            for n in range(N_WQ, N_SOUT):
                hi(n + 1)
                for s in (2 * (n - N_WQ), 2 * (n - N_WQ) + 1):
                    act.wait_ge(S["acc_evac"], acc_before(N_WQ) + s + 1)
                    nc.scalar.activation(sq_hi[:, s, :], sq_tmp[s % 4][:], ACT.Copy).then_inc(S["sq_split_hi"], 1)
            def sw_exps(c):
                _, sw_ng_, sw_z_, sw_es_, _ = sw_small[c % 2]
                act.wait_ge(S["sw_neg"], c + 1)
                for qb in range(4):
                    for i in range(2):
                        k, s_ = 2 * qb + i, sc[c % 3][:, qb, i, (0 if qb else P):256]
                        nc.scalar.activation(s_, s_, ACT.Exp, bias=sw_ng_[:, k:k + 1], accum_out=sw_z_[:, k:k + 1])
                act.wait_ge(S["sw_es"], c + 1)
                nc.scalar.activation(sw_es_, sw_es_, ACT.Exp).then_inc(S["sw_e"], 1)

            sw_exps(0)
            for c in range(KT):
                if c + 1 < KT:
                    sw_exps(c + 1)
                for qb in range(4):
                    u = 4 * c + qb
                    act.wait_ge(S["sw_tr"], u + 1)
                    if u >= 2:
                        act.wait_ge(S["sw_pv"], u - 1)
                    o4 = slice(0 if qb else 1, 2)
                    nc.scalar.activation(spt[u % 2][:].rearrange("p (i k) n -> p i k n", i=2)[:, :, o4, :],
                                         X[2 + u % 2][:].rearrange("p (i k n) -> p i k n", i=2, k=2)[:, :, o4, :],
                                         ACT.Copy).then_inc(S["sw_pt"], 1)
                act.wait_ge(S["sw_pv"], 4 * c + 4)
                nc.scalar.activation(s_hi[:, c, :], M[c % 2][:], ACT.Copy).then_inc(S["sw_hi"], 1)
            resid_norm(N_SOUT, 7, ("ln_mlp_2", 8, mem_of[2][0]))
            norm_rsqrt(7, "eps6")
            mlp(N_MLP3, 2, 8)
            norm_rsqrt(8, "eps6")

        @block.vector
        def _(dve):
            TTO, TS, STT = nc.vector.tensor_tensor, nc.vector.tensor_scalar, nc.vector.scalar_tensor_tensor

            def lo(n, r=None):
                dve.wait_ge(S["w_hi_ready"], n + 1 if r is None else n + 1 + r)
                cols = GLR if n == N_GLR else BW
                TTO(w_lo[:, n % 2, :, 0:cols], raw[:, n % 4, :, 0:cols], w_hi[:, n % 2, :, 0:cols].bitcast(f32),
                    ALU.subtract).then_inc(S["w_lo_ready"], 1)

            def evac_copy(n, c, dst, two=False):
                dve.wait_ge(S["acc_done"], 2 * n + c + 1)
                src = M[(acc_before(n) + c) % 4][:]
                nc.vector.tensor_copy(dst, src.rearrange("p (t n) -> p t n", t=2) if two else src).then_inc(S["acc_evac"], 1)

            def evac(n, c, dst):
                dve.wait_ge(S["acc_done"], 2 * n + c + 1)
                TTO(dst, M[(acc_before(n) + c) % 4], rstd[:], ALU.mult).then_inc(S["acc_evac"], 1)

            def evac_tm(n, c, dst, rc):
                _, t_, f_ = dst.shape
                dve.wait_ge(S["acc_done"], 2 * n + c + 1)
                src = M[(acc_before(n) + c) % 4][:, 0:t_ * f_].rearrange("p (t n) -> p t n", t=t_)
                TTO(dst, src, rc.unsqueeze(2).to_broadcast([P, t_, f_]), ALU.mult).then_inc(S["acc_evac"], 1)

            def resid_chunk(n, b, c):
                i = 2 * b + c
                dve.wait_ge(S["acc_done"], 2 * n + i + 1)
                TTO(h[:, i, :], h[:, i, :], M[(acc_before(n) + i) % 4], ALU.add).then_inc(S["acc_evac"], 1)

            def norm_step(i, c, j, src, w, lo_, hi_, tok=T, sem=("norm_sq", "norm_add", "x_hi", "x_lo")):
                b_ = nt if tok == T else mnt
                if c and not (sem[1] == "norm_add" and i in (0, 4)):
                    dve.wait_ge(S[sem[0]], 8 * i + c + 1)
                    if c > 1:
                        dve.wait_ge(S[sem[1]], 7 * i + c - 1)
                    TTO(b_[2][:, 0:tok], (b_[0] if c == 1 else b_[2])[:, 0:tok], b_[c % 2][:, 0:tok],
                        ALU.add).then_inc(S[sem[1]], 1)
                if w is not None:
                    dve.wait_ge(S[sem[2]], 8 * j + c + 1)
                    STT(lo_[:, c, :], src, w, hi_[:, c, :].bitcast(f32), ALU.mult, ALU.subtract).then_inc(S[sem[3]], 1)

            def resid(n, i, j, wname, woff, hi_, lo_):
                dve.wait_ge(S["acc_evac"], acc_before(n))
                for b in range(4):
                    lo(n + b + 1)
                    for c in range(2):
                        resid_chunk(n, b, c)
                        if 2 * b + c:
                            c_ = 2 * b + c - 1
                            norm_step(i, c_, j, h[:, c_, :], V(wname, woff + c_), lo_, hi_)
                norm_step(i, 7, j, h[:, 7, :], V(wname, woff + 7), lo_, hi_)

            def norm_final(i, wname, i2=None, j2=None, w2=None, hi_=None, lo_=None):
                dve.wait_ge(S["norm_rstd"], i + 1)
                for c in range(KT):
                    STT(h[:, c, :], h[:, c, :], V(wname, c), rstd[:], ALU.mult, ALU.mult).then_inc(S["h_final"], 1)
                    if c and w2:
                        norm_step(i2, c - 1, j2, h[:, c - 1, :], V(w2, c - 1), lo_, hi_)
                if w2:
                    norm_step(i2, 7, j2, h[:, 7, :], V(w2, 7), lo_, hi_)

            def mlp(n, nth, i_, j_, wname=None, woff=0, hi_=None, lo_=None):
                u_hi, u_lo = mem_of[nth][2:4]
                k = acc_before(n)
                for half in range(2):
                    with dve.Fori(0, 2) as j:
                        for b in range(4):
                            lo(n + b + 1, half * 16 + j * 4)
                            for c in range(2):
                                i = 2 * b + c
                                dve.wait_ge(S["acc_done"], 2 * n + i + 1 + half * 32 + j * 8)
                                STT(ut[c][:], M[(k + i) % 4], 0.0, rstd[:], ALU.max, ALU.mult).then_inc(S["acc_evac"], 1)
                                dve.wait_ge(S["up_hi"], 32 * nth + i + 1 + half * 16 + j * 8)
                                u_ = ds(j * 8 + i, 1)
                                TTO(u_lo[:, u_, :], us[c][:].unsqueeze(1), u_hi[:, u_, :].bitcast(f32),
                                    ALU.subtract).then_inc(S["up_lo"], 1)
                    if half == 0:
                        with dve.Fori(0, 2) as q:
                            for b in range(4):
                                lo(n + 9 + b, q * 4)
                                if b >= 2:
                                    for c in range(2):
                                        i = 2 * (b % 2) + c
                                        dve.wait_ge(S["acc_done"], 2 * (n + 8 + b) + c + 1 + q * 8)
                                        dve.wait_ge(S["acc_evac"], k + 16 + i + q * 4)
                                        h_ = h[:, ds(q * 4 + i, 1), :]
                                        TTO(h_, h_, M[(k + i) % 4].unsqueeze(1), ALU.add).then_inc(S["acc_evac"], 1)
                for q in range(2):
                    for b in range(4):
                        if n + 25 + 4 * q + b < N_END:
                            lo(n + 25 + 4 * q + b)
                        if b >= 2:
                            for c in range(2):
                                i = 4 * q + 2 * (b % 2) + c
                                dve.wait_ge(S["acc_done"], 2 * (n + 24 + 4 * q + b) + c + 1)
                                TTO(h[:, i, :], h[:, i, :], M[(k + i) % 4], ALU.add).then_inc(S["acc_evac"], 1)
                                if i:
                                    norm_step(i_, i - 1, j_, h[:, i - 1, :], wname and V(wname, woff + i - 1), lo_, hi_)
                norm_step(i_, 7, j_, h[:, 7, :], wname and V(wname, woff + 7), lo_, hi_)

            nc.vector.memset(p_rw[:, :, 0:1], 0.0).then_inc(S["rw_zero"], 1)
            dve.wait_ge(S["vec_tr"], 1)
            nc.vector.tensor_copy(vec[:], M[0][:, 0:VEC_ROWS]).then_inc(S["vec_ready"], 1)
            dve.wait_ge(S["vec_ready"], 1)
            nc.vector.tensor_scalar(sub_w, V("subln_w", 0), 1.0 - LAM_INIT, None, ALU.mult).then_inc(S["vec_ready"], 1)
            for c in range(KT):
                dve.wait_ge(S["xt_tr"], c + 1)
                nc.vector.tensor_copy(h[:, c, :], X[c % 4]).then_inc(S["xt_ev"], 1)
                if c:
                    norm_step(0, c - 1, 0, h[:, c - 1, :], V("norm_mix_w", c - 1), xm_lo, xm_hi)
            norm_step(0, 7, 0, h[:, 7, :], V("norm_mix_w", 7), xm_lo, xm_hi)
            lo(0)
            dve.wait_ge(S["ld_small"], 16 * 5)
            TTO(lamv[:, 0, :], lamv[:, 0, :], lamv[:, 1, :], ALU.mult).then_inc(S["lam_mul"], 1)
            dve.wait_ge(S["lam_mul"], 1)
            nc.vector.reduce_sum(lamd, lamv[:, 0, :], AX.X).then_inc(S["lam_mul"], 2)
            lo(1)
            dve.wait_ge(S["norm_rstd"], 1)
            for b in range(4):
                if b:
                    lo(b + 1)
                for c in range(2):
                    i = 2 * b + c
                    evac(b, c, (dq if i < 4 else dk)[:, i % 4, :])
            dve.wait_ge(S["lam_mm"], 1)
            TS(lamneg, X[3][:, 0:1], -1.0, -LAM_INIT, ALU.mult, ALU.add).then_inc(S["lam_ready"], 1)
            for b in range(2):
                lo(N_DV + b + 1)
                for i in range(2):
                    evac_tm(N_DV + b, i, dv[:, 2 * i:2 * i + 2, b * BW:b * BW + BW], rcol[:, 2 * i:2 * i + 2])
            def diff_y(hd):
                dve.wait_ge(S["da_rstd"], hd + 1)
                STT(y_diff[:, hd, :], da_out[:], sub_w, da_rs[:], ALU.mult, ALU.mult).then_inc(S["da_y"], 1)

            for u in range(16):
                hd, qb = u // 4, u % 4
                nk = (qb + 1) * P
                dve.wait_ge(S["da_score"], u + 1)
                for m in range(2):
                    nc.vector.memset(X[m][0:64, nk - 64:nk], NEG).then_inc(S["da_fill"], 1)
                dve.wait_ge(S["da_fill"], 2 * u + 2)
                for m in range(2):
                    nc.vector.reduce_max(da_mx[:, m:m + 1], X[m][:, 0:nk], AX.X).then_inc(S["da_max"], 1)
                dve.wait_ge(S["da_max"], 2 * u + 2)
                TS(da_ng, da_mx, -0.125, None, ALU.mult).then_inc(S["da_neg"], 1)
                dve.wait_ge(S["da_exp"], 2 * u + 2)
                nc.vector.reciprocal(da_r, da_z).then_inc(S["da_rz"], 1)
                dve.wait_ge(S["da_rz"], u + 1)
                TS(da_c[:, 0:1], da_r[:, 1:2], lamneg, None, ALU.mult).then_inc(S["da_c2"], 1)
                TS(de[0][:, 0:nk], de[0][:, 0:nk], da_r[:, 0:1], None, ALU.mult).then_inc(S["da_c2"], 1)
                dve.wait_ge(S["da_c2"], 2 * u + 2)
                STT(de[1][:, 0:nk], de[1][:, 0:nk], da_c[:, 0:1], de[0][:, 0:nk], ALU.mult, ALU.add).then_inc(S["da_attn"], 1)
                if u < 14:
                    n, c = N_RW + u // 2, u % 2
                    if c == 0:
                        lo(n + 1)
                    evac(n, c, p_rw[:, (2 * (n - N_RW) + c + 12) % 14, 1:T + 1])
                if qb == 0 and hd:
                    diff_y(hd - 1)
                if qb == 3:
                    dve.wait_ge(S["da_pv"], u + 1)
                    nc.vector.tensor_copy(da_out[:], X[3][:]).then_inc(S["da_o"], 1)
            diff_y(3)
            dve.wait_ge(S["da_y"], 4)
            dve.wait_ge(S["rw_p"], 14)
            rwkv_dve(dve)
            for i, c in enumerate(MIXED):
                dve.wait_ge(S["y_hi"], i + 1)
                TTO(y_lo[:, c, :], rkv(0, c) if c < 4 else y_diff[:, c - 4, :], y_hi[:, c, :].bitcast(f32),
                    ALU.subtract).then_inc(S["y_lo"], 1)
            def out_step(c):
                norm_step(1, c, 1, h[:, c, :], V("norm_mem_w", c), x2_lo, x2_hi)

            lo(N_WOUT + 1)
            resid_chunk(N_WOUT, 0, 0)
            resid_chunk(N_WOUT, 0, 1)
            out_step(0)
            out_step(1)
            for c in range(KT):
                if c % 2 == 0:
                    dve.wait_ge(S["mt_tr"], c // 2 + 1)
                    nc.vector.tensor_copy(memT[:, c:c + 2, :], X[c // 2].rearrange("p (a n) -> p a n", a=2)).then_inc(S["mt_ev"], 1)
                norm_step(0, c, 0, memT[:, c, :], V("norm_src_w", c), m_lo, m_hi, MEM, ("mn_sq", "mn_add", "mx_hi", "mx_lo"))
            for b in range(1, 4):
                lo(N_WOUT + b + 1)
                for c in range(2):
                    resid_chunk(N_WOUT, b, c)
                    if b > 1 or c:
                        out_step(2 * b + c - 1)
            out_step(7)

            def ms_lo_part(s):
                dve.wait_ge(S["ms_hi"], s + 1)
                TTO(ms_part(s, mk_lo, mv_lo, mq_lo), ms_tmp(s), ms_part(s, mk_hi, mv_hi, mq_hi).bitcast(f32),
                    ALU.subtract).then_inc(S["ms_lo"], 1)

            dve.wait_ge(S["mn_rstd"], 1)
            for s in range(24):
                n, c = N_MK + s // 2, s % 2
                if c == 0:
                    lo(n + 1)
                if s == 16:
                    dve.wait_ge(S["norm_rstd"], 2)
                dve.wait_ge(S["acc_done"], 2 * n + c + 1)
                if s >= 4:
                    dve.wait_ge(S["ms_lo"], s - 3)
                src = M[(acc_before(n) + c) % 4]
                if s < 8:
                    TTO(ms_tmp(s), src[:, 0:MEM], rstdm[:], ALU.mult).then_inc(S["acc_evac"], 1)
                elif s < 16:
                    TS(ms_tmp(s), src[:, 0:MEM], rcolm[:, c:c + 1], None, ALU.mult).then_inc(S["acc_evac"], 1)
                else:
                    TTO(ms_tmp(s), src, rstd[:], ALU.mult).then_inc(S["acc_evac"], 1)
                if s:
                    ms_lo_part(s - 1)
            ms_lo_part(23)

            def mem_maxima(hd):
                ma_mx, ma_ng, _, _ = ma_small[hd % 2]
                dve.wait_ge(S["ma_score"], hd + 1)
                nc.vector.reduce_max(ma_mx, mem_banks(hd).rearrange("p b (a n) -> p (b a) n", n=MEM), AX.X).then_inc(S["ma_max"], 1)
                dve.wait_ge(S["ma_max"], hd + 1)
                TS(ma_ng, ma_mx, -1.0 / 16, None, ALU.mult).then_inc(S["ma_neg"], 1)

            def mem_probabilities(hd):
                _, _, ma_z, ma_r = ma_small[hd % 2]
                dve.wait_ge(S["ma_exp"], hd + 1)
                nc.vector.reciprocal(ma_r, ma_z).then_inc(S["ma_rz"], 1)
                dve.wait_ge(S["ma_rz"], hd + 1)
                TTO(me[hd % 2][:], me[hd % 2][:], ma_r.unsqueeze(2).to_broadcast([P, 4, MEM]), ALU.mult).then_inc(S["ma_p"], 1)

            mem_maxima(0)
            mem_maxima(1)
            mem_probabilities(0)
            for hd in range(4):
                for t in range(2):
                    dve.wait_ge(S["ma_pt_hi"], 2 * hd + t + 1)
                    TTO(pt_lo[:, t, :], X[2 + t], pt_hi[:, t, :].bitcast(f32), ALU.subtract).then_inc(S["ma_pt_lo"], 1)
                if hd < 3:
                    mem_probabilities(hd + 1)
                if hd < 2:
                    mem_maxima(hd + 2)
                for i in range(2):
                    dve.wait_ge(S["ma_hi"], 2 * hd + i + 1)
                    TTO(o_lo[:, 2 * hd + i, :], M[i], o_hi[:, 2 * hd + i, :].bitcast(f32),
                        ALU.subtract).then_inc(S["ma_lo"], 1)
            resid(N_MO, 2, 2, "norm_mlp_w", 0, *mem_of[0][0:2])
            dve.wait_ge(S["norm_rstd"], 3)
            mlp(N_MLP1, 0, 3, None)
            norm_final(3, "norm_final_w", 4, 3, "ln_mix_2", g_hi, g_lo_)
            dve.wait_ge(S["st_bias"], 16)
            gla_dve(dve, lo, evac, evac_tm, resid)
            dve.wait_ge(S["norm_rstd"], 6)
            mlp(N_MLP2, 1, 6, 5, "kv_norm_2", 0, kx_hi, kx_lo)
            for c in range(KT):
                dve.wait_ge(S["x_hi"], 48 + c + 1)
                STT(sx_lo[:, c, :], h[:, c, :], V("ln_mix_2", 8 + c), sx_hi[:, c, :].bitcast(f32), ALU.mult,
                    ALU.subtract).then_inc(S["x_lo"], 1)
            lo(N_WQ)
            dve.wait_ge(S["norm_rstd"], 7)
            evac(N_KV, 0, kf[:])
            evac_tm(N_KV, 1, sv[:], rcol[:])
            for i in range(2):
                dve.wait_ge(S["sw_dup_hi"], i + 1)
                TTO(kd_lo[i][:], X[1 + i], kd_hi[i][:].bitcast(f32), ALU.subtract).then_inc(S["sw_dupev"], 1)

            def query_lo(s):
                dve.wait_ge(S["sq_split_hi"], s + 1)
                TTO(sq_lo[:, s, :], sq_tmp[s % 4][:], sq_hi[:, s, :].bitcast(f32), ALU.subtract).then_inc(S["sq_split_lo"], 1)

            for s in range(KT):
                if s % 2 == 0:
                    lo(N_WQ + s // 2 + 1)
                if s >= 4:
                    dve.wait_ge(S["sq_split_lo"], s - 3)
                evac(N_WQ + s // 2, s % 2, sq_tmp[s % 4][:])
                if s:
                    query_lo(s - 1)
            query_lo(KT - 1)
            dve.wait_ge(S["ld_bias"], 16)

            def sw_logits(c):
                sink = sinkb[:, 2 * c:2 * c + 2].unsqueeze(1).to_broadcast([P, 4, 2])
                if c >= 3:
                    dve.wait_ge(S["sw_tr"], 4 * (c - 2))
                s_, (sw_mx_, sw_ng_, _, sw_es_, _) = sc[c % 3], sw_small[c % 2]
                nc.vector.memset(s_[:, 0, :, 0:P], NEG).then_inc(S["sw_fill"], 1)
                for qb in range(4):
                    u, off = 4 * c + qb, 0 if qb else P
                    dve.wait_ge(S["sw_score"], u + 1)
                    STT(s_[:, qb, :, off:256], sw_banks(u)[:, :, off:256], 0.125, bias[:, 2 * c:2 * c + 2, off:256],
                        ALU.mult, ALU.add).then_inc(S["sw_s"], 1)
                dve.wait_ge(S["sw_fill"], c + 1)
                dve.wait_ge(S["sw_s"], 4 * c + 4)
                nc.vector.reduce_max(sw_mx_, s_[:].rearrange("p a b n -> p (a b) n"), AX.X).then_inc(S["sw_mx"], 1)
                dve.wait_ge(S["sw_mx"], c + 1)
                mx4 = sw_mx_.rearrange("p (a b) -> p a b", b=2)
                TTO(mx4, mx4, sink, ALU.max).then_inc(S["sw_m"], 1)
                dve.wait_ge(S["sw_m"], c + 1)
                TS(sw_ng_, sw_mx_, -1.0, None, ALU.mult).then_inc(S["sw_neg"], 1)
                TTO(sw_es_.rearrange("p (a b) -> p a b", b=2), sink, mx4, ALU.subtract).then_inc(S["sw_es"], 1)

            def sw_sums(c):
                _, _, sw_z_, sw_es_, sw_r_ = sw_small[c % 2]
                dve.wait_ge(S["sw_e"], c + 1)
                TTO(sw_es_, sw_es_, sw_z_, ALU.add).then_inc(S["sw_den"], 1)
                dve.wait_ge(S["sw_den"], c + 1)
                nc.vector.reciprocal(sw_r_, sw_es_).then_inc(S["sw_rd"], 1)

            def result_lo(c):
                dve.wait_ge(S["sw_hi"], c + 1)
                TTO(s_lo[:, c, :], M[c % 2][:], s_hi[:, c, :].bitcast(f32), ALU.subtract).then_inc(S["sw_lo"], 1)

            sw_logits(0)
            sw_logits(1)
            sw_sums(0)
            for c in range(KT):
                if c + 2 < KT:
                    sw_logits(c + 2)
                if c:
                    result_lo(c - 1)
                if c + 1 < KT:
                    sw_sums(c + 1)
            result_lo(KT - 1)
            resid(N_SOUT, 7, 7, "ln_mlp_2", 8, *mem_of[2][0:2])
            dve.wait_ge(S["norm_rstd"], 8)
            mlp(N_MLP3, 2, 8, None)
            norm_final(8, "ln_final_2")
            for i in range(2 * TT):
                dve.wait_ge(S["fin_tr"], i + 1)
                nc.vector.tensor_copy(ytm[:, i, :], X[2 + i % 2][:]).then_inc(S["fin_ev"], 1)


INPUTS = ["x", "mem", "norm_mix_w", "w_in", "mu_shift", "w_decay0", "w_decay_up", "a0", "a_up", "g_up", "k_k", "k_a", "r_k",
          "lnx_w", "lnx_b", "lam_q1", "lam_k1", "lam_q2", "lam_k2", "subln_w", "w_out", "norm_mem_w", "norm_src_w", "w_mq",
          "w_mk", "w_mv", "w_mo", "norm_mlp_w", "w_up", "w_down", "norm_final_w", "a_w_in_2", "a_w_gk2_2", "a_b_gk_2",
          "a_onorm_2", "a_w_out_2", "kv_norm_2", "w_kv_2", "b_w_q_2", "b_sinks_2", "b_w_out_2", "rel_table_2", "ln_mix_2",
          "ln_mlp_2", "w_up_2", "w_down_2", "ln_final_2"]


def kernel(**inputs):
    import concourse.bacc as _bacc
    from concourse.bass_utils import run_bass_kernel_spmd as _run

    nc = _bacc.Bacc("TRN2", target_bir_lowering=False, num_devices=1)
    given = {name: np.ascontiguousarray(inputs[name]) for name in INPUTS}
    given["vecs"] = np.concatenate([given.pop(name).reshape(-1, P) for name, _ in VECS])
    given["consts"] = constants()
    given["onehot"] = bucket_onehot()
    arrays, aps = {}, {}
    for name, a in given.items():
        arrays[f"in_{name}_dram"] = a
        aps[name] = nc.dram_tensor(f"in_{name}_dram", a.shape, mybir.dt.from_np(a.dtype), kind="ExternalInput").ap()
    out = nc.dram_tensor("out_0_dram", (1, T, D), mybir.dt.float32, kind="ExternalOutput").ap()
    program(nc, aps, out)
    r = _run(nc, [arrays], core_ids=[0])
    return r.results[0]["out_0_dram"]
```
